# Optimizing a Trainium2 kernel written in Bass

```python
import math
import jax
import jax.numpy as jnp
from jax import lax
import numpy as np

D_MODEL = 1024
BATCH = 1
SEQ = 1024
DEPTH = 1
DEC_BATCH = 8
DEC_SEQ = 16
PAST_LEN = 256

CHUNK = 64
N_MEM = 256
D_MIX = D_MODEL
D_RWKV = D_MIX // 2
RWKV_HEAD = 64
RWKV_HEADS = D_RWKV // RWKV_HEAD
W_LORA = 64
A_LORA = 64
G_LORA = 128
C_RWKV = 3 * D_RWKV + W_LORA + A_LORA + G_LORA
D_DIFF = D_MIX - D_RWKV
DIFF_HEADS = 4
DIFF_V = D_DIFF // DIFF_HEADS
DIFF_QK = DIFF_V // 2
C_DIFF_QK = DIFF_HEADS * 2 * DIFF_QK
C_DIFF = 2 * C_DIFF_QK + D_DIFF
C_IN = C_RWKV + C_DIFF
MEM_HEADS = 4
MEM_HEAD = D_MODEL // MEM_HEADS
N_GROUPS = 4
EXPERTS_PER_GROUP = 8
N_EXPERTS = N_GROUPS * EXPERTS_PER_GROUP
TOP_K = 2
D_EXPERT = D_MODEL // 2
MOE_BLOCK = 128
Q_BLOCK = 128
DEEPNORM_ALPHA = (2.0 * DEPTH) ** 0.25
DEEPNORM_BETA = (8.0 * DEPTH) ** -0.25
LN_EPS = 1e-5
RMS_EPS = 1e-5
RWKV_GN_EPS = 64e-5
NEG_INF = -1e30

kernel_name = 'hybrid_rwkv7_diffattn_hmoe_stream'

def layer_norm(x, g, b):
    xf = x.astype(jnp.float32)
    mu = jnp.mean(xf, -1, keepdims=True)
    var = jnp.mean(jnp.square(xf - mu), -1, keepdims=True)
    y = (xf - mu) * lax.rsqrt(var + LN_EPS) * g.astype(jnp.float32) + b.astype(jnp.float32)
    return y.astype(x.dtype)

def alibi_slopes():
    return jnp.asarray(np.array([2.0 ** (-8.0 * (h + 1) / DIFF_HEADS) for h in range(DIFF_HEADS)], np.float32))

def rwkv_scan(state0, r, w, k, v, kk, a):
    def step(s, inp):
        r_t, w_t, k_t, v_t, kk_t, a_t = inp
        sa = jnp.einsum('bhvk,bhk->bhv', s, -kk_t)
        s = (s * w_t[:, :, None, :] + sa[..., None] * (kk_t * a_t)[:, :, None, :]
             + v_t[..., None] * k_t[:, :, None, :])
        return s, jnp.einsum('bhvk,bhk->bhv', s, r_t)
    xs = tuple(jnp.swapaxes(t, 0, 1) for t in (r, w, k, v, kk, a))
    s_final, o = lax.scan(step, state0, xs)
    return s_final, jnp.swapaxes(o, 0, 1)

def rwkv_branch(p_a, shift_prev, state0, lp):
    B, S, _ = p_a.shape
    f32 = jnp.float32
    p_prev = jnp.concatenate([shift_prev.astype(p_a.dtype), p_a[:, :-1]], axis=1)
    ps = p_a + (p_prev - p_a) * lp['rwkv_mu']
    r = ps[..., :D_RWKV]
    k = ps[..., D_RWKV:2 * D_RWKV]
    v = ps[..., 2 * D_RWKV:3 * D_RWKV]
    o0 = 3 * D_RWKV
    w_lo = ps[..., o0:o0 + W_LORA]
    a_lo = ps[..., o0 + W_LORA:o0 + W_LORA + A_LORA]
    g_lo = ps[..., o0 + W_LORA + A_LORA:]
    w_log = -jax.nn.softplus(-(lp['rwkv_w0'] + jnp.tanh(w_lo) @ lp['rwkv_w2'])) - 0.5
    decay = jnp.exp(-jnp.exp(w_log.astype(f32)))
    a = jax.nn.sigmoid(lp['rwkv_a0'] + a_lo @ lp['rwkv_a2'])
    g = jax.nn.sigmoid(g_lo) @ lp['rwkv_g2']
    kk = (k * lp['rwkv_k_k']).reshape(B, S, RWKV_HEADS, RWKV_HEAD).astype(f32)
    kk = kk / jnp.maximum(jnp.sqrt(jnp.sum(jnp.square(kk), -1, keepdims=True)), 1e-12)
    k = k * (1.0 + (a - 1.0) * lp['rwkv_k_a'])
    hd = lambda t: t.reshape(B, S, RWKV_HEADS, RWKV_HEAD).astype(f32)
    rh, kh, vh, ah, wh = hd(r), hd(k), hd(v), hd(a), hd(decay)
    state, o = rwkv_scan(state0.astype(f32), rh, wh, kh, vh, kk, ah)
    mu = jnp.mean(o, -1, keepdims=True)
    var = jnp.mean(jnp.square(o - mu), -1, keepdims=True)
    o = ((o - mu) * lax.rsqrt(var + RWKV_GN_EPS)).reshape(B, S, D_RWKV)
    o = o * lp['rwkv_ln_w'].astype(f32) + lp['rwkv_ln_b'].astype(f32)
    bonus = jnp.sum(rh * kh * lp['rwkv_r_k'].astype(f32), -1, keepdims=True) * vh
    o = (o + bonus.reshape(B, S, D_RWKV)) * g.astype(f32)
    return o.astype(p_a.dtype), state, p_a[:, -1:]

def split_diff(p_b):
    B, S, _ = p_b.shape
    q = p_b[..., :C_DIFF_QK].reshape(B, S, DIFF_HEADS, 2 * DIFF_QK)
    k = p_b[..., C_DIFF_QK:2 * C_DIFF_QK].reshape(B, S, DIFF_HEADS, 2 * DIFF_QK)
    v = p_b[..., 2 * C_DIFF_QK:].reshape(B, S, DIFF_HEADS, DIFF_V)
    t = lambda z: jnp.transpose(z, (0, 2, 1, 3))
    return t(q), t(k), t(v)

def diff_lambda(lq1, lk1, lq2, lk2, lam_init):
    f = lambda z: z.astype(jnp.float32)
    return jnp.exp(jnp.sum(f(lq1) * f(lk1))) - jnp.exp(jnp.sum(f(lq2) * f(lk2))) + lam_init

def diff_attend(q, k, v, q_pos, k_pos, lam):
    B, H, Q, _ = q.shape
    K = k.shape[2]
    qh = q.reshape(B, H, Q, 2, DIFF_QK)
    kh = k.reshape(B, H, K, 2, DIFF_QK)
    s = jnp.einsum('bhqcd,bhkcd->bhcqk', qh, kh).astype(jnp.float32) * (DIFF_QK ** -0.5)
    dist = jnp.abs(q_pos[:, None] - k_pos[None, :]).astype(jnp.float32)
    s = s - alibi_slopes()[None, :, None, None, None] * dist
    visible = (k_pos[None, :] // CHUNK) <= (q_pos[:, None] // CHUNK)
    s = jnp.where(visible, s, NEG_INF)
    pr = jax.nn.softmax(s, axis=-1)
    attn = pr[:, :, 0] - lam * pr[:, :, 1]
    return jnp.einsum('bhqk,bhkd->bhqd', attn.astype(v.dtype), v)

def diff_attend_prompt(q, k, v, lam):
    B, H, S, C = q.shape
    nb = S // Q_BLOCK
    pos = jnp.arange(S, dtype=jnp.int32)
    qb = jnp.moveaxis(q.reshape(B, H, nb, Q_BLOCK, C), 2, 0)
    pb = pos.reshape(nb, Q_BLOCK)
    out = lax.map(lambda z: diff_attend(z[0], k, v, z[1], pos, lam), (qb, pb))
    return jnp.moveaxis(out, 0, 2).reshape(B, H, S, DIFF_V)

def diff_output(o, subln, lam_init):
    B, H, S, _ = o.shape
    of = o.astype(jnp.float32)
    of = of * lax.rsqrt(jnp.mean(jnp.square(of), -1, keepdims=True) + RMS_EPS)
    of = of * subln.astype(jnp.float32) * (1.0 - lam_init)
    return jnp.transpose(of, (0, 2, 1, 3)).reshape(B, S, D_DIFF).astype(o.dtype)

def mem_attend(h, mk, mv, wq, wo):
    B, S, _ = h.shape
    q = (h @ wq).reshape(B, S, MEM_HEADS, MEM_HEAD)
    k = mk.reshape(B, -1, MEM_HEADS, MEM_HEAD).astype(q.dtype)
    v = mv.reshape(B, -1, MEM_HEADS, MEM_HEAD).astype(q.dtype)
    s = jnp.einsum('bqhd,bkhd->bhqk', q, k).astype(jnp.float32) * (MEM_HEAD ** -0.5)
    p = jax.nn.softmax(s, axis=-1).astype(v.dtype)
    o = jnp.einsum('bhqk,bkhd->bqhd', p, v).reshape(B, S, D_MODEL)
    return o @ wo

def moe_dispatch(xf, expert, gates, w1, w3, w2):
    T, D = xf.shape
    A = T * TOP_K
    e = expert.reshape(A)
    tok = jnp.arange(A, dtype=jnp.int32) // TOP_K
    order = jnp.argsort(e)
    e_s = e[order]
    counts = jnp.bincount(e, length=N_EXPERTS)
    padded = (counts + MOE_BLOCK - 1) // MOE_BLOCK * MOE_BLOCK
    starts = jnp.cumsum(counts) - counts
    pends = jnp.cumsum(padded)
    pstarts = pends - padded
    dest = pstarts[e_s] + (jnp.arange(A, dtype=jnp.int32) - starts[e_s])
    nblk = -(-A // MOE_BLOCK) + N_EXPERTS
    P = nblk * MOE_BLOCK
    slot_tok = jnp.full((P,), T, jnp.int32).at[dest].set(tok[order])
    slot_gate = jnp.zeros((P,), gates.dtype).at[dest].set(gates.reshape(A)[order])
    blk_start = jnp.arange(nblk, dtype=jnp.int32) * MOE_BLOCK
    blk_exp = jnp.minimum(jnp.searchsorted(pends, blk_start, side='right'), N_EXPERTS - 1)
    x_pad = jnp.concatenate([xf, jnp.zeros((1, D), xf.dtype)], axis=0)

    def run(z):
        tb, gb, eb = z
        xb = x_pad[tb]
        hb = jax.nn.silu(xb @ w1[eb]) * (xb @ w3[eb])
        return (hb @ w2[eb]) * gb[:, None]

    yb = lax.map(run, (slot_tok.reshape(nblk, MOE_BLOCK), slot_gate.reshape(nblk, MOE_BLOCK), blk_exp))
    y = jnp.zeros((T + 1, D), yb.dtype).at[slot_tok].add(yb.reshape(P, D))
    return y[:T]

def hier_moe(h, lp):
    B, S, D = h.shape
    T = B * S
    f32 = jnp.float32
    xf = h.reshape(T, D)
    g_logit = (xf @ lp['moe_w_group']).astype(f32) + lp['moe_b_group'].astype(f32)
    grp = jnp.argmax(g_logit, axis=-1).astype(jnp.int32)
    g_prob = jnp.take_along_axis(jax.nn.softmax(g_logit, -1), grp[:, None], axis=-1)
    e_logit = ((xf @ lp['moe_w_expert']).astype(f32) + lp['moe_b_expert'].astype(f32))
    e_logit = e_logit.reshape(T, N_GROUPS, EXPERTS_PER_GROUP)
    e_logit = jnp.take_along_axis(e_logit, grp[:, None, None], axis=1)[:, 0]
    top_val, top_idx = lax.top_k(e_logit, TOP_K)
    gates = g_prob * jax.nn.softmax(top_val, axis=-1)
    expert = grp[:, None] * EXPERTS_PER_GROUP + top_idx.astype(jnp.int32)
    y = moe_dispatch(xf, expert, gates.astype(h.dtype), lp['moe_w1'], lp['moe_w3'], lp['moe_w2'])
    return y.reshape(B, S, D)

def trunk_layer(x, shift_prev, rwkv_state0, past_k, past_v, mk, mv, lp, lam_init):
    B, S, _ = x.shape
    p = x @ lp['w_in']
    p_a, p_b = p[..., :C_RWKV], p[..., C_RWKV:]
    o_a, rwkv_state, shift_new = rwkv_branch(p_a, shift_prev, rwkv_state0, lp)
    q, k, v = split_diff(p_b)
    lam = diff_lambda(lp['diff_lq1'], lp['diff_lk1'], lp['diff_lq2'], lp['diff_lk2'], lam_init)
    if past_k is None:
        o_b = diff_attend_prompt(q, k, v, lam)
    else:
        P = past_k.shape[2]
        k_all = jnp.concatenate([past_k.astype(k.dtype), k], axis=2)
        v_all = jnp.concatenate([past_v.astype(v.dtype), v], axis=2)
        q_pos = P + jnp.arange(S, dtype=jnp.int32)
        k_pos = jnp.arange(P + S, dtype=jnp.int32)
        o_b = diff_attend(q, k_all, v_all, q_pos, k_pos, lam)
    mix = jnp.concatenate([o_a, diff_output(o_b, lp['diff_subln'], lam_init)], axis=-1) @ lp['w_out']
    h1 = layer_norm(DEEPNORM_ALPHA * x + mix, lp['ln1_g'], lp['ln1_b'])
    h2 = layer_norm(DEEPNORM_ALPHA * h1 + mem_attend(h1, mk, mv, lp['mem_wq'], lp['mem_wo']),
                    lp['ln2_g'], lp['ln2_b'])
    y = layer_norm(DEEPNORM_ALPHA * h2 + hier_moe(h2, lp), lp['ln3_g'], lp['ln3_b'])
    return y, k, v, rwkv_state, shift_new

def setup_inputs(seed: int = 0) -> dict:
    key = jax.random.key(seed)
    ks = jax.random.split(key, 44)
    f32 = jnp.float32
    L = DEPTH
    inv = D_MODEL ** -0.5

    def nrm(i, shape, scale=1.0):
        return jax.random.normal(ks[i], shape, f32) * scale

    def gain(i, shape, base=1.0):
        return base + 0.05 * jax.random.normal(ks[i], shape, f32)

    return {
        'x_prompt': nrm(0, (BATCH, SEQ, D_MODEL)),
        'x_sample': nrm(1, (DEC_BATCH, DEC_SEQ, D_MODEL)),
        'mem_prompt': nrm(2, (BATCH, N_MEM, D_MODEL)),
        'cache_diff_k': nrm(3, (L, DEC_BATCH, DIFF_HEADS, PAST_LEN, 2 * DIFF_QK)),
        'cache_diff_v': nrm(4, (L, DEC_BATCH, DIFF_HEADS, PAST_LEN, DIFF_V)),
        'cache_mem_k': nrm(5, (L, DEC_BATCH, N_MEM, D_MODEL)),
        'cache_mem_v': nrm(6, (L, DEC_BATCH, N_MEM, D_MODEL)),
        'state_rwkv': nrm(7, (L, DEC_BATCH, RWKV_HEADS, RWKV_HEAD, RWKV_HEAD), 0.5),
        'state_shift': nrm(8, (L, DEC_BATCH, 1, C_RWKV)),
        'w_in': nrm(9, (L, D_MODEL, C_IN), inv),
        'rwkv_mu': jax.random.uniform(ks[10], (L, C_RWKV), f32),
        'rwkv_w0': nrm(11, (L, D_RWKV), 0.5),
        'rwkv_w2': nrm(12, (L, W_LORA, D_RWKV), 0.5 * W_LORA ** -0.5),
        'rwkv_a0': nrm(13, (L, D_RWKV), 0.1),
        'rwkv_a2': nrm(14, (L, A_LORA, D_RWKV), A_LORA ** -0.5),
        'rwkv_g2': nrm(15, (L, G_LORA, D_RWKV), G_LORA ** -0.5),
        'rwkv_k_k': gain(16, (L, D_RWKV), 0.85),
        'rwkv_k_a': gain(17, (L, D_RWKV)),
        'rwkv_r_k': nrm(18, (L, RWKV_HEADS, RWKV_HEAD), 0.1),
        'rwkv_ln_w': gain(19, (L, D_RWKV)),
        'rwkv_ln_b': nrm(20, (L, D_RWKV), 0.02),
        'diff_lq1': nrm(21, (L, DIFF_QK), 0.1),
        'diff_lk1': nrm(22, (L, DIFF_QK), 0.1),
        'diff_lq2': nrm(23, (L, DIFF_QK), 0.1),
        'diff_lk2': nrm(24, (L, DIFF_QK), 0.1),
        'diff_subln': gain(25, (L, DIFF_V)),
        'w_out': nrm(26, (L, D_MIX, D_MODEL), D_MIX ** -0.5 * DEEPNORM_BETA),
        'ln1_g': gain(27, (L, D_MODEL)),
        'ln1_b': nrm(28, (L, D_MODEL), 0.02),
        'mem_wq': nrm(29, (L, D_MODEL, D_MODEL), inv),
        'mem_wk': nrm(30, (L, D_MODEL, D_MODEL), inv),
        'mem_wv': nrm(31, (L, D_MODEL, D_MODEL), inv),
        'mem_wo': nrm(32, (L, D_MODEL, D_MODEL), inv * DEEPNORM_BETA),
        'ln2_g': gain(33, (L, D_MODEL)),
        'ln2_b': nrm(34, (L, D_MODEL), 0.02),
        'moe_w_group': nrm(35, (L, D_MODEL, N_GROUPS), inv),
        'moe_b_group': nrm(36, (L, N_GROUPS), 0.01),
        'moe_w_expert': nrm(37, (L, D_MODEL, N_EXPERTS), inv),
        'moe_b_expert': nrm(38, (L, N_EXPERTS), 0.01),
        'moe_w1': nrm(39, (L, N_EXPERTS, D_MODEL, D_EXPERT), inv),
        'moe_w3': nrm(40, (L, N_EXPERTS, D_MODEL, D_EXPERT), inv),
        'moe_w2': nrm(41, (L, N_EXPERTS, D_EXPERT, D_MODEL), D_EXPERT ** -0.5 * DEEPNORM_BETA),
        'ln3_g': gain(42, (L, D_MODEL)),
        'ln3_b': nrm(43, (L, D_MODEL), 0.02),
    }

def reference(x_prompt, x_sample, mem_prompt, cache_diff_k, cache_diff_v, cache_mem_k, cache_mem_v,
              state_rwkv, state_shift, w_in, rwkv_mu, rwkv_w0, rwkv_w2, rwkv_a0, rwkv_a2, rwkv_g2,
              rwkv_k_k, rwkv_k_a, rwkv_r_k, rwkv_ln_w, rwkv_ln_b, diff_lq1, diff_lk1, diff_lq2, diff_lk2,
              diff_subln, w_out, ln1_g, ln1_b, mem_wq, mem_wk, mem_wv, mem_wo, ln2_g, ln2_b,
              moe_w_group, moe_b_group, moe_w_expert, moe_b_expert, moe_w1, moe_w3, moe_w2, ln3_g, ln3_b):
    B = x_prompt.shape[0]
    yp, ys = x_prompt, x_sample
    pk, pv, pmk, pmv, prw, psh = [], [], [], [], [], []
    sk, sv, srw, ssh = [], [], [], []
    for l in range(DEPTH):
        lp = {
            'w_in': w_in[l], 'rwkv_mu': rwkv_mu[l], 'rwkv_w0': rwkv_w0[l], 'rwkv_w2': rwkv_w2[l],
            'rwkv_a0': rwkv_a0[l], 'rwkv_a2': rwkv_a2[l], 'rwkv_g2': rwkv_g2[l], 'rwkv_k_k': rwkv_k_k[l],
            'rwkv_k_a': rwkv_k_a[l], 'rwkv_r_k': rwkv_r_k[l], 'rwkv_ln_w': rwkv_ln_w[l],
            'rwkv_ln_b': rwkv_ln_b[l], 'diff_lq1': diff_lq1[l], 'diff_lk1': diff_lk1[l],
            'diff_lq2': diff_lq2[l], 'diff_lk2': diff_lk2[l], 'diff_subln': diff_subln[l],
            'w_out': w_out[l], 'ln1_g': ln1_g[l], 'ln1_b': ln1_b[l], 'mem_wq': mem_wq[l],
            'mem_wo': mem_wo[l], 'ln2_g': ln2_g[l], 'ln2_b': ln2_b[l],
            'moe_w_group': moe_w_group[l], 'moe_b_group': moe_b_group[l],
            'moe_w_expert': moe_w_expert[l], 'moe_b_expert': moe_b_expert[l],
            'moe_w1': moe_w1[l], 'moe_w3': moe_w3[l], 'moe_w2': moe_w2[l],
            'ln3_g': ln3_g[l], 'ln3_b': ln3_b[l],
        }
        lam_init = 0.8 - 0.6 * math.exp(-0.3 * l)
        mk_p = mem_prompt @ mem_wk[l]
        mv_p = mem_prompt @ mem_wv[l]
        yp, k_p, v_p, st_p, sh_p = trunk_layer(
            yp, jnp.zeros((B, 1, C_RWKV), yp.dtype),
            jnp.zeros((B, RWKV_HEADS, RWKV_HEAD, RWKV_HEAD), jnp.float32),
            None, None, mk_p, mv_p, lp, lam_init)
        ys, k_s, v_s, st_s, sh_s = trunk_layer(
            ys, state_shift[l], state_rwkv[l], cache_diff_k[l], cache_diff_v[l],
            cache_mem_k[l], cache_mem_v[l], lp, lam_init)
        pk.append(k_p)
        pv.append(v_p)
        pmk.append(mk_p)
        pmv.append(mv_p)
        prw.append(st_p)
        psh.append(sh_p)
        sk.append(k_s)
        sv.append(v_s)
        srw.append(st_s)
        ssh.append(sh_s)
    return (yp, ys, jnp.stack(pk), jnp.stack(pv), jnp.stack(pmk), jnp.stack(pmv), jnp.stack(prw),
            jnp.stack(psh), jnp.stack(sk), jnp.stack(sv), jnp.stack(srw), jnp.stack(ssh))


_drawn_inputs = setup_inputs


def setup_inputs(seed=0):
    import zlib

    import numpy as np

    out = dict(_drawn_inputs(seed))
    spreads = {}
    factors = {'rwkv_k_k': 23.865,
     'rwkv_ln_w': 4.047,
     'rwkv_ln_b': 17.51,
     'diff_lq1': 4.305,
     'diff_lk1': 6.132,
     'diff_subln': 3.151,
     'moe_b_group': 5.871,
     'moe_b_expert': 20.352,
     'ln3_b': 2.84}
    for name, (base, spread) in spreads.items():
        noise = np.random.default_rng([zlib.crc32(name.encode()), seed]).standard_normal(out[name].shape)
        drawn = base * np.exp(spread * noise) if base else spread * noise
        out[name] = jnp.asarray(drawn.astype(out[name].dtype))
    for name, factor in factors.items():
        out[name] = (out[name] * factor).astype(out[name].dtype)
    return out
```

```python
from contextlib import ExitStack

import concourse.bass as bass
from concourse import mybir

F32 = mybir.dt.float32
I32 = mybir.dt.int32
U32 = mybir.dt.uint32
ALU = mybir.AluOpType
ACT = mybir.ActivationFunctionType
AX = mybir.AxisListType
ds = bass.ds

P = 128
D = 1024
KT = D // P
SEQ = 1024
PT = SEQ // P
DB, DS = 8, 16
T = SEQ + DB * DS
NT = T // P
CHUNK = 64
HEADS = 4
QK = 64
C_RWKV = 1792
D_RWKV = 512
C_IN = 3328
PAST = 256
N_MEM = 256
NEG = -1e30
LAM_INIT = 0.2
ALPHA = 2.0 ** 0.25
LN_EPS = 1e-5
HALF = 512


def attention_heads(nc, xT, mixT, ident, io):
    c = ExitStack()
    with c:
        def sb(name, shape, dt=F32):
            return c.enter_context(nc.sbuf_tensor(name, shape, dt))

        sems = []

        def sem(name):
            sems.append(c.enter_context(nc.semaphore(name)))
            return sems[-1]

        wh = sb("w_head", [P, KT, 3, P])
        qT = sb("qT", [P, T + DS])
        kT = sb("kT", [P, T])
        v = sb("v_tok", [P, NT, P])
        ktok = sb("k_tok", [P, NT, P])
        kc = sb("k_cache_T", [P, 2, 4, PAST])
        vc = sb("v_cache", [P, 2, 4, 2, P])
        S = sb("scores", [P, 2, 2, SEQ])
        at = sb("attn", [P, 2, SEQ])
        aT = sb("attn_T", [P, 8, P])
        osb = sb("o_units", [P, 10, P])
        tabP = sb("bias_prompt", [P, SEQ])
        tabS = sb("bias_sample", [P, 2, 384])
        itmp = sb("iota_tmp", [P, SEQ], I32)
        stat = sb("softmax_stats", [P, 2, 8])
        ss = sb("o_square_sums", [P, 10])
        rst = sb("o_rstd", [P, 2, 10])
        sq = sb("square_scratch", [P, P])
        sub = sb("subln", [P, 1])
        lqk = sb("lambda_vectors", [P, 4, QK])
        lam = sb("lambda_terms", [P, 8])
        psS = c.enter_context(nc.psum_tensor("psS", [P, 2, SEQ], F32))
        psT = c.enter_context(nc.psum_tensor("psT", [P, 2, HALF], F32))
        psO = c.enter_context(nc.psum_tensor("psO", [P, HALF], F32))

        consts_in, w_in_, caches_in = sem("consts_in"), sem("w_head_in"), sem("caches_in")
        iota_done, tables = sem("iota_done"), sem("tables_done")
        pj_full, pj_evac = sem("transposed_ready"), sem("transposed_copied")
        s_ready, s_biased, s_exp = sem("scores_ready"), sem("scores_biased"), sem("scores_exp")
        at_ready, pv_done, o_saved = sem("attn_ready"), sem("pv_done"), sem("o_saved")
        dvec, actc = sem("dve_chain"), sem("lambda_exps")
        rms_var, rms_sqrt, o_scaled = sem("rms_var"), sem("rms_sqrt"), sem("o_scaled")
        bias_begun, scores_begun = sem("bias_begun"), sem("scores_begun")
        proj_done, kv_out = sem("projections_done"), sem("kv_stored")

        width = [P * (u + 1) for u in range(PT)] + [384, 384]
        groups = [-(-w // HALF) for w in width]
        NPROJ = 12
        JOBS = NPROJ + sum(groups) + 3
        first_job = [NPROJ + sum(groups[:u]) for u in range(10)]
        CH = T // 3

        block = c.enter_context(nc.Block())

        @block.sync
        def _(sp):
            sp.nop().then_inc(kv_out, 16)
            sp.dma_start(sub[:], io["subln"]).then_inc(consts_in, 16)
            for n, name in enumerate(("diff_lq1", "diff_lk1", "diff_lq2", "diff_lk2")):
                sp.dma_start(lqk[:, n, :], io[name].broadcast_to([P, QK])).then_inc(consts_in, 16)
            with sp.Fori(0, HEADS) as h:
                sp.wait_ge(proj_done, 1 + h)
                for n in range(3):
                    sp.dma_start(wh[:, :, n, :], io["w_in_diff"][:, :, n, ds(h * P, P)]).then_inc(w_in_, 16)
                sp.wait_ge(pv_done, 1 + 10 * h)
                for g in range(2):
                    sp.dma_start(kc[:, g, :, :], io["cache_kT"][ds(h, 1), 4 * g:4 * g + 4, :, :].rearrange(
                        "o b d k -> d (o b) k")).then_inc(caches_in, 16)
                    for b in range(4):
                        sp.dma_start(vc[:, g, b, :, :], io["cache_diff_v"][0, 4 * g + b, ds(h, 1), :, :].rearrange(
                            "o (t p) d -> p (o t) d", p=P)).then_inc(caches_in, 16)
                sp.wait_ge(pj_evac, 1 + JOBS * h + NPROJ)
                sp.dma_start(io["out_diff_k_prompt"][ds(h, 1), :, :].rearrange("o (t p) d -> p (o t) d", p=P),
                             ktok[:, 0:PT, :]).then_inc(kv_out, 16)
                sp.dma_start(io["out_diff_v_prompt"][ds(h, 1), :, :].rearrange("o (t p) d -> p (o t) d", p=P),
                             v[:, 0:PT, :]).then_inc(kv_out, 16)
                sp.dma_start(io["out_diff_k_sample"][ds(h, 1), :, :].rearrange("o p d -> p (o d)"),
                             ktok[:, PT, :]).then_inc(kv_out, 16)
                sp.dma_start(io["out_diff_v_sample"][ds(h, 1), :, :].rearrange("o p d -> p (o d)"),
                             v[:, PT, :]).then_inc(kv_out, 16)
            sp.wait_ge(kv_out, 16 + 64 * HEADS)

        @block.gpsimd
        def _(pool):
            nc.gpsimd.iota(itmp[:, :], pattern=[[-1, SEQ]], base=SEQ - P, channel_multiplier=1).then_inc(iota_done, 1)
            pool.wait_ge(tables, 1)
            for r in range(4):
                q = slice(32 * r, 32 * r + 32)
                nc.gpsimd.iota(itmp[q, 0:PAST], pattern=[[-1, PAST]], base=PAST, channel_multiplier=1)
                nc.gpsimd.iota(itmp[q, PAST:PAST + DS], pattern=[[-1, DS]], base=0,
                               channel_multiplier=1).then_inc(iota_done, 1)

        @block.vector
        def _(dve):
            chained = [0]

            def then(ins):
                chained[0] += 1
                ins.then_inc(dvec, 1)
                dve.wait_ge(dvec, chained[0])

            dve.nop().then_inc(s_biased, 1)
            slope = 8.0 * 2.0 ** -2
            dve.wait_ge(iota_done, 1)
            then(nc.vector.tensor_copy(tabP[:], itmp[:]))
            then(nc.vector.scalar_tensor_tensor(S[:, 0, 0, :], tabP[:], -1.0, tabP[:], ALU.mult, ALU.max))
            ins = nc.vector.tensor_scalar(tabP[:], S[:, 0, 0, :], -slope, None, ALU.mult)
            then(ins)
            nc.vector.memset(tabP[0:CHUNK, SEQ - CHUNK:SEQ], NEG).then_inc(tables, 1)
            dve.wait_ge(iota_done, 5)
            then(nc.vector.tensor_copy(S[:, 0, 0, 0:PAST + DS], itmp[:, 0:PAST + DS]))
            then(nc.vector.scalar_tensor_tensor(S[:, 1, 0, 0:PAST + DS], S[:, 0, 0, 0:PAST + DS], -1.0,
                                                S[:, 0, 0, 0:PAST + DS], ALU.mult, ALU.max))
            then(nc.vector.memset(tabS[:], NEG))
            for g in range(2):
                nc.vector.tensor_scalar(tabS[:, g, 0:PAST], S[:, 1, 0, 0:PAST], -slope, None, ALU.mult)
                for r in range(4):
                    q = slice(32 * r, 32 * r + 32)
                    o = PAST + DS * (4 * g + r)
                    ins = nc.vector.tensor_scalar(tabS[q, g, o:o + DS], S[q, 1, 0, PAST:PAST + DS], -slope, None,
                                                  ALU.mult)
            then(ins)
            then(nc.vector.memset(qT[:, T:T + DS], 0.0))
            dve.wait_ge(consts_in, 80)
            for n in range(2):
                then(nc.vector.tensor_tensor_reduce(sq[:, 0:QK], lqk[:, 2 * n, :], lqk[:, 2 * n + 1, :], 1.0, 0.0,
                                                    ALU.mult, ALU.add, lam[:, n:n + 1]))
            then(nc.vector.tensor_scalar(sub[:], sub[:], 1.0 - LAM_INIT, None, ALU.mult))
            dve.nop().then_inc(tables, 1)
            dve.wait_ge(actc, 1)
            then(nc.vector.tensor_tensor(lam[:, 4:5], lam[:, 3:4], lam[:, 2:3], ALU.subtract))
            then(nc.vector.tensor_scalar(lam[:, 5:6], lam[:, 4:5], -LAM_INIT, None, ALU.add))
            SETUP = chained[0]
            CHAIN = 10 * 2 + 10 * 4 + 3

            with dve.Fori(0, HEADS) as h:
                at_link = [0]

                def link(ins):
                    at_link[0] += 1
                    ins.then_inc(dvec, 1)
                    dve.wait_ge(dvec, CHAIN * h + SETUP + at_link[0])

                def bias_and_max(u):
                    dve.wait_ge(s_ready, 10 * h + u + 1)
                    dve.nop().then_inc(bias_begun, 1)
                    w = width[u]
                    tab = tabP[:, SEQ - w:SEQ] if u < PT else tabS[:, u - PT, :]
                    st = stat[:, u % 2, :]
                    for k in range(2):
                        ins = nc.vector.tensor_tensor_reduce(S[:, u % 2, k, 0:w], psS[:, k, 0:w], tab, 1.0, -3e38,
                                                             ALU.add, ALU.max, st[:, k:k + 1])
                    link(ins)
                    link(nc.vector.tensor_scalar(st[:, 2:4], st[:, 0:2], -0.125, None, ALU.mult))
                    dve.nop().then_inc(s_biased, 1)

                def combine(u):
                    dve.wait_ge(s_exp, 20 * h + 2 * u + 2)
                    w = width[u]
                    st = stat[:, u % 2, :]
                    link(nc.vector.reciprocal(st[:, 6:8], st[:, 4:6]))
                    link(nc.vector.tensor_scalar(st[:, 7:8], st[:, 7:8], lam[:, 5:6], None, ALU.mult))
                    link(nc.vector.tensor_scalar(S[:, u % 2, 1, 0:w], S[:, u % 2, 1, 0:w], st[:, 7:8], None, ALU.mult))
                    if u >= 2:
                        dve.wait_ge(pj_full, JOBS * h + first_job[u - 2] + groups[u - 2])
                    link(nc.vector.scalar_tensor_tensor(at[:, u % 2, 0:w], S[:, u % 2, 0, 0:w], st[:, 6:7],
                                                        S[:, u % 2, 1, 0:w], ALU.mult, ALU.add))
                    dve.nop().then_inc(at_ready, 1)

                bias_and_max(0)
                for u in range(10):
                    if u < 9:
                        bias_and_max(u + 1)
                    combine(u)
                nc.vector.tensor_scalar(tabP[:], tabP[:], 0.25, None, ALU.mult)
                nc.vector.tensor_scalar(tabS[:], tabS[:], 0.25, None, ALU.mult)
                dve.wait_ge(o_saved, 10 * h + 10)
                link(nc.vector.tensor_scalar(rst[:, 0, :], ss[:], 1.0 / P, 1e-5, ALU.mult, ALU.add))
                dve.nop().then_inc(rms_var, 1)
                dve.wait_ge(rms_sqrt, h + 1)
                link(nc.vector.reciprocal(rst[:, 0, :], rst[:, 1, :]))
                for u in range(10):
                    ins = nc.vector.tensor_scalar(osb[:, u, :], osb[:, u, :], rst[:, 0, u:u + 1], None, ALU.mult)
                link(ins)
                dve.nop().then_inc(o_scaled, 1)
                assert at_link[0] == CHAIN

        @block.scalar
        def _(act):
            act.nop().then_inc(pj_evac, 1)
            act.wait_ge(tables, 2)
            nc.scalar.activation(lam[:, 2:4], lam[:, 0:2], ACT.Exp).then_inc(actc, 1)
            with act.Fori(0, HEADS) as h:
                job = [0]

                def bank():
                    j = job[0]
                    job[0] += 1
                    act.wait_ge(pj_full, JOBS * h + j + 1)
                    return psT[:, j % 2, :]

                act.wait_ge(kv_out, 16 + 64 * h)
                for n in range(3):
                    nc.scalar.copy(qT[:, CH * n:CH * n + CH], bank()[:, 0:CH]).then_inc(pj_evac, 1)
                for n in range(3):
                    nc.scalar.copy(kT[:, CH * n:CH * n + CH], bank()[:, 0:CH]).then_inc(pj_evac, 1)
                for dst in (v, ktok):
                    for n in range(3):
                        k = min(4, NT - 4 * n)
                        nc.scalar.copy(dst[:, 4 * n:4 * n + k, :].rearrange("p t d -> p (t d)"),
                                       bank()[:, 0:k * P]).then_inc(pj_evac, 1)

                def exponentials(u):
                    act.wait_ge(s_biased, 1 + 10 * h + u + 1)
                    w, st = width[u], stat[:, u % 2, :]
                    for k in range(2):
                        nc.scalar.activation(S[:, u % 2, k, 0:w], S[:, u % 2, k, 0:w], ACT.Exp, bias=st[:, 2 + k:3 + k],
                                             scale=0.125, accum_out=st[:, 4 + k:5 + k]).then_inc(s_exp, 1)

                exponentials(0)
                for u in range(10):
                    if u < 9:
                        exponentials(u + 1)
                    for g in range(groups[u]):
                        k = min(HALF, width[u] - HALF * g)
                        nc.scalar.copy(aT[:, 4 * g:4 * g + k // P, :].rearrange("p t d -> p (t d)"),
                                       bank()[:, 0:k]).then_inc(pj_evac, 1)
                    act.wait_ge(pv_done, 1 + 10 * h + u + 1)
                    nc.scalar.copy(osb[:, u, :], psO[:, 0:P])
                    nc.scalar.activation(sq[:], psO[:, 0:P], ACT.Square, accum_out=ss[:, u:u + 1]).then_inc(o_saved, 1)
                act.wait_ge(rms_var, h + 1)
                nc.scalar.activation(rst[:, 1, :], rst[:, 0, :], ACT.Sqrt).then_inc(rms_sqrt, 1)
                for n in range(2):
                    nc.scalar.activation(mixT[:, ds(4 + h, 1), HALF * n:HALF * n + HALF].rearrange("p o t -> p (o t)"),
                                         bank(), ACT.Copy, scale=sub[:, 0:1]).then_inc(pj_evac, 1)
                src = bank()[:, 0:2 * P].rearrange("p (b i) -> p b i", i=32)[:, :, 0:DS]
                dst = mixT[:, ds(4 + h, 1), SEQ:T].rearrange("p o (b i) -> p (o b) i", i=DS)
                nc.scalar.activation(dst, src, ACT.Copy, scale=sub[:, 0:1]).then_inc(pj_evac, 1)
                assert job[0] == JOBS

        @block.tensor
        def _(pe):
            pe.nop().then_inc(proj_done, 1)
            pe.nop().then_inc(pv_done, 1)
            pe.wait_ge(tables, 2)
            with pe.Fori(0, HEADS) as h:
                job = [0]

                def bank():
                    j = job[0]
                    job[0] += 1
                    pe.wait_ge(pj_evac, 1 + JOBS * h + max(j - 1, 0))
                    return psT[:, j % 2, :]

                pe.wait_ge(w_in_, 48 * h + 48)
                for n in range(2):
                    for q in range(3):
                        o = bank()
                        for k in range(KT):
                            mm = nc.tensor.matmul(o[:, 0:CH], wh[:, k, n, :], xT[:, k, CH * q:CH * q + CH],
                                                  start=k == 0, stop=k == KT - 1)
                        mm.then_inc(pj_full, 1)
                for q in range(3):
                    o = bank()
                    for t in range(4 * q, min(4 * q + 4, NT)):
                        for k in range(KT):
                            mm = nc.tensor.matmul(o[:, (t % 4) * P:(t % 4) * P + P], xT[:, k, P * t:P * t + P],
                                                  wh[:, k, 2, :], start=k == 0, stop=k == KT - 1)
                    mm.then_inc(pj_full, 1)
                pe.wait_ge(pj_evac, 1 + JOBS * h + 6)
                for q in range(3):
                    o = bank()
                    for t in range(4 * q, min(4 * q + 4, NT)):
                        mm = nc.tensor.transpose(o[:, (t % 4) * P:(t % 4) * P + P], kT[:, P * t:P * t + P], ident[:])
                        if t == 0:
                            mm.then_inc(proj_done, 1)
                    mm.then_inc(pj_full, 1)

                def scores(u):
                    pe.wait_ge(s_biased, 1 + 10 * h + u)
                    pe.nop().then_inc(scores_begun, 1)
                    for k in range(2):
                        r = slice(QK * k, QK * k + QK)
                        if u < PT:
                            for c0 in range(0, width[u], HALF):
                                n = min(HALF, width[u] - c0)
                                mm = nc.tensor.matmul(psS[:, k, c0:c0 + n], qT[r, P * u:P * u + P], kT[r, c0:c0 + n],
                                                      start=True, stop=True)
                        else:
                            g = u - PT
                            for j in range(4):
                                o = SEQ + DS * (4 * g + j)
                                rows = slice(32 * j, 32 * j + 32)
                                nc.tensor.matmul(psS[rows, k, 0:PAST], qT[r, o:o + 32], kc[r, g, j, :],
                                                 start=True, stop=True)
                                mm = nc.tensor.matmul(psS[rows, k, PAST:384], qT[r, o:o + 32], kT[r, SEQ:T],
                                                      start=True, stop=True)
                    mm.then_inc(s_ready, 1)

                def weighted_values(u):
                    pe.wait_ge(at_ready, 10 * h + u + 1)
                    nb = width[u] // P
                    for g in range(groups[u]):
                        o = bank()
                        for b in range(4 * g, min(4 * g + 4, nb)):
                            mm = nc.tensor.transpose(o[:, (b % 4) * P:(b % 4) * P + P],
                                                     at[:, u % 2, P * b:P * b + P], ident[:])
                        mm.then_inc(pj_full, 1)
                    pe.wait_ge(pj_evac, 1 + JOBS * h + first_job[u] + groups[u])
                    if u < PT:
                        for b in range(nb):
                            mm = nc.tensor.matmul(psO[:, 0:P], aT[:, b, :], v[:, b, :], start=b == 0, stop=b == nb - 1)
                    else:
                        g = u - PT
                        for j in range(4):
                            rows = slice(32 * j, 32 * j + 32)
                            for b in range(3):
                                rhs = vc[:, g, j, b, :] if b < 2 else v[:, PT, :]
                                mm = nc.tensor.matmul(psO[rows, 0:P], aT[:, b, rows], rhs, start=b == 0, stop=b == 2)
                    mm.then_inc(pv_done, 1)

                pe.wait_ge(pj_evac, 1 + JOBS * h + NPROJ)
                pe.wait_ge(caches_in, 160 * h + 160)
                scores(0)
                for u in range(10):
                    if u < 9:
                        scores(u + 1)
                    weighted_values(u)
                pe.wait_ge(o_scaled, h + 1)
                for q in range(3):
                    o = bank()
                    for u in range(4 * q, min(4 * q + 4, 10)):
                        mm = nc.tensor.transpose(o[:, (u % 4) * P:(u % 4) * P + P], osb[:, u, :], ident[:])
                    mm.then_inc(pj_full, 1)
                assert job[0] == JOBS
            pe.wait_ge(pj_evac, 1 + JOBS * HEADS)
    return sems


RH = 8
NB = C_RWKV // P
XW = 1 + SEQ + DB * (DS + 1)
TW = DB * (DS + 1)
DECAY = 0.6065306597126334


def rwkv_projection(nc, xT, pool_dmas, pa_d, io):
    with ExitStack() as c:
        def sb(name, shape, dt=F32):
            return c.enter_context(nc.sbuf_tensor(name, shape, dt))

        sems = []

        def sem(name):
            sems.append(c.enter_context(nc.semaphore(name)))
            return sems[-1]

        w = sb("w_block", [P, 2, KT, P])
        row = sb("pa_row", [P, 2, XW])
        shift = sb("shift_in", [P, NB, DB])
        last = sb("shift_out", [P, NB, DB + 1])
        ps = c.enter_context(nc.psum_tensor("ps_proj", [P, 6, HALF], F32))
        w_got, s_in = [pool_dmas["w_even_in"], pool_dmas["w_odd_in"]], pool_dmas["shift_loaded"]
        full, copied, zero = sem("proj_full"), sem("proj_copied"), sem("row_zeroed")
        row_ready, row_out, last_out = sem("row_ready"), sem("row_stored"), sem("shift_stored")
        block = c.enter_context(nc.Block())
        GROUPS = [(0, HALF), (HALF, HALF), (SEQ, P)]

        @block.sync
        def _(sp):
            sp.nop().then_inc(row_out, 16)
            sp.wait_ge(zero, 1)
            with sp.Fori(0, NB // 2) as i:
                for b in range(2):
                    sp.wait_ge(row_ready, 1 + 2 * i + b + 1)
                    sp.dma_start(pa_d[:, ds(2 * i + b, 1), :].rearrange("p o x -> p (o x)"),
                                   row[:, b, :]).then_inc(row_out, 16)
            sp.wait_ge(row_ready, 1 + NB)
            sp.dma_start(io["out_shift"], last[:]).then_inc(last_out, 16)
            sp.wait_ge(row_out, 16 + 16 * NB)
            sp.wait_ge(last_out, 16)

        @block.gpsimd
        def _(pool):
            nc.gpsimd.memset(row[:, :, 0:1], 0.0).then_inc(zero, 1)
            pool.dma_start(shift[:], io["shiftT"]).then_inc(s_in, 16)
            with pool.Fori(0, NB // 2) as i:
                for b in range(2):
                    pool.wait_ge(full, 1 + 6 * i)
                    pool.dma_start(w[:, b, :, :].rearrange("p k (o n) -> p k o n", o=1),
                                 io["w_in_rwkv"][:, :, ds(2 * i + b, 1), :]).then_inc(w_got[b], 16)

        @block.scalar
        def _(act):
            act.nop().then_inc(row_ready, 1)
            act.wait_ge(s_in, 16)
            with act.Fori(0, NB // 2) as i:
                for b in range(2):
                    act.wait_ge(row_out, 16 + 32 * i)
                    for q, (c0, n) in enumerate(GROUPS):
                        act.wait_ge(full, 1 + 6 * i + 3 * b + q + 1)
                        if q < 2:
                            nc.scalar.copy(row[:, b, 1 + c0:1 + c0 + n], ps[:, 3 * b + q, 0:n]).then_inc(copied, 1)
                        else:
                            dst = row[:, b, 1 + SEQ:XW].rearrange("p (b i) -> p b i", i=DS + 1)
                            src = ps[:, 3 * b + q, 0:n].rearrange("p (b i) -> p b i", i=DS)
                            nc.scalar.copy(dst[:, :, 1:DS + 1], src).then_inc(copied, 1)
                            nc.scalar.copy(last[:, ds(2 * i + b, 1), 1:DB + 1].rearrange("p o b -> p (o b)"),
                                           src[:, :, DS - 1])
                            nc.scalar.copy(dst[:, :, 0],
                                           shift[:, ds(2 * i + b, 1), :].rearrange("p o b -> p (o b)"))
                            nc.scalar.copy(last[:, ds(2 * i + b, 1), 0:1].rearrange("p o b -> p (o b)"),
                                           ps[:, 3 * b + 1, HALF - 1:HALF]).then_inc(row_ready, 1)

        @block.tensor
        def _(pe):
            pe.nop().then_inc(full, 1)
            with pe.Fori(0, NB // 2) as i:
                for b in range(2):
                    pe.wait_ge(w_got[b], 16 * i + 16)
                    for q, (c0, n) in enumerate(GROUPS):
                        pe.wait_ge(row_ready, 1 + 2 * i)
                        for k in range(KT):
                            mm = nc.tensor.matmul(ps[:, 3 * b + q, 0:n], w[:, b, k, :], xT[:, k, c0:c0 + n],
                                                  start=k == 0, stop=k == KT - 1)
                        mm.then_inc(full, 1)
    return sems


def rwkv(nc, mixT, ident, pa_d, io):
    with ExitStack() as c:
        def sb(name, shape, dt=F32):
            return c.enter_context(nc.sbuf_tensor(name, shape, dt))

        sems = []

        def sem(name):
            sems.append(c.enter_context(nc.semaphore(name)))
            return sems[-1]

        vecs = sb("rwkv_vectors", [P, 6, 4])
        mu = sb("mu", [P, NB])
        w2 = sb("w2_a2", [P, D_RWKV])
        g2 = sb("g2", [P, D_RWKV])
        lnw = sb("gn_w", [P, D_RWKV])
        lnb = sb("gn_b", [P, D_RWKV])
        pair1 = sb("pair_ones", [P, P])
        hone = sb("head_ones", [P, 2])
        i64 = sb("ident_64_twice", [P, 64])
        cmask = [sb(f"causal_{n}", [P, 4, P]) for n in ("prompt", "sample")]
        lmask = sb("level_masks", [P, 6, P])
        notfirst = [sb(f"not_first_{n}", [P, HALF]) for n in ("prompt", "sample")]
        oneseq = sb("rows_of_sequence", [P, DB])
        colseq = sb("cols_of_sequence", [P, DB, P])
        x = sb("pa_tile", [P, NB, TW])
        sh = sb("shifted", [P, NB, P])
        low = sb("lora_in", [P, 2, P])
        dec = sb("decay", [P, HALF])
        rate = sb("rate", [P, HALF])
        kk = sb("kk", [P, HALF])
        t1 = sb("scratch_1", [P, HALF])
        t2 = sb("scratch_2", [P, HALF])
        W = sb("decay_product", [P, HALF])
        Wi = sb("decay_product_inverse", [P, HALF])
        beta = sb("beta", [P, 4, P])
        kap = sb("kappa", [P, 4, P])
        kr = sb("khat_rho", [P, 4, 2, P])
        rk = sb("bonus_products", [P, HALF])
        bt = sb("beta_tok", [P, RH, 64])
        kt = sb("kappa_tok", [P, RH, 64])
        kv = sb("khat_tok_and_mv", [P, RH, 2, 64])
        vt = sb("v_tok_rwkv", [P, RH, 64])
        pg = sb("minus_p_g", [P, RH, 2, 64])
        G = sb("grams", [P, 4, 4, P])
        N = sb("level_n", [P, 6, 4, P])
        XT = sb("x_transposed", [P, 4, P])
        X = sb("x_inverse", [P, 4, P])
        Y = sb("y_level", [P, 4, P])
        QT = sb("q_transposed", [P, 4, P])
        AB = sb("a_b", [P, 2, 2, 2, 64])
        St = sb("state", [P, 2, 4, 64])
        ABs = sb("a_b_sample", [P, 2, DB, 64])
        Qs = sb("q_by_sequence", [P, DB, P])
        ex = sb("values_by_sequence", [P, 3, DB, 64])
        Ss = sb("state_sample", [P, 4, DB, 64])
        So = sb("state_sample_new", [P, 4, DB, 64])
        o = sb("o_rwkv", [P, RH, 64])
        o2 = sb("o_scratch", [P, RH, 64])
        gn = sb("gn_stats", [P, 5, RH])

        pA = c.enter_context(nc.psum_tensor("pA", [P, 4, HALF], F32))
        pB = c.enter_context(nc.psum_tensor("pB", [P, 2, HALF], F32))
        pC = c.enter_context(nc.psum_tensor("pC", [P, HALF], F32))
        pD = c.enter_context(nc.psum_tensor("pD", [P, HALF], F32))

        cin, masks, x_got = sem("rwkv_consts_in"), sem("masks_made"), sem("pa_tile_in")
        x_used, vch, mixed = sem("pa_tile_used"), sem("dve_chain2"), sem("shift_mixed")
        lora_in, lora_out, lora_used = sem("lora_in_ready"), sem("lora_out_ready"), sem("lora_out_used")
        sig, decays, kk_sq, nrm = sem("sigmoids"), sem("decays_ready"), sem("kk_squares"), sem("norms_summed")
        nrm_in, nrm_sqrt = sem("norms_clamped"), sem("norms_sqrt")
        ch_ready, tr, tr_copied = sem("channel_values_ready"), sem("turned"), sem("turned_copied")
        gram, gram_used, lev = sem("gram_ready"), sem("gram_masked"), sem("levels_masked")
        x0, inv, inv_used, inv_c = sem("x0_ready"), sem("inverse_step"), sem("inverse_y"), sem("inverse_copied")
        mv, mv_c, pgd, pg_c = sem("mv_ready"), sem("mv_copied"), sem("pg_ready"), sem("pg_copied")
        qab, qab_used = sem("q_a_b_ready"), sem("q_a_b_used")
        st_mm, st_new = sem("state_product"), sem("state_updated")
        o_mm, o_copied = sem("o_ready"), sem("o_copied")
        x_turned, gn_var, gn_sqrt, bonus = sem("x_turned"), sem("gn_var"), sem("gn_sqrt"), sem("bonus_ready")
        gate, o_fin, o_tr, o_mix = sem("gate_ready"), sem("o_final"), sem("o_turned"), sem("o_in_mix")
        st_out, exq, ab_mm, exv = sem("states_stored"), sem("q_expanded"), sem("ab_ready"), sem("values_expanded")
        ab_used, state_seen = sem("ab_used"), sem("state_seen")
        block = c.enter_context(nc.Block())
        CONSTS = 16 * 12
        MASKS = 82

        def bc(vec, n):
            return vec.rearrange("p (g o) -> p g o", o=1).broadcast_to([P, vec.shape[1], n])

        def g4(ap):
            return ap.rearrange("p (g t) -> p g t", g=4)

        @block.sync
        def _(sp):
            for n, name in enumerate(("w0", "a0", "k_k", "k_a", "r_k")):
                sp.dma_start(vecs[:, n, :], io[name]).then_inc(cin, 16)
            sp.dma_start(mu[:], io["mu"]).then_inc(cin, 16)
            sp.dma_start(w2[0:64, :], io["w2"]).then_inc(cin, 16)
            sp.dma_start(w2[64:P, :], io["a2"]).then_inc(cin, 16)
            sp.dma_start(g2[:], io["g2"]).then_inc(cin, 16)
            sp.dma_start(lnw[:], io["rwkv_ln_w"].broadcast_to([P, D_RWKV])).then_inc(cin, 16)
            sp.dma_start(lnb[:], io["rwkv_ln_b"].broadcast_to([P, D_RWKV])).then_inc(cin, 16)
            sp.dma_start(Ss[:], io["state"]).then_inc(cin, 16)
            with sp.Fori(0, PT) as t:
                sp.wait_ge(x_used, 1 + t)
                sp.dma_start(x[:, :, 0:P + 1], pa_d[:, :, ds(P * t, P + 1)]).then_inc(x_got, 16)
            sp.wait_ge(x_used, 1 + PT)
            sp.dma_start(x[:, :, :], pa_d[:, :, 1 + SEQ:XW]).then_inc(x_got, 16)
            sp.wait_ge(st_new, 1 + 4 * PT)
            sp.dma_start(io["out_state_prompt"], St[:, 0, :, :]).then_inc(st_out, 16)
            sp.wait_ge(st_new, 1 + 4 * PT + 4)
            sp.dma_start(io["out_state_sample"], So[:]).then_inc(st_out, 16)
            sp.wait_ge(st_out, 32)

        @block.gpsimd
        def _(pool):
            made = [0]

            def then(ins):
                made[0] += 1
                ins.then_inc(masks, 1)
                pool.wait_ge(masks, made[0])

            def keep(ap, pattern, base, mult, cmp=ALU.is_ge, fill=0.0):
                then(nc.gpsimd.affine_select(out=ap, in_=ap, compare_op=cmp, fill=fill, base=base, pattern=pattern,
                                             channel_multiplier=mult))

            def blocks(ap, size):
                v = ap.rearrange("p (b i) -> p b i", i=size)
                keep(v, [[-size, P // size], [0, size]], 0, 1)
                keep(v, [[size, P // size], [0, size]], size - 1, -1)

            for m, size in ((cmask[0], CHUNK), (cmask[1], DS)):
                for n, (value, strict) in enumerate(((-1.0, 1), (1.0, 0), (1.0, 1), (1.0, 0))):
                    then(nc.gpsimd.memset(m[:, n, :], value))
                    keep(m[:, n, :], [[1, P]], -strict, -1)
                    blocks(m[:, n, :], size)
            for l in range(6):
                s = 1 << l
                then(nc.gpsimd.memset(lmask[:, l, :], 1.0))
                blocks(lmask[:, l, :], 2 * s)
                v = lmask[:, l, :].rearrange("p (b i) -> p b i", i=2 * s)
                keep(v, [[2 * s, P // (2 * s)], [0, 2 * s]], s - 1, -1)
                keep(v, [[0, P // (2 * s)], [1, 2 * s]], -s, 0)
            for m, size in ((notfirst[0], CHUNK), (notfirst[1], DS)):
                then(nc.gpsimd.memset(m[:], 1.0))
                then(nc.gpsimd.memset(m[:].rearrange("p (b i) -> p b i", i=size)[:, :, 0:1], 0.0))
            then(nc.gpsimd.memset(pair1[:], 1.0))
            blocks(pair1[:], 64)
            then(nc.gpsimd.memset(hone[:], 1.0))
            keep(hone[:], [[-64, 2]], 0, 1)
            keep(hone[:], [[64, 2]], 63, -1)
            then(nc.gpsimd.memset(i64[:], 0.0))
            keep(i64[:], [[-1, 64]], 0, 1, ALU.not_equal, 1.0)
            keep(i64[:], [[-1, 64]], -64, 1, ALU.not_equal, 1.0)
            then(nc.gpsimd.memset(oneseq[:], 1.0))
            keep(oneseq[:], [[-DS, DB]], 0, 1)
            keep(oneseq[:], [[DS, DB]], DS - 1, -1)
            then(nc.gpsimd.memset(colseq[:], 1.0))
            keep(colseq[:], [[-DS, DB], [1, P]], 0, 0)
            keep(colseq[:], [[DS, DB], [-1, P]], DS - 1, 0)
            then(nc.gpsimd.memset(St[:, 0, :, :], 0.0))
            assert made[0] == MASKS, made[0]

            def levels(t, g):
                pool.wait_ge(gram_used, 8 * t + 4 * g + 4)
                pool.wait_ge(pgd, 1 + 2 * t + g)
                for l in range(6):
                    ins = nc.gpsimd.tensor_tensor(N[:, l, :, :], G[:, :, 0, :],
                                                  lmask[:, l:l + 1, :].broadcast_to([P, 4, P]), ALU.mult)
                ins.then_inc(lev, 1)

            with pool.Fori(0, PT) as t:
                levels(t, 0)
                levels(t, 1)
            levels(PT, 0)
            levels(PT, 1)

        VCH = 60

        @block.vector
        def _(dve):
            def tile(t, sample):
                at_link = [0]

                def link(ins):
                    at_link[0] += 1
                    ins.then_inc(vch, 1)
                    dve.wait_ge(vch, VCH * t + 1 + at_link[0])

                if sample:
                    xv = x[:].rearrange("p c (b i) -> p c b i", i=DS + 1)
                    cur, prev = xv[:, :, :, 1:DS + 1], xv[:, :, :, 0:DS]
                    shv = sh[:].rearrange("p c (b i) -> p c b i", i=DS)
                else:
                    cur, prev, shv = x[:, :, 1:P + 1], x[:, :, 0:P], sh[:]
                m0 = notfirst[sample]
                size = DS if sample else CHUNK
                dve.wait_ge(x_got, 16 * t + 16)
                dve.wait_ge(gate, 1 + t)
                if sample:
                    for n in range(NB):
                        ins = nc.vector.tensor_tensor(shv[:, n], prev[:, n], cur[:, n], ALU.subtract)
                else:
                    ins = nc.vector.tensor_tensor(shv, prev, cur, ALU.subtract)
                link(ins)
                link(nc.vector.tensor_tensor(sh[:], sh[:], bc(mu[:], P), ALU.mult))
                if sample:
                    for n in range(NB):
                        ins = nc.vector.tensor_tensor(shv[:, n], shv[:, n], cur[:, n], ALU.add)
                else:
                    ins = nc.vector.tensor_tensor(shv, shv, cur, ALU.add)
                link(ins)
                dve.nop().then_inc(mixed, 1)
                dve.nop().then_inc(x_used, 1)
                r, k = sh[:, 0:4, :], sh[:, 4:8, :]
                dve.wait_ge(lora_out, t + 1)
                link(nc.vector.tensor_tensor(g4(dec[:]), g4(pA[:, 0, :]), bc(vecs[:, 0, :], P), ALU.add))
                link(nc.vector.tensor_tensor(g4(rate[:]), g4(pA[:, 1, :]), bc(vecs[:, 1, :], P), ALU.add))
                dve.nop().then_inc(lora_used, 1)
                link(nc.vector.tensor_tensor(g4(kk[:]), k, bc(vecs[:, 2, :], P), ALU.mult))
                link(nc.vector.tensor_tensor(t1[:], kk[:], kk[:], ALU.mult))
                dve.nop().then_inc(kk_sq, 1)
                dve.wait_ge(nrm, t + 1)
                link(nc.vector.tensor_scalar(t2[:], pA[:, 2, :], 1e-24, None, ALU.max))
                dve.nop().then_inc(nrm_in, 1)
                dve.wait_ge(sig, t + 1)
                link(nc.vector.tensor_tensor(g4(t1[:]), g4(rate[:]), bc(vecs[:, 3, :], P), ALU.mult))
                link(nc.vector.tensor_tensor(g4(t1[:]), g4(t1[:]), bc(vecs[:, 5, :], P), ALU.add))
                link(nc.vector.tensor_tensor(k, k, g4(t1[:]), ALU.mult))
                dve.wait_ge(nrm_sqrt, t + 1)
                link(nc.vector.reciprocal(t2[:], t2[:]))
                link(nc.vector.tensor_tensor(kk[:], kk[:], t2[:], ALU.mult))
                dve.wait_ge(decays, t + 1)
                link(nc.vector.tensor_tensor(t1[:], dec[:], m0[:], ALU.mult))
                link(nc.vector.tensor_tensor(dec[:], dec[:], t1[:], ALU.subtract))
                link(nc.vector.tensor_tensor_scan(W[:], t1[:], dec[:], 0.0, ALU.mult, ALU.add))
                link(nc.vector.reciprocal(Wi[:], W[:]))
                krv = kr[:, :, 0, :]
                link(nc.vector.tensor_tensor(krv[:, :, 1:P], g4(kk[:])[:, :, 1:P], g4(W[:])[:, :, 0:P - 1], ALU.mult))
                for n in range(4):
                    ins = nc.vector.tensor_copy(krv[:, n, :].rearrange("p (b i) -> p b i", i=size)[:, :, 0],
                                                g4(kk[:])[:, n, :].rearrange("p (b i) -> p b i", i=size)[:, :, 0])
                link(ins)
                link(nc.vector.tensor_tensor(kr[:, :, 1, :], r, g4(W[:]), ALU.mult))
                link(nc.vector.tensor_tensor(kk[:], kk[:], rate[:], ALU.mult))
                link(nc.vector.tensor_tensor(beta[:], g4(kk[:]), g4(Wi[:]), ALU.mult))
                link(nc.vector.tensor_tensor(kap[:], k, g4(Wi[:]), ALU.mult))
                link(nc.vector.tensor_tensor(g4(rk[:]), r, k, ALU.mult))
                link(nc.vector.tensor_tensor(g4(rk[:]), g4(rk[:]), bc(vecs[:, 4, :], P), ALU.mult))
                dve.nop().then_inc(ch_ready, 1)

                for g in range(2):
                    dve.wait_ge(tr_copied, 4 * t + 4)
                    for h in range(4):
                        dve.wait_ge(gram, 8 * t + 4 * g + h + 1)
                        nc.vector.tensor_tensor(G[:, h, :, :].rearrange("p k t -> p (k t)"), pA[:, h, :],
                                                cmask[sample][:].rearrange("p k t -> p (k t)"),
                                                ALU.mult).then_inc(gram_used, 1)
                    idb = ident[:].rearrange("p (o t) -> p o t", o=1).broadcast_to([P, 4, P])
                    dve.wait_ge(lev, 2 * t + g + 1)
                    nc.vector.tensor_tensor(XT[:], N[:, 0, :, :], idb, ALU.add).then_inc(x0, 1)
                    for l in range(1, 6):
                        dve.wait_ge(inv, 22 * t + 11 * g + 2 * l)
                        nc.vector.tensor_tensor(Y[:], g4(pB[:, 0, :]), idb, ALU.add).then_inc(inv_used, 1)
                    dve.wait_ge(qab, 2 * t + g + 1)
                    ins = nc.vector.tensor_tensor(QT[:, 2 * g:2 * g + 2, :],
                                                  pC[:, 0:2 * P].rearrange("p (g t) -> p g t", g=2),
                                                  kr[:, 2 * g:2 * g + 2, 1, :], ALU.add)
                    if not sample:
                        Wc = g4(W[:])[:, 2 * g:2 * g + 2, :].rearrange("p g (c i) -> p g c i", i=CHUNK)
                        Wc = Wc[:, :, :, CHUNK - 1:CHUNK]
                        for cc in range(2):
                            nc.vector.tensor_tensor(
                                AB[:, 0, :, cc, :], pB[:, cc, 0:P].rearrange("p (g k) -> p g k", k=64),
                                i64[:].rearrange("p (o k) -> p o k", o=1).broadcast_to([P, 2, 64]), ALU.add)
                            ins = nc.vector.tensor_tensor(
                                AB[:, 1, :, cc, :], pB[:, cc, P:2 * P].rearrange("p (g k) -> p g k", k=64),
                                Wc[:, :, cc, :].broadcast_to([P, 2, 64]), ALU.mult)
                    link(ins)
                    dve.nop().then_inc(qab_used, 1)
                    if not sample:
                        for cc in range(2):
                            dve.wait_ge(st_mm, 4 * t + 2 * g + cc + 1)
                            for n in range(2):
                                q = 2 * g + n
                                col = P * q + CHUNK * cc + CHUNK - 1
                                ins = nc.vector.scalar_tensor_tensor(
                                    St[:, 1 - cc, q, :], pD[:, 64 * n:64 * n + 64], W[:, col:col + 1],
                                    AB[:, 1, n, cc, :], ALU.mult, ALU.add)
                            ins.then_inc(st_new, 1)
                    else:
                        for n in range(2):
                            q = 2 * g + n
                            qe = nc.vector.tensor_tensor(
                                Qs[:], QT[:, q:q + 1, :].broadcast_to([P, DB, P]), colseq[:], ALU.mult)
                            link(qe)
                            dve.nop().then_inc(exq, 1)
                            for hf in range(2):
                                h = 2 * q + hf
                                e = 4 * g + 2 * n + hf
                                if e:
                                    dve.wait_ge(ab_mm, e)
                                seq = oneseq[:].rearrange("p (b o) -> p b o", o=1).broadcast_to([P, DB, 64])
                                for z, src in enumerate((bt[:, h:h + 1, :], vt[:, h:h + 1, :], pg[:, h, 1:2, :])):
                                    ins = nc.vector.tensor_tensor(ex[:, z, :, :], src.broadcast_to([P, DB, 64]), seq,
                                                                  ALU.mult)
                                ins.then_inc(exv, 1)
                            dve.wait_ge(ab_mm, 4 * g + 2 * n + 2)
                            Wc = W[:, P * q:P * q + P].rearrange("p (b i) -> p b i", i=DS)[:, :, DS - 1:DS]
                            nc.vector.tensor_tensor(ABs[:, 0, :, :], pB[:, 0, :].rearrange("p (b k) -> p b k", k=64),
                                                    i64[:].rearrange("p (o k) -> p o k", o=1).broadcast_to([P, DB, 64]),
                                                    ALU.add)
                            nc.vector.tensor_tensor(ABs[:, 1, :, :], pB[:, 1, :].rearrange("p (b k) -> p b k", k=64),
                                                    Wc.broadcast_to([P, DB, 64]), ALU.mult).then_inc(ab_used, 1)
                            dve.wait_ge(st_mm, 4 * t + 2 * g + n + 1)
                            link(nc.vector.tensor_tensor(So[:, q, :, :], pC[:].rearrange("p (b k) -> p b k", k=64),
                                                         Wc.broadcast_to([P, DB, 64]), ALU.mult))
                            nc.vector.tensor_tensor(So[:, q, :, :], So[:, q, :, :], ABs[:, 1, :, :],
                                                    ALU.add).then_inc(st_new, 1)
                dve.wait_ge(o_copied, 2 * t + 2)
                bh = lambda s: s.rearrange("p (h o) -> p h o", o=1).broadcast_to([P, RH, 64])
                while at_link[0] < (VCH - 11):
                    link(dve.nop())
                link(nc.vector.tensor_reduce(gn[:, 0, :], o[:], AX.X, ALU.add))
                link(nc.vector.tensor_scalar(gn[:, 1, :], gn[:, 0, :], 1.0 / 64, None, ALU.mult))
                link(nc.vector.tensor_tensor(o[:], o[:], bh(gn[:, 1, :]), ALU.subtract))
                link(nc.vector.tensor_tensor(o2[:], o[:], o[:], ALU.mult))
                link(nc.vector.tensor_reduce(gn[:, 2, :], o2[:], AX.X, ALU.add))
                link(nc.vector.tensor_scalar(gn[:, 2, :], gn[:, 2, :], 1.0 / 64, 64e-5, ALU.mult, ALU.add))
                dve.nop().then_inc(gn_var, 1)
                dve.wait_ge(gn_sqrt, t + 1)
                link(nc.vector.reciprocal(gn[:, 4, :], gn[:, 3, :]))
                link(nc.vector.tensor_tensor(o[:], o[:], bh(gn[:, 4, :]), ALU.mult))
                flat = lambda a: a[:].rearrange("p h k -> p (h k)")
                link(nc.vector.tensor_tensor(flat(o), flat(o), lnw[:], ALU.mult))
                dve.wait_ge(gate, 1 + t + 1)
                nc.vector.tensor_tensor(flat(o), flat(o), lnb[:], ALU.add)
                link(nc.vector.tensor_tensor(o2[:], vt[:], bh(pD[:, 0:RH]), ALU.mult))
                link(nc.vector.tensor_tensor(o[:], o[:], o2[:], ALU.add))
                nc.vector.tensor_tensor(flat(o), flat(o), pC[:], ALU.mult).then_inc(o_fin, 1)
                assert at_link[0] == VCH, at_link[0]

            dve.nop().then_inc(x_used, 1)
            dve.nop().then_inc(st_new, 1)
            dve.wait_ge(cin, CONSTS)
            nc.vector.tensor_scalar(vecs[:, 5, :], vecs[:, 3, :], -1.0, 1.0, ALU.mult, ALU.add).then_inc(vch, 1)
            dve.wait_ge(vch, 1)
            dve.wait_ge(masks, MASKS)
            with dve.Fori(0, PT) as t:
                tile(t, 0)
            tile(PT, 1)

        @block.scalar
        def _(act):
            def tile(t, sample):
                dst = slice(0, P)
                act.wait_ge(mixed, t + 1)
                nc.scalar.activation(low[0:64, 0, :], sh[0:64, 12, :], ACT.Tanh)
                nc.scalar.copy(low[64:P, 0, :], sh[64:P, 12, :])
                nc.scalar.activation(low[:, 1, :], sh[:, 13, :], ACT.Sigmoid).then_inc(lora_in, 1)
                act.wait_ge(lora_used, t + 1)
                nc.scalar.activation(rate[:], rate[:], ACT.Sigmoid)
                nc.scalar.activation(dec[:], dec[:], ACT.Sigmoid).then_inc(sig, 1)
                act.wait_ge(nrm_in, t + 1)
                nc.scalar.activation(t2[:], t2[:], ACT.Sqrt).then_inc(nrm_sqrt, 1)
                act.wait_ge(sig, t + 1)
                nc.scalar.activation(dec[:], dec[:], ACT.Exp, scale=-DECAY).then_inc(decays, 1)
                for n, d in enumerate((bt[:], kt[:], kv[:, :, 0, :], vt[:])):
                    act.wait_ge(tr, 4 * t + n + 1)
                    nc.scalar.copy(d, pA[:, n, :].rearrange("p (h k) -> p h k", k=64)).then_inc(tr_copied, 1)
                for g in range(2):
                    for n in range(0, 11, 2):
                        act.wait_ge(inv, 22 * t + 11 * g + n + 1)
                        if n == 0:
                            nc.scalar.copy(X[:].rearrange("p h t -> p (h t)"), pB[:, 1, :]).then_inc(inv_c, 1)
                        else:
                            nc.scalar.copy(XT[:].rearrange("p h t -> p (h t)"), pB[:, 1, :]).then_inc(inv_c, 1)
                            if n < 10:
                                act.wait_ge(x_turned, 8 * t + 4 * g + n // 2)
                                nc.scalar.copy(X[:].rearrange("p h t -> p (h t)"), pC[:]).then_inc(inv_c, 1)
                    act.wait_ge(mv, 2 * t + g + 1)
                    nc.scalar.copy(kv[:, 4 * g:4 * g + 4, 1, :],
                                   pC[:, 0:256].rearrange("p (h k) -> p h k", k=64)).then_inc(mv_c, 1)
                    act.wait_ge(pgd, 1 + 2 * t + g + 1)
                    nc.scalar.mul(pg[:, 4 * g:4 * g + 4, :, :].rearrange("p h z k -> p (h z k)"), pD[:],
                                  -1.0).then_inc(pg_c, 1)
                    act.wait_ge(o_mm, 2 * t + g + 1)
                    nc.scalar.copy(o[:, 4 * g:4 * g + 4, :], pA[:, :, 0:64]).then_inc(o_copied, 1)
                act.wait_ge(gn_var, t + 1)
                nc.scalar.activation(gn[:, 3, :], gn[:, 2, :], ACT.Sqrt).then_inc(gn_sqrt, 1)
                act.wait_ge(o_tr, t + 1)
                src = pB[:, 0, :].rearrange("p (g t) -> p g t", g=4)
                nc.scalar.copy(mixT[:, 0:4, ds(P * t, P)], src).then_inc(o_mix, 1)

            act.nop().then_inc(o_mix, 1)
            act.wait_ge(masks, MASKS)
            with act.Fori(0, PT) as t:
                tile(t, 0)
            tile(PT, 1)

        @block.tensor
        def _(pe):
            def tile(t, sample):
                pe.wait_ge(lora_in, t + 1)
                pe.wait_ge(o_mix, 1 + t)
                for q in range(4):
                    mm = nc.tensor.matmul(pA[:, 0, P * q:P * q + P], w2[0:64, P * q:P * q + P], low[0:64, 0, :],
                                          start=True, stop=True)
                for q in range(4):
                    mm = nc.tensor.matmul(pA[:, 1, P * q:P * q + P], w2[64:P, P * q:P * q + P], low[64:P, 0, :],
                                          start=True, stop=True)
                mm.then_inc(lora_out, 1)
                pe.wait_ge(kk_sq, t + 1)
                nc.tensor.matmul(pA[:, 2, :], pair1[:], t1[:], start=True, stop=True).then_inc(nrm, 1)
                pe.wait_ge(ch_ready, t + 1)
                for n in range(4):
                    for q in range(4):
                        src = (beta[:, q, :], kap[:, q, :], kr[:, q, 0, :], sh[:, 8 + q, :])[n]
                        mm = nc.tensor.transpose(pA[:, n, P * q:P * q + P], src, ident[:])
                    mm.then_inc(tr, 1)
                pe.wait_ge(tr_copied, 4 * t + 4)
                for g in range(2):
                    for h in range(4):
                        q, hf = 2 * g + h // 2, slice(64 * (h % 2), 64 * (h % 2) + 64)
                        if g and h == 0:
                            pe.wait_ge(o_copied, 2 * t + 1)
                        nc.tensor.matmul(pA[:, h, 0:256], beta[hf, q, :], kr[hf, q, :, :].rearrange("p z t -> p (z t)"),
                                         start=True, stop=True)
                        nc.tensor.matmul(pA[:, h, 256:512], kap[hf, q, :],
                                         kr[hf, q, :, :].rearrange("p z t -> p (z t)"),
                                         start=True, stop=True).then_inc(gram, 1)
                    pe.wait_ge(x0, 2 * t + g + 1)
                    for h in range(4):
                        mm = nc.tensor.transpose(pB[:, 1, P * h:P * h + P], XT[:, h, :], ident[:])
                    mm.then_inc(inv, 1)
                    for l in range(1, 6):
                        pe.wait_ge(inv_c, 20 * t + 10 * g + 2 * l - 1)
                        for h in range(4):
                            mm = nc.tensor.matmul(pB[:, 0, P * h:P * h + P], N[:, l, h, :], X[:, h, :],
                                                  start=True, stop=True)
                        mm.then_inc(inv, 1)
                        pe.wait_ge(inv_used, 10 * t + 5 * g + l)
                        for h in range(4):
                            mm = nc.tensor.matmul(pB[:, 1, P * h:P * h + P], Y[:, h, :], XT[:, h, :],
                                                  start=True, stop=True)
                        mm.then_inc(inv, 1)
                        if l < 5:
                            pe.wait_ge(inv_c, 20 * t + 10 * g + 2 * l)
                            for h in range(4):
                                mm = nc.tensor.transpose(pC[:, P * h:P * h + P], XT[:, h, :], ident[:])
                            mm.then_inc(x_turned, 1)
                    for h in range(4):
                        mm = nc.tensor.matmul(pC[:, 64 * h:64 * h + 64], G[:, h, 2, :], vt[:, 4 * g + h, :],
                                              start=True, stop=True)
                    mm.then_inc(mv, 1)
                    pe.wait_ge(inv_c, 20 * t + 10 * g + 10)
                    pe.wait_ge(mv_c, 2 * t + g + 1)
                    for h in range(4):
                        mm = nc.tensor.matmul(pD[:, P * h:P * h + P], XT[:, h, :],
                                              kv[:, 4 * g + h, :, :].rearrange("p z k -> p (z k)"),
                                              start=True, stop=True)
                    mm.then_inc(pgd, 1)
                    pe.wait_ge(pg_c, 2 * t + g + 1)
                    for h in range(4):
                        hh, n, hf = 4 * g + h, h // 2, slice(64 * (h % 2), 64 * (h % 2) + 64)
                        mm = nc.tensor.matmul(pC[hf, P * n:P * n + P], pg[:, hh, 0, :], G[:, h, 1, :],
                                              start=True, stop=True)
                    if not sample:
                        for h in range(4):
                            hh, n, hf = 4 * g + h, h // 2, slice(64 * (h % 2), 64 * (h % 2) + 64)
                            for cc in range(2):
                                rows = slice(64 * cc, 64 * cc + 64)
                                a0, b0 = slice(64 * n, 64 * n + 64), slice(P + 64 * n, P + 64 * n + 64)
                                nc.tensor.matmul(pB[hf, cc, a0], pg[rows, hh, 0, :], bt[rows, hh, :],
                                                 start=True, stop=True)
                                nc.tensor.matmul(pB[hf, cc, b0], kt[rows, hh, :], vt[rows, hh, :],
                                                 start=True, stop=False)
                                mm = nc.tensor.matmul(pB[hf, cc, b0], bt[rows, hh, :],
                                                      pg[rows, hh, 1, :], start=False, stop=True)
                    mm.then_inc(qab, 1)
                    pe.wait_ge(qab_used, 2 * t + g + 1)
                    if not sample:
                        for h in range(4):
                            hh, n, hf = 4 * g + h, h // 2, slice(64 * (h % 2), 64 * (h % 2) + 64)
                            oc = pA[:, h, 0:64]
                            nc.tensor.matmul(oc, G[:, h, 3, :], vt[:, hh, :], start=True, stop=False)
                            nc.tensor.matmul(oc, G[:, h, 1, :], pg[:, hh, 1, :], start=False, stop=True)
                        pe.wait_ge(st_new, 1 + 4 * t)
                        pe.nop().then_inc(state_seen, 1)
                        for h in range(4):
                            n, hf = h // 2, slice(64 * (h % 2), 64 * (h % 2) + 64)
                            nc.tensor.matmul(pA[0:64, h, 0:64], QT[hf, 2 * g + n, 0:64],
                                             St[hf, 0, 2 * g + n, :], start=False, stop=True, skip_group_check=True)
                        for h in range(4):
                            n, hf = h // 2, slice(64 * (h % 2), 64 * (h % 2) + 64)
                            mm = nc.tensor.matmul(pD[hf, 64 * n:64 * n + 64], AB[hf, 0, n, 0, :],
                                                  St[hf, 0, 2 * g + n, :], start=True, stop=True)
                        mm.then_inc(st_mm, 1)
                        pe.wait_ge(st_new, 1 + 4 * t + 2 * g + 1)
                        pe.nop().then_inc(state_seen, 1)
                        for h in range(4):
                            hh, n, hf = 4 * g + h, h // 2, slice(64 * (h % 2), 64 * (h % 2) + 64)
                            mm = nc.tensor.matmul(pA[64:P, h, 0:64], QT[hf, 2 * g + n, 64:P],
                                                  St[hf, 1, 2 * g + n, :], start=False, stop=True,
                                                  skip_group_check=True)
                        mm.then_inc(o_mm, 1)
                        for h in range(4):
                            n, hf = h // 2, slice(64 * (h % 2), 64 * (h % 2) + 64)
                            mm = nc.tensor.matmul(pD[hf, 64 * n:64 * n + 64], AB[hf, 0, n, 1, :],
                                                  St[hf, 1, 2 * g + n, :], start=True, stop=True)
                        mm.then_inc(st_mm, 1)
                    else:
                        for n in range(2):
                            q = 2 * g + n
                            pe.wait_ge(exq, 2 * g + n + 1)
                            for hf in range(2):
                                h = 2 * n + hf
                                hh, e = 4 * g + h, 4 * g + 2 * n + hf
                                rows = slice(64 * hf, 64 * hf + 64)
                                oc = pA[:, h, 0:64]
                                nc.tensor.matmul(oc, G[:, h, 3, :], vt[:, hh, :], start=True, stop=False)
                                nc.tensor.matmul(oc, G[:, h, 1, :], pg[:, hh, 1, :], start=False, stop=False)
                                for b in range(DB):
                                    mm = nc.tensor.matmul(oc, Qs[rows, b, :], Ss[rows, q, b, :], start=False,
                                                          stop=b == DB - 1)
                                if h == 3:
                                    mm.then_inc(o_mm, 1)
                                pe.wait_ge(exv, e + 1)
                                flat = lambda a: a.rearrange("p b k -> p (b k)")
                                nc.tensor.matmul(pB[rows, 0, :], pg[:, hh, 0, :], flat(ex[:, 0]), start=True, stop=True)
                                nc.tensor.matmul(pB[rows, 1, :], kt[:, hh, :], flat(ex[:, 1]), start=True, stop=False)
                                nc.tensor.matmul(pB[rows, 1, :], bt[:, hh, :], flat(ex[:, 2]), start=False,
                                                 stop=True).then_inc(ab_mm, 1)
                            pe.wait_ge(ab_used, 2 * g + n + 1)
                            for b in range(DB):
                                for hf in range(2):
                                    rows = slice(64 * hf, 64 * hf + 64)
                                    mm = nc.tensor.matmul(pC[rows, 64 * b:64 * b + 64], ABs[rows, 0, b, :],
                                                          Ss[rows, q, b, :], start=True, stop=True)
                            mm.then_inc(st_mm, 1)
                            pe.wait_ge(st_new, 1 + 4 * PT + 2 * g + n + 1)
                pe.wait_ge(st_new, 1 + 4 * t + 4)
                for q in range(4):
                    nc.tensor.matmul(pD[:, 2 * q:2 * q + 2], rk[:, P * q:P * q + P], hone[:], start=True, stop=True)
                nc.tensor.matmul(pC[:], low[:, 1, :], g2[:], start=True, stop=True).then_inc(gate, 1)
                pe.wait_ge(o_fin, t + 1)
                for q in range(4):
                    mm = nc.tensor.transpose(pB[:, 0, P * q:P * q + P],
                                             o[:, 2 * q:2 * q + 2, :].rearrange("p h k -> p (h k)"), ident[:])
                mm.then_inc(o_tr, 1)

            pe.nop().then_inc(gate, 1)
            pe.nop().then_inc(pgd, 1)
            pe.wait_ge(cin, CONSTS)
            pe.wait_ge(masks, MASKS)
            with pe.Fori(0, PT) as t:
                tile(t, 0)
            tile(PT, 1)
    return sems


FFN = 512
EXPERTS = 32
GROUPS4 = 4
PER_GROUP = EXPERTS // GROUPS4
TOPK = 2
MAX_BLOCKS = 2 * T // P + EXPERTS
SLOTS = MAX_BLOCKS * P
LOGITS = GROUPS4 + EXPERTS
MH = 4
MSCALE = 1.0 / 16.0


def mix_and_norm(nc, mixT, h1_d, io):
    with ExitStack() as c:
        def sb(name, shape, dt=F32):
            return c.enter_context(nc.sbuf_tensor(name, shape, dt))

        def sem(name):
            return c.enter_context(nc.semaphore(name))

        w = sb("w_out", [P, KT, D])
        g, b = sb("ln1_g", [P, D]), sb("ln1_b", [P, D])
        ms = sb("mix_tile", [P, 3, KT, P])
        x = sb("x_tile", [P, 3, D])
        r = sb("residual", [P, 3, D])
        st = sb("ln_stats", [P, 3, 16])
        bn = sb("bn_stats", [P, 2, 6])
        ps = c.enter_context(nc.psum_tensor("ps_mix", [P, 3, D], F32))
        cin, w_got = sem("ln1_in"), sem("w_out_in")
        x_got = [sem(f"x_tile_in_{u}") for u in range(3)]
        stored = [sem(f"h1_stored_{u}") for u in range(3)]
        staged, mm_done, ch, var, root = sem("mix_staged"), sem("mix_product"), sem("dve_chain3"), sem("ln1_var"), \
            sem("ln1_sqrt")
        normed, scaled, h_ready = sem("ln1_normed"), sem("ln1_scaled"), sem("h1_ready")
        aggr_begun = sem("ln1_aggregation_begun")
        block = c.enter_context(nc.Block())

        @block.sync
        def _(sp):
            for u in range(3):
                sp.nop().then_inc(stored[u], 16)
            sp.dma_start(w[:], io["w_out"]).then_inc(w_got, 16)
            sp.dma_start(g[:], io["ln1_g"].broadcast_to([P, D])).then_inc(cin, 16)
            sp.dma_start(b[:], io["ln1_b"].broadcast_to([P, D])).then_inc(cin, 16)
            with sp.Fori(0, 3) as i:
                for u in range(3):
                    sp.wait_ge(normed, 1 + 3 * i)
                    sp.dma_start(x[:, u, :], io["x"][ds(3 * P * i + P * u, P), :]).then_inc(x_got[u], 16)
                for u in range(3):
                    sp.wait_ge(h_ready, 3 * i + u + 1)
                    sp.dma_start(h1_d[ds(3 * P * i + P * u, P), :], r[:, u, :]).then_inc(stored[u], 16)
            for u in range(3):
                sp.wait_ge(stored[u], 64)

        @block.gpsimd
        def _(pool):
            pool.wait_ge(cin, 32)
            with pool.Fori(0, 3) as i:
                for u in range(3):
                    pool.wait_ge(mm_done, 1 + 3 * i)
                    nc.gpsimd.tensor_copy(ms[:, u, :, :], mixT[:, :, ds(3 * P * i + P * u, P)]).then_inc(staged, 1)
                for u in range(3):
                    pool.wait_ge(normed, 1 + 3 * i + u + 1)
                    nc.gpsimd.tensor_tensor(r[:, u, :], r[:, u, :], g[:], ALU.mult).then_inc(scaled, 1)
                    pool.wait_ge(scaled, 3 * i + u + 1)
                    nc.gpsimd.tensor_tensor(r[:, u, :], r[:, u, :], b[:], ALU.add).then_inc(h_ready, 1)

        @block.tensor
        def _(pe):
            pe.nop().then_inc(mm_done, 1)
            pe.wait_ge(w_got, 16)
            with pe.Fori(0, 3) as i:
                for u in range(3):
                    pe.wait_ge(staged, 3 * i + u + 1)
                    pe.wait_ge(normed, 1 + 3 * i)
                    for n in range(2):
                        for k in range(KT):
                            mm = nc.tensor.matmul(ps[:, u, HALF * n:HALF * n + HALF], ms[:, u, k, :],
                                                  w[:, k, HALF * n:HALF * n + HALF], start=k == 0, stop=k == KT - 1)
                    mm.then_inc(mm_done, 1)

        @block.scalar
        def _(act):
            with act.Fori(0, 3) as i:
                for u in range(3):
                    act.wait_ge(var, 3 * i + u + 1)
                    nc.scalar.activation(st[:, u, 3:4], st[:, u, 2:3], ACT.Sqrt).then_inc(root, 1)

        @block.vector
        def _(dve):
            dve.nop().then_inc(normed, 1)
            with dve.Fori(0, 3) as i:
                at = [0]

                def link(ins):
                    at[0] += 1
                    ins.then_inc(ch, 1)
                    dve.wait_ge(ch, 15 * i + at[0])

                for u in range(3):
                    dve.wait_ge(x_got[u], 16 * i + 16)
                    dve.wait_ge(mm_done, 1 + 3 * i + u + 1)
                    dve.wait_ge(stored[u], 16 * i + 16)
                    link(nc.vector.scalar_tensor_tensor(r[:, u, :], x[:, u, :], ALPHA, ps[:, u, :], ALU.mult, ALU.add))
                    for n in range(2):
                        ins = nc.vector.bn_stats(bn[:, n, :], r[:, u, HALF * n:HALF * n + HALF])
                    link(ins)
                    dve.nop().then_inc(aggr_begun, 1)
                    link(nc.vector.bn_aggr(st[:, u, 0:2], bn[:].rearrange("p n s -> p (n s)")))
                    link(nc.vector.tensor_scalar(st[:, u, 2:3], st[:, u, 1:2], LN_EPS, None, ALU.add))
                    dve.nop().then_inc(var, 1)
                    dve.wait_ge(root, 3 * i + u + 1)
                    link(nc.vector.reciprocal(st[:, u, 4:5], st[:, u, 3:4]))
                    nc.vector.tensor_scalar(r[:, u, :], r[:, u, :], st[:, u, 0:1], st[:, u, 4:5], ALU.subtract,
                                            ALU.mult).then_inc(normed, 1)


def memory_and_router(nc, ident, L, h1_d, h2_d, io):
    with ExitStack() as c:
        def sb(name, shape, dt=F32):
            return c.enter_context(nc.sbuf_tensor(name, shape, dt))

        def sem(name):
            return c.enter_context(nc.semaphore(name))

        wq, wo = sb("mem_wq", [P, KT, D]), sb("mem_wo", [P, KT, D])
        mkT, mv = sb("mem_kT", [P, KT, N_MEM]), sb("mem_v", [P, 2, D])
        g, b = sb("ln2_g", [P, D]), sb("ln2_b", [P, D])
        wr = sb("w_router", [P, KT, LOGITS])
        h1 = sb("h1", [P, D])
        hT = sb("h_T", [P, KT, P])
        q = sb("mem_q", [P, D])
        qT = sb("mem_qT", [P, KT, P + DS])
        S = sb("mem_probs", [P, 2 * D])
        PT_ = sb("mem_probs_T", [P, 16, P])
        oT = sb("mem_oT", [P, KT, P])
        r = sb("h2", [P, D])
        ck, cv = sb("cache_mem_kT", [P, 2, KT, N_MEM]), sb("cache_mem_v", [P, 2, 2, D])
        st = sb("mem_stats", [P, 4, 8])
        bn = sb("bn_stats2", [P, 2, 6])
        zero = sb("zero_row", [1, D])
        pT = c.enter_context(nc.psum_tensor("pT", [P, D], F32))
        pM = c.enter_context(nc.psum_tensor("pM", [P, D], F32))
        pS = c.enter_context(nc.psum_tensor("pS", [P, 2 * D], F32))

        kv_done, kv_copied, kv_out = sem("mem_product"), sem("mem_copied"), sem("mem_stored")
        kv_in, w_in_ = sem("mem_weights_in"), sem("attention_weights_in")
        with nc.Block() as block:
            @block.sync
            def _(sp):
                for k in range(4):
                    sp.dma_start(S[:, 512 * k:512 * k + 512].rearrange("p (a t) -> p a t", a=2),
                                 io["memT"][:, 2 * k:2 * k + 2, :]).then_inc(kv_in, 16)
                sp.dma_start(wq[:], io["mem_wk"]).then_inc(kv_in, 16)
                sp.dma_start(wo[:], io["mem_wv"]).then_inc(kv_in, 16)
                sp.dma_start(g[:], io["ln2_g"].broadcast_to([P, D])).then_inc(w_in_, 16)
                sp.dma_start(b[:], io["ln2_b"].broadcast_to([P, D])).then_inc(w_in_, 16)
                sp.dma_start(wr[:, :, 0:GROUPS4], io["w_group"]).then_inc(w_in_, 16)
                sp.dma_start(wr[:, :, GROUPS4:LOGITS], io["w_expert"]).then_inc(w_in_, 16)
                sp.wait_ge(kv_copied, 4)
                sp.dma_start(io["out_mem_k"], cv[:, 0, :, :]).then_inc(kv_out, 16)
                sp.wait_ge(kv_copied, 8)
                sp.dma_start(io["out_mem_v"], mv[:]).then_inc(kv_out, 16)
                sp.wait_ge(kv_done, 8)
                sp.dma_start(wq[:], io["mem_wq"]).then_inc(w_in_, 16)
                sp.dma_start(wo[:], io["mem_wo"]).then_inc(w_in_, 16)
                sp.wait_ge(kv_out, 32)
                sp.wait_ge(w_in_, 96)

            @block.tensor
            def _(pe):
                pe.wait_ge(kv_in, 96)
                mT = S[:].rearrange("p (k t) -> p k t", k=KT)
                for n in range(8):
                    wgt, m, h = (wq, wo)[n // 4], n // 2 % 2, n % 2
                    if n >= 2:
                        pe.wait_ge(kv_copied, n - 1)
                    for k in range(KT):
                        mm = nc.tensor.matmul(pM[:, HALF * (n % 2):HALF * (n % 2) + HALF], mT[:, k, P * m:P * m + P],
                                              wgt[:, k, HALF * h:HALF * h + HALF], start=k == 0, stop=k == KT - 1)
                    mm.then_inc(kv_done, 1)
                pe.wait_ge(kv_copied, 4)
                for n in range(4):
                    for j in range(4):
                        kt, m = (4 * n + j) // 2, j % 2
                        mm = nc.tensor.transpose(pS[:, HALF * n + P * j:HALF * n + P * j + P],
                                                 cv[:, 0, m, P * kt:P * kt + P], ident[:])
                    mm.then_inc(kv_done, 1)

            @block.scalar
            def _(act):
                for n in range(8):
                    m, h = n // 2 % 2, n % 2
                    act.wait_ge(kv_done, n + 1)
                    dst = (cv[:, 0, m, HALF * h:HALF * h + HALF], mv[:, m, HALF * h:HALF * h + HALF])[n // 4]
                    nc.scalar.copy(dst, pM[:, HALF * (n % 2):HALF * (n % 2) + HALF]).then_inc(kv_copied, 1)
                for n in range(4):
                    act.wait_ge(kv_done, 9 + n)
                    nc.scalar.copy(mkT[:, 2 * n:2 * n + 2, :].rearrange("p k t -> p (k t)"),
                                   pS[:, HALF * n:HALF * n + HALF]).then_inc(kv_copied, 1)
                act.wait_ge(kv_copied, 12)

        h_in, h_turned, hT_c = sem("h1_in"), sem("h_turned"), sem("h_T_copied")
        q_mm, q_c, q_turned, qT_c = sem("q_product"), sem("q_copied"), sem("q_turned"), sem("qT_copied")
        s_mm, s_max, s_exp, s_norm = sem("mem_scores"), sem("mem_max"), sem("mem_exp"), sem("mem_normed")
        p_turned, p_c, o_mm, o_c = sem("probs_turned"), sem("probs_T_copied"), sem("mem_o"), sem("mem_o_copied")
        y_mm, ch, var, root, h_out = sem("wo_product"), sem("dve_chain4"), sem("ln2_var"), sem("ln2_sqrt"), sem("h2_out")
        r_ready, lg_mm, lg_c, pad = sem("h2_ready"), sem("logits_ready"), sem("logits_copied"), sem("pads_zero")
        scaled, normed = sem("ln2_scaled"), sem("ln2_normed")
        aggr_begun = sem("ln2_aggregation_begun")
        k_in = [sem("cache_k_in_0"), sem("cache_k_in_1")]
        v_in = [sem("cache_v_in_0"), sem("cache_v_in_1")]
        block = c.enter_context(nc.Block())
        VCH = 11

        @block.sync
        def _(sp):
            sp.nop().then_inc(h_out, 16)
            for n in range(2):
                sp.dma_start(ck[:, n, :, :], io["cache_mem_kT"][n]).then_inc(k_in[n], 16)
                sp.dma_start(cv[:, n, :, :], io["cache_mem_v"][n]).then_inc(v_in[n], 16)

            def load(t):
                sp.wait_ge(r_ready, 1 + t)
                sp.dma_start(h1[:], h1_d[ds(P * t, P), :]).then_inc(h_in, 16)

            def store(t):
                sp.wait_ge(r_ready, 1 + t + 1)
                sp.dma_start(h2_d[ds(P * t, P), :], r[:]).then_inc(h_out, 16)

            with sp.Fori(0, PT) as t:
                load(t)
                store(t)
            load(PT)
            for s in range(2, DB):
                sp.wait_ge(s_mm, PT + s - 1)
                sp.dma_start(ck[:, s % 2, :, :], io["cache_mem_kT"][s]).then_inc(k_in[s % 2], 16)
            for s in range(2, DB):
                sp.wait_ge(o_mm, PT + s - 1)
                sp.dma_start(cv[:, s % 2, :, :], io["cache_mem_v"][s]).then_inc(v_in[s % 2], 16)
            store(PT)
            sp.wait_ge(pad, 2)
            sp.dma_start(h2_d[T:T + 1, :], zero[:]).then_inc(h_out, 16)
            sp.wait_ge(h_out, 16 * (NT + 2))

        @block.gpsimd
        def _(pool):
            pool.nop().then_inc(r_ready, 1)
            nc.gpsimd.memset(qT[:, :, P:P + DS], 0.0).then_inc(pad, 1)
            nc.gpsimd.memset(zero[:], 0.0).then_inc(pad, 1)
            with pool.Fori(0, NT) as t:
                pool.wait_ge(normed, t + 1)
                nc.gpsimd.tensor_tensor(r[:], r[:], g[:], ALU.mult).then_inc(scaled, 1)
                pool.wait_ge(scaled, t + 1)
                nc.gpsimd.tensor_tensor(r[:], r[:], b[:], ALU.add).then_inc(r_ready, 1)

        @block.tensor
        def _(pe):
            def tile(t, sample):
                pe.wait_ge(h_in, 16 * t + 16)
                for k in range(KT):
                    mm = nc.tensor.transpose(pT[:, P * k:P * k + P], h1[:, P * k:P * k + P], ident[:])
                mm.then_inc(h_turned, 1)
                pe.wait_ge(hT_c, 2 * t + 1)
                for n in range(2):
                    for k in range(KT):
                        mm = nc.tensor.matmul(pM[:, HALF * n:HALF * n + HALF], hT[:, k, :],
                                              wq[:, k, HALF * n:HALF * n + HALF], start=k == 0, stop=k == KT - 1)
                mm.then_inc(q_mm, 1)
                pe.wait_ge(q_c, t + 1)
                for k in range(KT):
                    mm = nc.tensor.transpose(pT[:, P * k:P * k + P], q[:, P * k:P * k + P], ident[:])
                mm.then_inc(q_turned, 1)
                pe.wait_ge(qT_c, t + 1)
                if not sample:
                    for h in range(MH):
                        for k in range(2):
                            mm = nc.tensor.matmul(pS[:, N_MEM * h:N_MEM * h + N_MEM], qT[:, 2 * h + k, 0:P],
                                                  mkT[:, 2 * h + k, :], start=k == 0, stop=k == 1)
                    mm.then_inc(s_mm, 1)
                    pe.wait_ge(s_norm, t + 1)
                    for n in range(2):
                        for j in range(4):
                            mm = nc.tensor.transpose(pT[:, HALF * n + P * j:HALF * n + P * j + P],
                                                     S[:, HALF * n + P * j:HALF * n + P * j + P], ident[:])
                    mm.then_inc(p_turned, 1)
                    pe.wait_ge(p_c, t + 1)
                    for cb in range(KT):
                        for k in range(2):
                            mm = nc.tensor.matmul(pM[:, P * cb:P * cb + P], mv[:, k, P * cb:P * cb + P],
                                                  PT_[:, 2 * (cb // 2) + k, :], start=k == 0, stop=k == 1)
                    mm.then_inc(o_mm, 1)
                else:
                    pe.wait_ge(pad, 1)
                    for s in range(DB):
                        pe.wait_ge(k_in[s % 2], 16 * (s // 2) + 16)
                        for h in range(MH):
                            for k in range(2):
                                mm = nc.tensor.matmul(pS[32 * h:32 * h + 32, N_MEM * s:N_MEM * s + N_MEM],
                                                      qT[:, 2 * h + k, DS * s:DS * s + 32],
                                                      ck[:, s % 2, 2 * h + k, :], start=k == 0, stop=k == 1)
                        mm.then_inc(s_mm, 1)
                    pe.wait_ge(s_norm, t + 1)
                    for n in range(2):
                        if n:
                            pe.wait_ge(p_c, t + 1)
                        for j in range(8):
                            mm = nc.tensor.transpose(pT[:, P * j:P * j + P],
                                                     S[:, P * (8 * n + j):P * (8 * n + j) + P], ident[:])
                        mm.then_inc(p_turned, 1)
                    pe.wait_ge(p_c, t + 2)
                    for s in range(DB):
                        pe.wait_ge(v_in[s % 2], 16 * (s // 2) + 16)
                        for cb in range(KT):
                            for k in range(2):
                                mm = nc.tensor.matmul(pM[:, P * cb + DS * s:P * cb + DS * s + DS],
                                                      cv[:, s % 2, k, P * cb:P * cb + P],
                                                      PT_[:, 2 * s + k, 32 * (cb // 2):32 * (cb // 2) + DS],
                                                      start=k == 0, stop=k == 1)
                        mm.then_inc(o_mm, 1)
                pe.wait_ge(o_c, t + 1)
                for n in range(2):
                    for k in range(KT):
                        mm = nc.tensor.matmul(pS[:, HALF * n:HALF * n + HALF], oT[:, k, :],
                                              wo[:, k, HALF * n:HALF * n + HALF], start=k == 0, stop=k == KT - 1)
                mm.then_inc(y_mm, 1)
                pe.wait_ge(r_ready, 1 + t + 1)
                for k in range(KT):
                    mm = nc.tensor.transpose(pT[:, P * k:P * k + P], r[:, P * k:P * k + P], ident[:])
                mm.then_inc(h_turned, 1)
                pe.wait_ge(hT_c, 2 * t + 2)
                for k in range(KT):
                    mm = nc.tensor.matmul(pM[:, 0:LOGITS], hT[:, k, :], wr[:, k, :], start=k == 0, stop=k == KT - 1)
                mm.then_inc(lg_mm, 1)
                pe.wait_ge(lg_c, t + 1)

            with pe.Fori(0, PT) as t:
                tile(t, 0)
            tile(PT, 1)

        @block.scalar
        def _(act):
            def copy_T(dst, src):
                for n in range(2):
                    ins = nc.scalar.copy(dst[:, 4 * n:4 * n + 4, 0:P],
                                         src[:, HALF * n:HALF * n + HALF].rearrange("p (k t) -> p k t", k=4))
                return ins

            def tile(t, sample):
                act.wait_ge(h_turned, 2 * t + 1)
                copy_T(hT, pT).then_inc(hT_c, 1)
                act.wait_ge(q_turned, t + 1)
                copy_T(qT, pT).then_inc(qT_c, 1)
                act.wait_ge(s_max, t + 1)
                parts = DB if sample else MH
                for h in range(parts):
                    ins = nc.scalar.activation(S[:, N_MEM * h:N_MEM * h + N_MEM], pS[:, N_MEM * h:N_MEM * h + N_MEM],
                                               ACT.Exp, bias=st[:, 1, h:h + 1], scale=MSCALE,
                                               accum_out=st[:, 2, h:h + 1])
                ins.then_inc(s_exp, 1)
                for n in range(2 if sample else 1):
                    act.wait_ge(p_turned, t + n + 1)
                    copy_T(PT_[:, 8 * n:8 * n + 8, :], pT).then_inc(p_c, 1)
                act.wait_ge(var, t + 1)
                nc.scalar.activation(st[:, 3, 3:4], st[:, 3, 2:3], ACT.Sqrt).then_inc(root, 1)
                act.wait_ge(h_turned, 2 * t + 2)
                copy_T(hT, pT).then_inc(hT_c, 1)

            with act.Fori(0, PT) as t:
                tile(t, 0)
            tile(PT, 1)

        @block.vector
        def _(dve):
            def tile(t, sample):
                at = [0]

                def link(ins):
                    at[0] += 1
                    ins.then_inc(ch, 1)
                    dve.wait_ge(ch, VCH * t + at[0])

                dve.wait_ge(q_mm, t + 1)
                nc.vector.tensor_copy(q[:], pM[:]).then_inc(q_c, 1)
                parts = DB if sample else MH
                w = N_MEM * parts
                dve.wait_ge(s_mm, t + parts if sample else t + 1)
                link(nc.vector.tensor_reduce(st[:, 0, 0:parts], pS[:, 0:w].rearrange("p (h m) -> p h m", m=N_MEM),
                                             AX.X, ALU.max))
                link(nc.vector.tensor_scalar(st[:, 1, 0:parts], st[:, 0, 0:parts], -MSCALE, None, ALU.mult))
                dve.nop().then_inc(s_max, 1)
                dve.wait_ge(s_exp, t + 1)
                link(nc.vector.reciprocal(st[:, 0, 0:parts], st[:, 2, 0:parts]))
                for h in range(parts):
                    ins = nc.vector.tensor_scalar(S[:, N_MEM * h:N_MEM * h + N_MEM], S[:, N_MEM * h:N_MEM * h + N_MEM],
                                                  st[:, 0, h:h + 1], None, ALU.mult)
                ins.then_inc(s_norm, 1)
                dve.wait_ge(o_mm, t + DB if sample else t + 1)
                nc.vector.tensor_copy(oT[:].rearrange("p k t -> p (k t)"), pM[:]).then_inc(o_c, 1)
                dve.wait_ge(y_mm, t + 1)
                dve.wait_ge(h_out, 16 * t + 16)
                link(nc.vector.scalar_tensor_tensor(r[:], h1[:], ALPHA, pS[:, 0:D], ALU.mult, ALU.add))
                for n in range(2):
                    ins = nc.vector.bn_stats(bn[:, n, :], r[:, HALF * n:HALF * n + HALF])
                link(ins)
                dve.nop().then_inc(aggr_begun, 1)
                link(nc.vector.bn_aggr(st[:, 3, 0:2], bn[:].rearrange("p n s -> p (n s)")))
                link(nc.vector.tensor_scalar(st[:, 3, 2:3], st[:, 3, 1:2], LN_EPS, None, ALU.add))
                dve.nop().then_inc(var, 1)
                dve.wait_ge(root, t + 1)
                link(nc.vector.reciprocal(st[:, 3, 4:5], st[:, 3, 3:4]))
                nc.vector.tensor_scalar(r[:], r[:], st[:, 3, 0:1], st[:, 3, 4:5], ALU.subtract,
                                        ALU.mult).then_inc(normed, 1)
                dve.wait_ge(lg_mm, t + 1)
                while at[0] < VCH - 1:
                    link(dve.nop())
                dst = L[:, ds(t, 1), :].rearrange("p o e -> p (o e)") if not sample else L[:, PT, :]
                link(nc.vector.tensor_copy(dst, pM[:, 0:LOGITS]))
                dve.nop().then_inc(lg_c, 1)

            with dve.Fori(0, PT) as t:
                tile(t, 0)
            tile(PT, 1)


def route(nc, L, rt, pool_dmas, io):
    with ExitStack() as c:
        def sb(name, shape, dt=F32):
            return c.enter_context(nc.sbuf_tensor(name, shape, dt))

        def sem(name):
            return c.enter_context(nc.semaphore(name))

        bias = sb("router_bias", [P, LOGITS])
        gl, eg = sb("group_logits", [P, NT, 4]), sb("group_hot", [P, NT, 4])
        gt, io4 = sb("group_tmp", [P, NT, 4]), sb("iota_4", [P, 4])
        el, tmp, pos = sb("expert_logits", [P, NT, EXPERTS]), sb("expert_tmp", [P, NT, EXPERTS]), sb(
            "positions", [P, NT, EXPERTS])
        oh = sb("expert_hot", [P, 2, NT, EXPERTS])
        both = sb("both_hot", [P, NT, EXPERTS])
        io32, ioi = sb("iota_32", [P, EXPERTS]), sb("iota_int", [P, MAX_BLOCKS + 2], I32)
        s = sb("route_scalars", [P, 10, NT])
        m2 = sb("slots_float", [P, 2, NT])
        upper, ones = sb("strict_upper", [P, P]), sb("all_ones", [P, P])
        cnt, cnti = sb("expert_counts", [P, 6, EXPERTS]), sb("expert_counts_int", [P, EXPERTS], I32)
        cmp_ = sb("block_compare", [P, MAX_BLOCKS + 2, EXPERTS])
        iob, be = sb("iota_blocks", [P, MAX_BLOCKS + 2]), sb("block_expert_float", [P, MAX_BLOCKS + 2])
        tok = sb("token_numbers", [P, NT], I32)
        pair = sb("slot_values", [P, 2, NT, 3], I32)
        fill = sb("empty_rows", [P, MAX_BLOCKS + 2, 3], I32)
        pr = c.enter_context(nc.psum_tensor("ps_rank", [P, HALF], F32))
        pc = c.enter_context(nc.psum_tensor("ps_count", [P, HALF], F32))
        b_in, io_done, ch, ex_in, ex = sem("router_bias_in"), sem("iotas"), sem("dve_chain5"), sem("exp_args"), sem("exps")
        hots, ranks, out, filled = sem("choices_ready"), sem("ranks_ready"), sem("slots_ready"), sem("slots_cleared")
        scat = pool_dmas["slots_scattered"]
        fills = sem("fill_made")
        block = c.enter_context(nc.Block())
        W = MAX_BLOCKS + 2

        @block.sync
        def _(sp):
            sp.dma_start(bias[:, 0:4], io["b_group"].broadcast_to([P, 4])).then_inc(b_in, 16)
            sp.dma_start(bias[:, 4:LOGITS], io["b_expert"].broadcast_to([P, EXPERTS])).then_inc(b_in, 16)
            sp.wait_ge(fills, 3)
            sp.dma_start(io["slots"].rearrange("(b p) z -> p b z", p=P), fill[:]).then_inc(filled, 16)
            sp.wait_ge(filled, 16)

        @block.gpsimd
        def _(pool):
            nc.gpsimd.iota(ioi[:], pattern=[[1, W]], base=0, channel_multiplier=0).then_inc(io_done, 1)
            nc.gpsimd.iota(tok[:], pattern=[[P, NT]], base=0, channel_multiplier=1).then_inc(io_done, 1)
            nc.gpsimd.memset(upper[:], 1.0).then_inc(io_done, 1)
            nc.gpsimd.memset(ones[:], 1.0).then_inc(io_done, 1)
            pool.wait_ge(io_done, 4)
            nc.gpsimd.affine_select(out=upper[:], in_=upper[:], compare_op=ALU.is_ge, fill=0.0, base=-1,
                                    pattern=[[1, P]], channel_multiplier=-1).then_inc(io_done, 1)
            nc.gpsimd.memset(fill[:, :, 0:1], T).then_inc(fills, 1)
            nc.gpsimd.memset(fill[:, :, 1:2], 0).then_inc(fills, 1)
            nc.gpsimd.iota(fill[:, :, 2], pattern=[[P, W]], base=2 * T, channel_multiplier=1).then_inc(fills, 1)
            pool.wait_ge(filled, 16)
            pool.wait_ge(out, 1)
            for t in range(NT):
                for z in range(2):
                    nc.gpsimd.indirect_dma_start(
                        out=io["slots"], out_offset=bass.IndirectOffsetOnAxis(ap=rt["slot"][:, z, t:t + 1], axis=0),
                        in_=pair[:, z, t, :], in_offset=None).then_inc(scat, 16)
            pool.wait_ge(scat, 16 * 2 * NT)

        @block.tensor
        def _(pe):
            pe.wait_ge(io_done, 5)
            pe.wait_ge(hots, 1)
            flat = both[:].rearrange("p t e -> p (t e)")
            nc.tensor.matmul(pr[:, 0:NT * EXPERTS], upper[:], flat, start=True, stop=True)
            nc.tensor.matmul(pc[:, 0:NT * EXPERTS], ones[:], flat, start=True, stop=True).then_inc(ranks, 1)

        @block.scalar
        def _(act):
            act.wait_ge(ex_in, 1)
            nc.scalar.activation(gt[:], gt[:], ACT.Exp)
            nc.scalar.activation(s[:, 5, :], s[:, 5, :], ACT.Exp).then_inc(ex, 1)

        @block.vector
        def _(dve):
            n = [0]

            def link(ins):
                n[0] += 1
                ins.then_inc(ch, 1)
                dve.wait_ge(ch, n[0])

            V = nc.vector

            def across(vec, k):
                return vec.rearrange("p (t o) -> p t o", o=1).broadcast_to([P, NT, k])

            def over(row, k):
                return row.rearrange("p (o k) -> p o k", o=1).broadcast_to([P, NT, k])

            def first_of_max(x, hot, scratch, io_row, k, mx, idx):
                link(V.tensor_reduce(mx, x, AX.X, ALU.max))
                link(V.tensor_tensor(hot, x, across(mx, k), ALU.is_equal))
                link(V.tensor_scalar(hot, hot, -1.0, -1000.0, ALU.add, ALU.mult))
                link(V.tensor_tensor(scratch, hot, over(io_row, k), ALU.add))
                link(V.tensor_reduce(idx, scratch, AX.X, ALU.min))
                link(V.tensor_tensor(hot, over(io_row, k), across(idx, k), ALU.is_equal))

            dve.wait_ge(b_in, 32)
            dve.wait_ge(io_done, 4)
            link(V.tensor_copy(iob[:], ioi[:]))
            link(V.tensor_copy(io4[:], iob[:, 0:4]))
            link(V.tensor_copy(io32[:], iob[:, 0:EXPERTS]))
            link(V.tensor_tensor(gl[:], L[:, :, 0:4], over(bias[:, 0:4], 4), ALU.add))
            link(V.tensor_tensor(el[:], L[:, :, 4:LOGITS], over(bias[:, 4:LOGITS], EXPERTS), ALU.add))
            first_of_max(gl[:], eg[:], gt[:], io4[:], 4, s[:, 0, :], s[:, 1, :])
            link(V.tensor_tensor(gt[:], gl[:], across(s[:, 0, :], 4), ALU.subtract))
            hot8 = eg[:].rearrange("p t (g o) -> p (t g) o", o=1).broadcast_to([P, NT * 4, PER_GROUP])
            e8 = lambda a: a.rearrange("p t (g e) -> p (t g) e", g=4)
            link(V.tensor_tensor(e8(tmp[:]), e8(el[:]), hot8, ALU.mult))
            link(V.tensor_scalar(eg[:], eg[:], -1.0, -NEG, ALU.add, ALU.mult))
            link(V.tensor_tensor(e8(el[:]), e8(tmp[:]), hot8, ALU.add))
            first_of_max(el[:], oh[:, 0], tmp[:], io32[:], EXPERTS, s[:, 2, :], s[:, 3, :])
            link(V.tensor_scalar(tmp[:], oh[:, 0], 3 * NEG, None, ALU.mult))
            link(V.tensor_tensor(el[:], el[:], tmp[:], ALU.add))
            first_of_max(el[:], oh[:, 1], tmp[:], io32[:], EXPERTS, s[:, 4, :], s[:, 3, :])
            link(V.tensor_tensor(s[:, 5, :], s[:, 4, :], s[:, 2, :], ALU.subtract))
            dve.nop().then_inc(ex_in, 1)
            link(V.tensor_tensor(both[:], oh[:, 0], oh[:, 1], ALU.add))
            dve.nop().then_inc(hots, 1)
            dve.wait_ge(ex, 1)
            link(V.tensor_reduce(s[:, 6, :], gt[:], AX.X, ALU.add))
            link(V.tensor_scalar(s[:, 7, :], s[:, 5, :], 1.0, None, ALU.add))
            link(V.tensor_tensor(s[:, 6, :], s[:, 6, :], s[:, 7, :], ALU.mult))
            link(V.reciprocal(s[:, 8, :], s[:, 6, :]))
            link(V.tensor_tensor(s[:, 9, :], s[:, 8, :], s[:, 5, :], ALU.mult))
            dve.wait_ge(ranks, 1)
            link(V.tensor_copy(pos[:].rearrange("p t e -> p (t e)"), pr[:, 0:NT * EXPERTS]))
            link(V.tensor_copy(cnt[:, 0, :], pc[:, 0:EXPERTS]))
            for t in range(1, NT):
                link(V.tensor_tensor(pos[:, t, :], pos[:, t, :], cnt[:, 0, :], ALU.add))
                link(V.tensor_tensor(cnt[:, 0, :], cnt[:, 0, :], pc[:, EXPERTS * t:EXPERTS * t + EXPERTS], ALU.add))
            link(V.tensor_scalar(cnt[:, 1, :], cnt[:, 0, :], float(P - 1), None, ALU.add))
            link(V.tensor_copy(cnti[:], cnt[:, 1, :]))
            link(V.tensor_scalar(cnti[:], cnti[:], 7, None, ALU.arith_shift_right))
            link(V.tensor_copy(cnt[:, 1, :], cnti[:]))
            link(V.memset(cnt[:, 2, :], 1.0))
            link(V.tensor_tensor_scan(cnt[:, 3, :], cnt[:, 2, :], cnt[:, 1, :], 0.0, ALU.mult, ALU.add))
            link(V.tensor_tensor(cnt[:, 4, :], cnt[:, 3, :], cnt[:, 1, :], ALU.subtract))
            link(V.tensor_scalar(cnt[:, 4, :], cnt[:, 4, :], float(P), None, ALU.mult))
            link(V.tensor_tensor(pos[:], pos[:], over(cnt[:, 4, :], EXPERTS), ALU.add))
            for z in range(2):
                link(V.tensor_tensor(tmp[:], pos[:], oh[:, z], ALU.mult))
                link(V.tensor_reduce(m2[:, z, :], tmp[:], AX.X, ALU.add))
                link(V.tensor_copy(pair[:, z, :, 0], tok[:]))
                link(V.tensor_copy(pair[:, z, :, 1].bitcast(F32), s[:, 8 + z, :]))
                link(V.tensor_scalar(pair[:, z, :, 2], tok[:], 2, z, ALU.mult, ALU.add))
            link(V.tensor_copy(rt["slot"][:], m2[:]))
            dve.nop().then_inc(out, 1)
            wide = lambda a: a.rearrange("p (b o) -> p b o", o=1).broadcast_to([P, W, EXPERTS])
            link(V.tensor_tensor(cmp_[:], wide(iob[:]),
                                 cnt[:, 3, :].rearrange("p (o e) -> p o e", o=1).broadcast_to([P, W, EXPERTS]),
                                 ALU.is_ge))
            link(V.tensor_reduce(be[:], cmp_[:], AX.X, ALU.add))
            link(V.tensor_scalar(be[:], be[:], float(EXPERTS - 1), None, ALU.min))
            link(V.tensor_copy(rt["block_expert"][:], be[:]))
            link(V.tensor_scalar(cnt[:, 5, 0:1], cnt[:, 3, EXPERTS - 1:EXPERTS], 1.0, None, ALU.add))
            link(V.tensor_copy(rt["pairs"][:], cnt[:, 5, 0:1]))
            link(V.tensor_scalar(rt["pairs"][:], rt["pairs"][:], 1, None, ALU.arith_shift_right))


def experts(nc, ident, rt, pool_dmas, h2_d, y_d, io):
    with ExitStack() as c:
        def sb(name, shape, dt=F32):
            return c.enter_context(nc.sbuf_tensor(name, shape, dt))

        def sem(name):
            return c.enter_context(nc.semaphore(name))

        w1, w3, w2 = sb("w1", [P, 2, KT, FFN]), sb("w3", [P, 2, KT, FFN]), sb("w2", [P, 2, FFN // P, D])
        tk, gt = sb("slots_to_gather", [P, 2, 3], I32), sb("slots_to_scatter", [P, 2, 3], I32)
        xg = sb("gathered", [P, 2, D])
        xT = sb("gathered_T", [P, 2, KT, P])
        sg, hb, hT = sb("sigmoid", [P, 2, FFN]), sb("hidden", [P, 2, FFN]), sb("hidden_T", [P, 2, FFN // P, P])
        y = sb("expert_out", [P, 2, D])
        pT = c.enter_context(nc.psum_tensor("pT2", [P, 2, HALF], F32))
        pH = c.enter_context(nc.psum_tensor("pH", [P, 2, 2, HALF], F32))
        pY = c.enter_context(nc.psum_tensor("pY", [P, 2, HALF], F32))
        w13_in = [sem(f"w1_w3_in_{u}") for u in range(2)]
        w2_in = [sem(f"w2_in_{u}") for u in range(2)]
        tk_in = [pool_dmas[f"tokens_in_{u}"] for u in range(2)]
        gt_in = [sem(f"gates_in_{u}") for u in range(2)]
        xg_in = [pool_dmas[f"rows_in_{u}"] for u in range(2)]
        y_out = [pool_dmas[f"outputs_scattered_{u}"] for u in range(2)]
        turned, xT_c, h_mm, sig, hid, h_turned, hT_c, y_mm, y_c, ch = (sem(n) for n in (
            "rows_turned", "rows_T_copied", "hidden_product", "sigmoid_ready", "hidden_ready", "hidden_turned",
            "hidden_T_copied", "out_product", "out_gated", "hidden_chain"))
        gather_begun, y_free = sem("gather_begun_moe"), sem("outputs_stored")
        block = c.enter_context(nc.Block())

        def passes(eng):
            return eng.value_load(rt["pairs"][0:1, 0:1], min_val=1, max_val=(MAX_BLOCKS + 1) // 2)

        @block.sync
        def _(sp):
            with sp.Fori(0, passes(sp)) as i:
                for u in range(2):
                    e = sp.value_load(rt["block_expert"][0:1, ds(2 * i + u, 1)], min_val=0, max_val=EXPERTS - 1)
                    sp.wait_ge(h_mm, 2 * i + u + 1)
                    sp.dma_start(w1[:, u, :, :].rearrange("p k (o n) -> p o k n", o=1),
                                 io["moe_w1"][:, ds(e, 1), :, :]).then_inc(w13_in[u], 16)
                    sp.dma_start(w3[:, u, :, :].rearrange("p k (o n) -> p o k n", o=1),
                                 io["moe_w3"][:, ds(e, 1), :, :]).then_inc(w13_in[u], 16)
                    sp.wait_ge(y_mm, 2 * i + u + 1)
                    sp.dma_start(w2[:, u, :, :].rearrange("p k (o n) -> p o k n", o=1),
                                 io["moe_w2"][:, ds(e, 1), :, :]).then_inc(w2_in[u], 16)
                for u in range(2):
                    sp.wait_ge(y_free, 1 + 2 * i)
                    sp.dma_start(gt[:, u, :], io["slots"][ds(2 * P * i + P * u, P), :]).then_inc(gt_in[u], 16)

        @block.gpsimd
        def _(pool):
            def gather(i, u):
                pool.dma_start(tk[:, u, :], io["slots"][ds(2 * P * i + P * u, P), :]).then_inc(tk_in[u], 16)
                pool.wait_ge(tk_in[u], 16 * i + 16)
                pool.nop().then_inc(gather_begun, 1)
                nc.gpsimd.indirect_dma_start(
                    out=xg[:, u, :], out_offset=None, in_=h2_d,
                    in_offset=bass.IndirectOffsetOnAxis(ap=tk[:, u, 0:1], axis=0)).then_inc(xg_in[u], 16)

            pool.nop().then_inc(y_free, 1)
            gather(0, 0)
            gather(0, 1)
            n = passes(pool)
            with pool.Fori(0, n) as i:
                for u in range(2):
                    pool.wait_ge(turned, 1 + 4 * i + 2 * u + 2)
                    pool.nop().then_inc(gather_begun, 1)
                    gather(i + 1, u)
                for u in range(2):
                    pool.wait_ge(y_c, 1 + 2 * i + u + 1)
                    pool.nop().then_inc(gather_begun, 1)
                    nc.gpsimd.indirect_dma_start(
                        out=y_d, out_offset=bass.IndirectOffsetOnAxis(ap=gt[:, u, 2:3], axis=0),
                        in_=y[:, u, :], in_offset=None).then_inc(y_out[u], 16)
                for u in range(2):
                    pool.wait_ge(y_out[u], 16 * i + 16)
                    pool.nop().then_inc(y_free, 1)
            for u in range(2):
                pool.wait_ge(xg_in[u], 16 * n + 16)
                pool.nop().then_inc(gather_begun, 1)

        @block.tensor
        def _(pe):
            pe.nop().then_inc(h_mm, 2)
            pe.nop().then_inc(y_mm, 2)
            pe.nop().then_inc(turned, 1)
            with pe.Fori(0, passes(pe)) as i:
                def hidden(u):
                    pe.wait_ge(xg_in[u], 16 * i + 16)
                    for z in range(2):
                        pe.wait_ge(xT_c, 1 + 4 * i + 2 * u + z)
                        for k in range(4):
                            c0 = P * (4 * z + k)
                            mm = nc.tensor.transpose(pT[:, 0, P * k:P * k + P], xg[:, u, c0:c0 + P], ident[:])
                        mm.then_inc(turned, 1)
                    pe.wait_ge(xT_c, 1 + 4 * i + 2 * u + 2)
                    pe.wait_ge(w13_in[u], 32 * i + 32)
                    pe.wait_ge(hid, 1 + 2 * i)
                    for z, w in enumerate((w1, w3)):
                        for k in range(KT):
                            mm = nc.tensor.matmul(pH[:, u, z, :], xT[:, u, k, :], w[:, u, k, :], start=k == 0,
                                                  stop=k == KT - 1)
                    mm.then_inc(h_mm, 1)

                def output(u):
                    pe.wait_ge(hid, 1 + 2 * i + u + 1)
                    pe.wait_ge(hT_c, 1 + 2 * i + u)
                    for k in range(4):
                        mm = nc.tensor.transpose(pT[:, 1, P * k:P * k + P], hb[:, u, P * k:P * k + P], ident[:])
                    mm.then_inc(h_turned, 1)
                    pe.wait_ge(hT_c, 1 + 2 * i + u + 1)
                    pe.wait_ge(w2_in[u], 16 * i + 16)
                    pe.wait_ge(y_c, 1 + 2 * i + u)
                    for z in range(2):
                        for k in range(4):
                            mm = nc.tensor.matmul(pY[:, z, :], hT[:, u, k, :], w2[:, u, k, HALF * z:HALF * z + HALF],
                                                  start=k == 0, stop=k == 3)
                    mm.then_inc(y_mm, 1)

                hidden(0)
                hidden(1)
                output(0)
                output(1)

        @block.scalar
        def _(act):
            for s in (xT_c, hT_c):
                act.nop().then_inc(s, 1)
            with act.Fori(0, passes(act)) as i:
                def rows(u):
                    for z in range(2):
                        act.wait_ge(turned, 1 + 4 * i + 2 * u + z + 1)
                        nc.scalar.copy(xT[:, u, 4 * z:4 * z + 4, :].rearrange("p k t -> p (k t)"),
                                       pT[:, 0, :]).then_inc(xT_c, 1)

                def sigmoid(u):
                    act.wait_ge(h_mm, 2 + 2 * i + u + 1)
                    nc.scalar.activation(sg[:, u, :], pH[:, u, 0, :], ACT.Sigmoid).then_inc(sig, 1)

                rows(0)
                rows(1)
                sigmoid(0)
                sigmoid(1)
                for u in range(2):
                    act.wait_ge(h_turned, 2 * i + u + 1)
                    nc.scalar.copy(hT[:, u, :, :].rearrange("p k t -> p (k t)"), pT[:, 1, :]).then_inc(hT_c, 1)

        @block.vector
        def _(dve):
            for s in (hid, y_c):
                dve.nop().then_inc(s, 1)
            with dve.Fori(0, passes(dve)) as i:
                for u in range(2):
                    dve.wait_ge(sig, 2 * i + u + 1)
                    nc.vector.tensor_tensor(sg[:, u, :], sg[:, u, :], pH[:, u, 0, :], ALU.mult).then_inc(ch, 1)
                    dve.wait_ge(ch, 2 * i + u + 1)
                    nc.vector.tensor_tensor(hb[:, u, :], sg[:, u, :], pH[:, u, 1, :], ALU.mult).then_inc(hid, 1)
                for u in range(2):
                    dve.wait_ge(y_mm, 2 + 2 * i + u + 1)
                    dve.wait_ge(gt_in[u], 16 * i + 16)
                    dve.wait_ge(y_free, 1 + 2 * i)
                    nc.vector.tensor_scalar(y[:, u, :], pY[:].rearrange("p z n -> p (z n)"),
                                            gt[:, u, 1:2].bitcast(F32), None, ALU.mult).then_inc(y_c, 1)


def combine(nc, h2_d, y_d, io):
    with ExitStack() as c:
        def sb(name, shape, dt=F32):
            return c.enter_context(nc.sbuf_tensor(name, shape, dt))

        def sem(name):
            return c.enter_context(nc.semaphore(name))

        g, b = sb("ln3_g", [P, D]), sb("ln3_b", [P, D])
        h, r = sb("h2_rows", [P, 3, D]), sb("out_rows", [P, 3, D])
        ya = sb("expert_rows", [P, 3, 2, D])
        st, bn = sb("ln3_stats", [P, 3, 16]), sb("bn_stats3", [P, 2, 6])
        cin = sem("ln3_in")
        h_in = [sem(f"h2_in_{u}") for u in range(3)]
        y_in = [sem(f"expert_rows_in_{u}") for u in range(3)]
        stored = [sem(f"y_stored_{u}") for u in range(3)]
        ch, var, root, normed, scaled, ready = (sem(n) for n in (
            "dve_chain6", "ln3_var", "ln3_sqrt", "ln3_normed", "ln3_scaled", "y_ready"))
        aggr_begun = sem("ln3_aggregation_begun")
        block = c.enter_context(nc.Block())

        @block.sync
        def _(sp):
            for u in range(3):
                sp.nop().then_inc(stored[u], 16)
            sp.dma_start(g[:], io["ln3_g"].broadcast_to([P, D])).then_inc(cin, 16)
            sp.dma_start(b[:], io["ln3_b"].broadcast_to([P, D])).then_inc(cin, 16)
            with sp.Fori(0, 3) as i:
                for u in range(3):
                    sp.wait_ge(normed, 1 + 3 * i)
                    sp.dma_start(h[:, u, :], h2_d[ds(3 * P * i + P * u, P), :]).then_inc(h_in[u], 16)
                    sp.dma_start(ya[:, u, :, :], y_d[ds(6 * P * i + 2 * P * u, 2 * P), :].rearrange(
                        "(p z) n -> p z n", z=2)).then_inc(y_in[u], 16)
                for u in range(3):
                    sp.wait_ge(ready, 3 * i + u + 1)
                    sp.dma_start(io["out_y"][ds(3 * P * i + P * u, P), :], r[:, u, :]).then_inc(stored[u], 16)
            for u in range(3):
                sp.wait_ge(stored[u], 64)

        @block.scalar
        def _(act):
            with act.Fori(0, 3) as i:
                for u in range(3):
                    act.wait_ge(var, 3 * i + u + 1)
                    nc.scalar.activation(st[:, u, 3:4], st[:, u, 2:3], ACT.Sqrt).then_inc(root, 1)

        @block.vector
        def _(dve):
            dve.nop().then_inc(normed, 1)
            dve.wait_ge(cin, 32)
            with dve.Fori(0, 3) as i:
                at = [0]

                def link(ins):
                    at[0] += 1
                    ins.then_inc(ch, 1)
                    dve.wait_ge(ch, 24 * i + at[0])

                for u in range(3):
                    dve.wait_ge(h_in[u], 16 * i + 16)
                    dve.wait_ge(y_in[u], 16 * i + 16)
                    dve.wait_ge(stored[u], 16 * i + 16)
                    link(nc.vector.scalar_tensor_tensor(r[:, u, :], h[:, u, :], ALPHA, ya[:, u, 0, :], ALU.mult,
                                                        ALU.add))
                    link(nc.vector.tensor_tensor(r[:, u, :], r[:, u, :], ya[:, u, 1, :], ALU.add))
                    for n in range(2):
                        ins = nc.vector.bn_stats(bn[:, n, :], r[:, u, HALF * n:HALF * n + HALF])
                    link(ins)
                    dve.nop().then_inc(aggr_begun, 1)
                    link(nc.vector.bn_aggr(st[:, u, 0:2], bn[:].rearrange("p n s -> p (n s)")))
                    link(nc.vector.tensor_scalar(st[:, u, 2:3], st[:, u, 1:2], LN_EPS, None, ALU.add))
                    dve.nop().then_inc(var, 1)
                    dve.wait_ge(root, 3 * i + u + 1)
                    link(nc.vector.reciprocal(st[:, u, 4:5], st[:, u, 3:4]))
                    link(nc.vector.tensor_scalar(r[:, u, :], r[:, u, :], st[:, u, 0:1], st[:, u, 4:5], ALU.subtract,
                                                 ALU.mult))
                    dve.nop().then_inc(normed, 1)
                    link(nc.vector.tensor_tensor(r[:, u, :], r[:, u, :], g[:], ALU.mult))
                    nc.vector.tensor_tensor(r[:, u, :], r[:, u, :], b[:], ALU.add).then_inc(ready, 1)


def setup(nc, xT, ident, io):
    with nc.semaphore("x_in") as x_in, nc.semaphore("zeroed") as zeroed, nc.semaphore("ident_made") as made:
        sems = [x_in, zeroed, made]
        with nc.Block() as block:
            @block.sync
            def _(sp):
                sp.dma_start(xT[:], io["xT"]).then_inc(x_in, 16)
                sp.wait_ge(x_in, 16)

            @block.gpsimd
            def _(pool):
                nc.gpsimd.memset(ident[:], 0.0).then_inc(zeroed, 1)
                pool.wait_ge(zeroed, 1)
                nc.gpsimd.affine_select(out=ident[:], in_=ident[:], compare_op=ALU.not_equal, fill=1.0, base=0,
                                        pattern=[[-1, P]], channel_multiplier=1).then_inc(made, 1)
                pool.wait_ge(made, 1)
    return sems


def clear(nc, sems):
    with nc.Block() as block:
        @block.gpsimd
        def _(pool):
            for s in sems:
                pool.sem_clear(s)


def program(nc, io):
    with ExitStack() as c:
        ident = c.enter_context(nc.sbuf_tensor("ident", [P, P], F32))
        L = c.enter_context(nc.sbuf_tensor("router_logits", [P, NT, LOGITS], F32))
        rt = {
            "slot": c.enter_context(nc.sbuf_tensor("choice_slots", [P, 2, NT], I32)),
            "block_expert": c.enter_context(nc.sbuf_tensor("block_expert", [P, MAX_BLOCKS + 2], I32)),
            "pairs": c.enter_context(nc.sbuf_tensor("block_pairs", [P, 1], I32)),
        }
        pool_dmas = {n: c.enter_context(nc.semaphore(n)) for n in (
            "w_even_in", "w_odd_in", "shift_loaded", "slots_scattered", "tokens_in_0", "tokens_in_1", "rows_in_0", "rows_in_1",
            "outputs_scattered_0", "outputs_scattered_1")}
        with nc.sbuf_tensor("mixT", [P, KT, T], F32) as mixT:
            with nc.sbuf_tensor("xT", [P, KT, T], F32) as xT:
                sems = setup(nc, xT, ident, io)
                sems += attention_heads(nc, xT, mixT, ident, io)
                sems += rwkv_projection(nc, xT, pool_dmas, io["pa"], io)
            sems += rwkv(nc, mixT, ident, io["pa"], io)
            clear(nc, sems)
            mix_and_norm(nc, mixT, io["h1"], io)
        memory_and_router(nc, ident, L, io["h1"], io["h2"], io)
        route(nc, L, rt, pool_dmas, io)
        experts(nc, ident, rt, pool_dmas, io["h2"], io["y_rows"], io)
        combine(nc, io["h2"], io["y_rows"], io)


def kernel(**inputs):
    import numpy as np
    import concourse.bacc as bacc
    from concourse.bass_utils import run_bass_kernel_spmd

    nc = bacc.Bacc("TRN2", target_bir_lowering=False, num_devices=1)
    a = {k: np.ascontiguousarray(v) for k, v in inputs.items()}
    arrays, io = {}, {}

    def give(name, array):
        array = np.ascontiguousarray(array)
        arrays["in_" + name] = array
        io[name] = nc.dram_tensor("in_" + name, array.shape, mybir.dt.from_np(array.dtype), kind="ExternalInput").ap()
        return io[name]

    def take(name, shape):
        io[name] = nc.dram_tensor(name, shape, F32, kind="ExternalOutput").ap()

    x_all = np.concatenate([a["x_prompt"].reshape(SEQ, D), a["x_sample"].reshape(DB * DS, D)])
    io["xT"] = give("xT_", x_all.T).rearrange("(k p) t -> p k t", p=P)
    give("w_in", a["w_in"][0])
    io["w_in_diff"] = io["w_in"][:, C_RWKV:C_IN].rearrange("(k p) (s n) -> p k s n", p=P, s=3)
    give("cache_kT", a["cache_diff_k"][0].transpose(1, 0, 3, 2))
    give("cache_diff_v", a["cache_diff_v"])
    for n in ("diff_lq1", "diff_lk1", "diff_lq2", "diff_lk2"):
        give(n, a[n])
    give("subln", a["diff_subln"].reshape(P, 1))
    per_block = lambda v, n: v.reshape(n, P).T
    per_pair = lambda v: per_block(v, 4)
    io["w_in_rwkv"] = io["w_in"][:, 0:C_RWKV].rearrange("(k p) (c n) -> p k c n", p=P, n=P)
    give("shiftT", a["state_shift"].reshape(DB, NB, P).transpose(2, 1, 0))
    for n in ("w0", "a0", "k_k", "k_a", "r_k"):
        give(n, per_pair(a["rwkv_" + n]))
    give("mu", per_block(a["rwkv_mu"], NB))
    for n in ("w2", "a2", "g2"):
        give(n, a["rwkv_" + n][0])
    give("rwkv_ln_w", a["rwkv_ln_w"])
    give("rwkv_ln_b", a["rwkv_ln_b"])
    give("state", a["state_rwkv"].reshape(DB, 4, 2, 64, 64).transpose(2, 4, 1, 0, 3).reshape(P, 4, DB, 64))
    io["pa"] = nc.dram_tensor("pa_rows", (P, NB, XW), F32, kind="Internal").ap()
    give("x", x_all)
    rows = lambda w: w.rearrange("(k p) n -> p k n", p=P)
    for n in ("w_out", "mem_wq", "mem_wk", "mem_wv", "mem_wo"):
        io[n] = rows(give(n, a[n][0]))
    for n in ("ln1_g", "ln1_b", "ln2_g", "ln2_b", "ln3_g", "ln3_b"):
        give(n, a[n])
    io["memT"] = rows(give("memT", a["mem_prompt"][0].T))
    io["w_group"] = rows(give("w_group", a["moe_w_group"][0]))
    io["w_expert"] = rows(give("w_expert", a["moe_w_expert"][0]))
    give("b_group", a["moe_b_group"])
    give("b_expert", a["moe_b_expert"])
    io["cache_mem_kT"] = give("cache_mem_kT", a["cache_mem_k"][0].transpose(0, 2, 1)).rearrange(
        "b (k p) m -> b p k m", p=P)
    io["cache_mem_v"] = give("cache_mem_v", a["cache_mem_v"][0]).rearrange("b (m p) n -> b p m n", p=P)
    for n in ("w1", "w3", "w2"):
        io["moe_" + n] = give("moe_" + n, a["moe_" + n][0]).rearrange("e (k p) n -> p e k n", p=P)
    io["h1"] = nc.dram_tensor("h1_rows", (T, D), F32, kind="Internal").ap()
    io["h2"] = nc.dram_tensor("h2_rows_and_zero", (T + 1, D), F32, kind="Internal").ap()
    io["y_rows"] = nc.dram_tensor("y_rows", (2 * T + SLOTS + 2 * P, D), F32, kind="Internal").ap()
    io["slots"] = nc.dram_tensor("slots", (SLOTS + 2 * P, 3), I32, kind="Internal").ap()
    take("out_y", (T, D))
    take("out_mem_k_rows", (N_MEM, D))
    take("out_mem_v_rows", (N_MEM, D))
    for n in ("out_mem_k", "out_mem_v"):
        io[n] = io[n + "_rows"].rearrange("(m p) n -> p m n", p=P)
    take("out_shift", (P, NB, DB + 1))
    take("out_state_prompt", (P, 4, 64))
    take("out_state_sample", (P, 4, DB, 64))
    take("out_diff_k_prompt", (HEADS, SEQ, P))
    take("out_diff_v_prompt", (HEADS, SEQ, P))
    take("out_diff_k_sample", (HEADS, P, P))
    take("out_diff_v_sample", (HEADS, P, P))
    program(nc, io)
    r = run_bass_kernel_spmd(nc, [arrays], core_ids=[0]).results[0]
    sample = lambda o: o.reshape(HEADS, DB, DS, P).transpose(1, 0, 2, 3)[None]
    shift = r["out_shift"].transpose(2, 1, 0).reshape(DB + 1, C_RWKV)
    st_p = r["out_state_prompt"].reshape(2, 64, 4, 64).transpose(2, 0, 3, 1).reshape(1, 1, RH, 64, 64)
    st_s = r["out_state_sample"].reshape(2, 64, 4, DB, 64).transpose(3, 2, 0, 4, 1).reshape(1, DB, RH, 64, 64)
    return (r["out_y"][None, 0:SEQ], r["out_y"][SEQ:T].reshape(DB, DS, D), r["out_diff_k_prompt"][None, None], r["out_diff_v_prompt"][None, None],
            r["out_mem_k_rows"][None, None], r["out_mem_v_rows"][None, None], st_p, shift[None, None, 0:1],
            sample(r["out_diff_k_sample"]), sample(r["out_diff_v_sample"]), st_s, shift[None, 1:, None])
```

```python
from contextlib import ExitStack

import concourse.bass as bass
from concourse import mybir

F32 = mybir.dt.float32
I32 = mybir.dt.int32
U32 = mybir.dt.uint32
ALU = mybir.AluOpType
ACT = mybir.ActivationFunctionType
AX = mybir.AxisListType
ds = bass.ds

P = 128
D = 1024
KT = D // P
SEQ = 1024
PT = SEQ // P
DB, DS = 8, 16
T = SEQ + DB * DS
NT = T // P
CHUNK = 64
HEADS = 4
QK = 64
C_RWKV = 1792
D_RWKV = 512
C_IN = 3328
PAST = 256
N_MEM = 256
NEG = -1e30
LAM_INIT = 0.2
ALPHA = 2.0 ** 0.25
LN_EPS = 1e-5
HALF = 512


def attention_heads(nc, xT, mixT, ident, io):
    c = ExitStack()
    with c:
        def sb(name, shape, dt=F32):
            return c.enter_context(nc.sbuf_tensor(name, shape, dt))

        sems = []

        def sem(name):
            sems.append(c.enter_context(nc.semaphore(name)))
            return sems[-1]

        wh = sb("w_head", [P, KT, 3, P])
        qT = sb("qT", [P, T + DS])
        kT = sb("kT", [P, T])
        v = sb("v_tok", [P, NT, P])
        ktok = sb("k_tok", [P, NT, P])
        kc = sb("k_cache_T", [P, 2, 4, PAST])
        vc = sb("v_cache", [P, 2, 4, 2, P])
        S = sb("scores", [P, 2, 2, SEQ])
        at = sb("attn", [P, 2, SEQ])
        aT = sb("attn_T", [P, 8, P])
        osb = sb("o_units", [P, 10, P])
        tabP = sb("bias_prompt", [P, SEQ])
        tabS = sb("bias_sample", [P, 2, 384])
        itmp = sb("iota_tmp", [P, SEQ], I32)
        stat = sb("softmax_stats", [P, 2, 8])
        ss = sb("o_square_sums", [P, 10])
        rst = sb("o_rstd", [P, 2, 10])
        sq = sb("square_scratch", [P, P])
        sub = sb("subln", [P, 1])
        lqk = sb("lambda_vectors", [P, 4, QK])
        lam = sb("lambda_terms", [P, 8])
        psS = c.enter_context(nc.psum_tensor("psS", [P, 2, SEQ], F32))
        psT = c.enter_context(nc.psum_tensor("psT", [P, 2, HALF], F32))
        psO = c.enter_context(nc.psum_tensor("psO", [P, HALF], F32))

        consts_in, w_in_, caches_in = sem("consts_in"), sem("w_head_in"), sem("caches_in")
        iota_done, tables = sem("iota_done"), sem("tables_done")
        pj_full, pj_evac = sem("transposed_ready"), sem("transposed_copied")
        s_ready, s_biased, s_exp = sem("scores_ready"), sem("scores_biased"), sem("scores_exp")
        at_ready, pv_done, o_saved = sem("attn_ready"), sem("pv_done"), sem("o_saved")
        dvec, actc = sem("dve_chain"), sem("lambda_exps")
        rms_var, rms_sqrt, o_scaled = sem("rms_var"), sem("rms_sqrt"), sem("o_scaled")
        bias_begun, scores_begun = sem("bias_begun"), sem("scores_begun")
        proj_done, kv_out = sem("projections_done"), sem("kv_stored")

        width = [P * (u + 1) for u in range(PT)] + [384, 384]
        groups = [-(-w // HALF) for w in width]
        NPROJ = 12
        JOBS = NPROJ + sum(groups) + 3
        first_job = [NPROJ + sum(groups[:u]) for u in range(10)]
        CH = T // 3

        block = c.enter_context(nc.Block())

        @block.sync
        def _(sp):
            sp.nop().then_inc(kv_out, 16)
            sp.dma_start(sub[:], io["subln"]).then_inc(consts_in, 16)
            for n, name in enumerate(("diff_lq1", "diff_lk1", "diff_lq2", "diff_lk2")):
                sp.dma_start(lqk[:, n, :], io[name].broadcast_to([P, QK])).then_inc(consts_in, 16)
            with sp.Fori(0, HEADS) as h:
                sp.wait_ge(proj_done, 1 + h)
                for n in range(3):
                    sp.dma_start(wh[:, :, n, :], io["w_in_diff"][:, :, n, ds(h * P, P)]).then_inc(w_in_, 16)
                sp.wait_ge(pv_done, 1 + 10 * h)
                for g in range(2):
                    sp.dma_start(kc[:, g, :, :], io["cache_kT"][ds(h, 1), 4 * g:4 * g + 4, :, :].rearrange(
                        "o b d k -> d (o b) k")).then_inc(caches_in, 16)
                    for b in range(4):
                        sp.dma_start(vc[:, g, b, :, :], io["cache_diff_v"][0, 4 * g + b, ds(h, 1), :, :].rearrange(
                            "o (t p) d -> p (o t) d", p=P)).then_inc(caches_in, 16)
                sp.wait_ge(pj_evac, 1 + JOBS * h + NPROJ)
                sp.dma_start(io["out_diff_k_prompt"][ds(h, 1), :, :].rearrange("o (t p) d -> p (o t) d", p=P),
                             ktok[:, 0:PT, :]).then_inc(kv_out, 16)
                sp.dma_start(io["out_diff_v_prompt"][ds(h, 1), :, :].rearrange("o (t p) d -> p (o t) d", p=P),
                             v[:, 0:PT, :]).then_inc(kv_out, 16)
                sp.dma_start(io["out_diff_k_sample"][ds(h, 1), :, :].rearrange("o p d -> p (o d)"),
                             ktok[:, PT, :]).then_inc(kv_out, 16)
                sp.dma_start(io["out_diff_v_sample"][ds(h, 1), :, :].rearrange("o p d -> p (o d)"),
                             v[:, PT, :]).then_inc(kv_out, 16)
            sp.wait_ge(kv_out, 16 + 64 * HEADS)

        @block.gpsimd
        def _(pool):
            nc.gpsimd.iota(itmp[:, :], pattern=[[-1, SEQ]], base=SEQ - P, channel_multiplier=1).then_inc(iota_done, 1)
            pool.wait_ge(tables, 1)
            for r in range(4):
                q = slice(32 * r, 32 * r + 32)
                nc.gpsimd.iota(itmp[q, 0:PAST], pattern=[[-1, PAST]], base=PAST, channel_multiplier=1)
                nc.gpsimd.iota(itmp[q, PAST:PAST + DS], pattern=[[-1, DS]], base=0,
                               channel_multiplier=1).then_inc(iota_done, 1)

        @block.vector
        def _(dve):
            chained = [0]

            def then(ins):
                chained[0] += 1
                ins.then_inc(dvec, 1)
                dve.wait_ge(dvec, chained[0])

            dve.nop().then_inc(s_biased, 1)
            slope = 8.0 * 2.0 ** -2
            dve.wait_ge(iota_done, 1)
            then(nc.vector.tensor_copy(tabP[:], itmp[:]))
            then(nc.vector.scalar_tensor_tensor(S[:, 0, 0, :], tabP[:], -1.0, tabP[:], ALU.mult, ALU.max))
            ins = nc.vector.tensor_scalar(tabP[:], S[:, 0, 0, :], -slope, None, ALU.mult)
            then(ins)
            nc.vector.memset(tabP[0:CHUNK, SEQ - CHUNK:SEQ], NEG).then_inc(tables, 1)
            dve.wait_ge(iota_done, 5)
            then(nc.vector.tensor_copy(S[:, 0, 0, 0:PAST + DS], itmp[:, 0:PAST + DS]))
            then(nc.vector.scalar_tensor_tensor(S[:, 1, 0, 0:PAST + DS], S[:, 0, 0, 0:PAST + DS], -1.0,
                                                S[:, 0, 0, 0:PAST + DS], ALU.mult, ALU.max))
            then(nc.vector.memset(tabS[:], NEG))
            for g in range(2):
                nc.vector.tensor_scalar(tabS[:, g, 0:PAST], S[:, 1, 0, 0:PAST], -slope, None, ALU.mult)
                for r in range(4):
                    q = slice(32 * r, 32 * r + 32)
                    o = PAST + DS * (4 * g + r)
                    ins = nc.vector.tensor_scalar(tabS[q, g, o:o + DS], S[q, 1, 0, PAST:PAST + DS], -slope, None,
                                                  ALU.mult)
            then(ins)
            then(nc.vector.memset(qT[:, T:T + DS], 0.0))
            dve.wait_ge(consts_in, 80)
            for n in range(2):
                then(nc.vector.tensor_tensor_reduce(sq[:, 0:QK], lqk[:, 2 * n, :], lqk[:, 2 * n + 1, :], 1.0, 0.0,
                                                    ALU.mult, ALU.add, lam[:, n:n + 1]))
            then(nc.vector.tensor_scalar(sub[:], sub[:], 1.0 - LAM_INIT, None, ALU.mult))
            dve.nop().then_inc(tables, 1)
            dve.wait_ge(actc, 1)
            then(nc.vector.tensor_tensor(lam[:, 4:5], lam[:, 3:4], lam[:, 2:3], ALU.subtract))
            then(nc.vector.tensor_scalar(lam[:, 5:6], lam[:, 4:5], -LAM_INIT, None, ALU.add))
            SETUP = chained[0]
            CHAIN = 10 * 2 + 10 * 4 + 3

            with dve.Fori(0, HEADS) as h:
                at_link = [0]

                def link(ins):
                    at_link[0] += 1
                    ins.then_inc(dvec, 1)
                    dve.wait_ge(dvec, CHAIN * h + SETUP + at_link[0])

                def bias_and_max(u):
                    dve.wait_ge(s_ready, 10 * h + u + 1)
                    dve.nop().then_inc(bias_begun, 1)
                    w = width[u]
                    tab = tabP[:, SEQ - w:SEQ] if u < PT else tabS[:, u - PT, :]
                    st = stat[:, u % 2, :]
                    for k in range(2):
                        ins = nc.vector.tensor_tensor_reduce(S[:, u % 2, k, 0:w], psS[:, k, 0:w], tab, 1.0, -3e38,
                                                             ALU.add, ALU.max, st[:, k:k + 1])
                    link(ins)
                    link(nc.vector.tensor_scalar(st[:, 2:4], st[:, 0:2], -0.125, None, ALU.mult))
                    dve.nop().then_inc(s_biased, 1)

                def combine(u):
                    dve.wait_ge(s_exp, 20 * h + 2 * u + 2)
                    w = width[u]
                    st = stat[:, u % 2, :]
                    link(nc.vector.reciprocal(st[:, 6:8], st[:, 4:6]))
                    link(nc.vector.tensor_scalar(st[:, 7:8], st[:, 7:8], lam[:, 5:6], None, ALU.mult))
                    link(nc.vector.tensor_scalar(S[:, u % 2, 1, 0:w], S[:, u % 2, 1, 0:w], st[:, 7:8], None, ALU.mult))
                    if u >= 2:
                        dve.wait_ge(pj_full, JOBS * h + first_job[u - 2] + groups[u - 2])
                    link(nc.vector.scalar_tensor_tensor(at[:, u % 2, 0:w], S[:, u % 2, 0, 0:w], st[:, 6:7],
                                                        S[:, u % 2, 1, 0:w], ALU.mult, ALU.add))
                    dve.nop().then_inc(at_ready, 1)

                bias_and_max(0)
                for u in range(10):
                    if u < 9:
                        bias_and_max(u + 1)
                    combine(u)
                nc.vector.tensor_scalar(tabP[:], tabP[:], 0.25, None, ALU.mult)
                nc.vector.tensor_scalar(tabS[:], tabS[:], 0.25, None, ALU.mult)
                dve.wait_ge(o_saved, 10 * h + 10)
                link(nc.vector.tensor_scalar(rst[:, 0, :], ss[:], 1.0 / P, 1e-5, ALU.mult, ALU.add))
                dve.nop().then_inc(rms_var, 1)
                dve.wait_ge(rms_sqrt, h + 1)
                link(nc.vector.reciprocal(rst[:, 0, :], rst[:, 1, :]))
                for u in range(10):
                    ins = nc.vector.tensor_scalar(osb[:, u, :], osb[:, u, :], rst[:, 0, u:u + 1], None, ALU.mult)
                link(ins)
                dve.nop().then_inc(o_scaled, 1)
                assert at_link[0] == CHAIN

        @block.scalar
        def _(act):
            act.nop().then_inc(pj_evac, 1)
            act.wait_ge(tables, 2)
            nc.scalar.activation(lam[:, 2:4], lam[:, 0:2], ACT.Exp).then_inc(actc, 1)
            with act.Fori(0, HEADS) as h:
                job = [0]

                def bank():
                    j = job[0]
                    job[0] += 1
                    act.wait_ge(pj_full, JOBS * h + j + 1)
                    return psT[:, j % 2, :]

                act.wait_ge(kv_out, 16 + 64 * h)
                for n in range(3):
                    nc.scalar.copy(qT[:, CH * n:CH * n + CH], bank()[:, 0:CH]).then_inc(pj_evac, 1)
                for n in range(3):
                    nc.scalar.copy(kT[:, CH * n:CH * n + CH], bank()[:, 0:CH]).then_inc(pj_evac, 1)
                for dst in (v, ktok):
                    for n in range(3):
                        k = min(4, NT - 4 * n)
                        nc.scalar.copy(dst[:, 4 * n:4 * n + k, :].rearrange("p t d -> p (t d)"),
                                       bank()[:, 0:k * P]).then_inc(pj_evac, 1)

                def exponentials(u):
                    act.wait_ge(s_biased, 1 + 10 * h + u + 1)
                    w, st = width[u], stat[:, u % 2, :]
                    for k in range(2):
                        nc.scalar.activation(S[:, u % 2, k, 0:w], S[:, u % 2, k, 0:w], ACT.Exp, bias=st[:, 2 + k:3 + k],
                                             scale=0.125, accum_out=st[:, 4 + k:5 + k]).then_inc(s_exp, 1)

                exponentials(0)
                for u in range(10):
                    if u < 9:
                        exponentials(u + 1)
                    for g in range(groups[u]):
                        k = min(HALF, width[u] - HALF * g)
                        nc.scalar.copy(aT[:, 4 * g:4 * g + k // P, :].rearrange("p t d -> p (t d)"),
                                       bank()[:, 0:k]).then_inc(pj_evac, 1)
                    act.wait_ge(pv_done, 1 + 10 * h + u + 1)
                    nc.scalar.copy(osb[:, u, :], psO[:, 0:P])
                    nc.scalar.activation(sq[:], psO[:, 0:P], ACT.Square, accum_out=ss[:, u:u + 1]).then_inc(o_saved, 1)
                act.wait_ge(rms_var, h + 1)
                nc.scalar.activation(rst[:, 1, :], rst[:, 0, :], ACT.Sqrt).then_inc(rms_sqrt, 1)
                for n in range(2):
                    nc.scalar.activation(mixT[:, ds(4 + h, 1), HALF * n:HALF * n + HALF].rearrange("p o t -> p (o t)"),
                                         bank(), ACT.Copy, scale=sub[:, 0:1]).then_inc(pj_evac, 1)
                src = bank()[:, 0:2 * P].rearrange("p (b i) -> p b i", i=32)[:, :, 0:DS]
                dst = mixT[:, ds(4 + h, 1), SEQ:T].rearrange("p o (b i) -> p (o b) i", i=DS)
                nc.scalar.activation(dst, src, ACT.Copy, scale=sub[:, 0:1]).then_inc(pj_evac, 1)
                assert job[0] == JOBS

        @block.tensor
        def _(pe):
            pe.nop().then_inc(proj_done, 1)
            pe.nop().then_inc(pv_done, 1)
            pe.wait_ge(tables, 2)
            with pe.Fori(0, HEADS) as h:
                job = [0]

                def bank():
                    j = job[0]
                    job[0] += 1
                    pe.wait_ge(pj_evac, 1 + JOBS * h + max(j - 1, 0))
                    return psT[:, j % 2, :]

                pe.wait_ge(w_in_, 48 * h + 48)
                for n in range(2):
                    for q in range(3):
                        o = bank()
                        for k in range(KT):
                            mm = nc.tensor.matmul(o[:, 0:CH], wh[:, k, n, :], xT[:, k, CH * q:CH * q + CH],
                                                  start=k == 0, stop=k == KT - 1)
                        mm.then_inc(pj_full, 1)
                for q in range(3):
                    o = bank()
                    for t in range(4 * q, min(4 * q + 4, NT)):
                        for k in range(KT):
                            mm = nc.tensor.matmul(o[:, (t % 4) * P:(t % 4) * P + P], xT[:, k, P * t:P * t + P],
                                                  wh[:, k, 2, :], start=k == 0, stop=k == KT - 1)
                    mm.then_inc(pj_full, 1)
                pe.wait_ge(pj_evac, 1 + JOBS * h + 6)
                for q in range(3):
                    o = bank()
                    for t in range(4 * q, min(4 * q + 4, NT)):
                        mm = nc.tensor.transpose(o[:, (t % 4) * P:(t % 4) * P + P], kT[:, P * t:P * t + P], ident[:])
                        if t == 0:
                            mm.then_inc(proj_done, 1)
                    mm.then_inc(pj_full, 1)

                def scores(u):
                    pe.wait_ge(s_biased, 1 + 10 * h + u)
                    pe.nop().then_inc(scores_begun, 1)
                    for k in range(2):
                        r = slice(QK * k, QK * k + QK)
                        if u < PT:
                            for c0 in range(0, width[u], HALF):
                                n = min(HALF, width[u] - c0)
                                mm = nc.tensor.matmul(psS[:, k, c0:c0 + n], qT[r, P * u:P * u + P], kT[r, c0:c0 + n],
                                                      start=True, stop=True)
                        else:
                            g = u - PT
                            for j in range(4):
                                o = SEQ + DS * (4 * g + j)
                                rows = slice(32 * j, 32 * j + 32)
                                nc.tensor.matmul(psS[rows, k, 0:PAST], qT[r, o:o + 32], kc[r, g, j, :],
                                                 start=True, stop=True)
                                mm = nc.tensor.matmul(psS[rows, k, PAST:384], qT[r, o:o + 32], kT[r, SEQ:T],
                                                      start=True, stop=True)
                    mm.then_inc(s_ready, 1)

                def weighted_values(u):
                    pe.wait_ge(at_ready, 10 * h + u + 1)
                    nb = width[u] // P
                    for g in range(groups[u]):
                        o = bank()
                        for b in range(4 * g, min(4 * g + 4, nb)):
                            mm = nc.tensor.transpose(o[:, (b % 4) * P:(b % 4) * P + P],
                                                     at[:, u % 2, P * b:P * b + P], ident[:])
                        mm.then_inc(pj_full, 1)
                    pe.wait_ge(pj_evac, 1 + JOBS * h + first_job[u] + groups[u])
                    if u < PT:
                        for b in range(nb):
                            mm = nc.tensor.matmul(psO[:, 0:P], aT[:, b, :], v[:, b, :], start=b == 0, stop=b == nb - 1)
                    else:
                        g = u - PT
                        for j in range(4):
                            rows = slice(32 * j, 32 * j + 32)
                            for b in range(3):
                                rhs = vc[:, g, j, b, :] if b < 2 else v[:, PT, :]
                                mm = nc.tensor.matmul(psO[rows, 0:P], aT[:, b, rows], rhs, start=b == 0, stop=b == 2)
                    mm.then_inc(pv_done, 1)

                pe.wait_ge(pj_evac, 1 + JOBS * h + NPROJ)
                pe.wait_ge(caches_in, 160 * h + 160)
                scores(0)
                for u in range(10):
                    if u < 9:
                        scores(u + 1)
                    weighted_values(u)
                pe.wait_ge(o_scaled, h + 1)
                for q in range(3):
                    o = bank()
                    for u in range(4 * q, min(4 * q + 4, 10)):
                        mm = nc.tensor.transpose(o[:, (u % 4) * P:(u % 4) * P + P], osb[:, u, :], ident[:])
                    mm.then_inc(pj_full, 1)
                assert job[0] == JOBS
            pe.wait_ge(pj_evac, 1 + JOBS * HEADS)
    return sems


RH = 8
NB = C_RWKV // P
XW = 1 + SEQ + DB * (DS + 1)
TW = DB * (DS + 1)
DECAY = 0.6065306597126334


def rwkv_projection(nc, xT, pool_dmas, pa_d, io):
    with ExitStack() as c:
        def sb(name, shape, dt=F32):
            return c.enter_context(nc.sbuf_tensor(name, shape, dt))

        sems = []

        def sem(name):
            sems.append(c.enter_context(nc.semaphore(name)))
            return sems[-1]

        w = sb("w_block", [P, 2, KT, P])
        row = sb("pa_row", [P, 2, XW])
        shift = sb("shift_in", [P, NB, DB])
        last = sb("shift_out", [P, NB, DB + 1])
        ps = c.enter_context(nc.psum_tensor("ps_proj", [P, 6, HALF], F32))
        w_got, s_in = [pool_dmas["w_even_in"], pool_dmas["w_odd_in"]], pool_dmas["shift_loaded"]
        full, copied, zero = sem("proj_full"), sem("proj_copied"), sem("row_zeroed")
        row_ready, row_out, last_out = sem("row_ready"), sem("row_stored"), sem("shift_stored")
        block = c.enter_context(nc.Block())
        GROUPS = [(0, HALF), (HALF, HALF), (SEQ, P)]

        @block.sync
        def _(sp):
            sp.nop().then_inc(row_out, 16)
            sp.wait_ge(zero, 1)
            with sp.Fori(0, NB // 2) as i:
                for b in range(2):
                    sp.wait_ge(row_ready, 1 + 2 * i + b + 1)
                    sp.dma_start(pa_d[:, ds(2 * i + b, 1), :].rearrange("p o x -> p (o x)"),
                                   row[:, b, :]).then_inc(row_out, 16)
            sp.wait_ge(row_ready, 1 + NB)
            sp.dma_start(io["out_shift"], last[:]).then_inc(last_out, 16)
            sp.wait_ge(row_out, 16 + 16 * NB)
            sp.wait_ge(last_out, 16)

        @block.gpsimd
        def _(pool):
            nc.gpsimd.memset(row[:, :, 0:1], 0.0).then_inc(zero, 1)
            pool.dma_start(shift[:], io["shiftT"]).then_inc(s_in, 16)
            with pool.Fori(0, NB // 2) as i:
                for b in range(2):
                    pool.wait_ge(full, 1 + 6 * i)
                    pool.dma_start(w[:, b, :, :].rearrange("p k (o n) -> p k o n", o=1),
                                 io["w_in_rwkv"][:, :, ds(2 * i + b, 1), :]).then_inc(w_got[b], 16)

        @block.scalar
        def _(act):
            act.nop().then_inc(row_ready, 1)
            act.wait_ge(s_in, 16)
            with act.Fori(0, NB // 2) as i:
                for b in range(2):
                    act.wait_ge(row_out, 16 + 32 * i)
                    for q, (c0, n) in enumerate(GROUPS):
                        act.wait_ge(full, 1 + 6 * i + 3 * b + q + 1)
                        if q < 2:
                            nc.scalar.copy(row[:, b, 1 + c0:1 + c0 + n], ps[:, 3 * b + q, 0:n]).then_inc(copied, 1)
                        else:
                            dst = row[:, b, 1 + SEQ:XW].rearrange("p (b i) -> p b i", i=DS + 1)
                            src = ps[:, 3 * b + q, 0:n].rearrange("p (b i) -> p b i", i=DS)
                            nc.scalar.copy(dst[:, :, 1:DS + 1], src).then_inc(copied, 1)
                            nc.scalar.copy(last[:, ds(2 * i + b, 1), 1:DB + 1].rearrange("p o b -> p (o b)"),
                                           src[:, :, DS - 1])
                            nc.scalar.copy(dst[:, :, 0],
                                           shift[:, ds(2 * i + b, 1), :].rearrange("p o b -> p (o b)"))
                            nc.scalar.copy(last[:, ds(2 * i + b, 1), 0:1].rearrange("p o b -> p (o b)"),
                                           ps[:, 3 * b + 1, HALF - 1:HALF]).then_inc(row_ready, 1)

        @block.tensor
        def _(pe):
            pe.nop().then_inc(full, 1)
            with pe.Fori(0, NB // 2) as i:
                for b in range(2):
                    pe.wait_ge(w_got[b], 16 * i + 16)
                    for q, (c0, n) in enumerate(GROUPS):
                        pe.wait_ge(row_ready, 1 + 2 * i)
                        for k in range(KT):
                            mm = nc.tensor.matmul(ps[:, 3 * b + q, 0:n], w[:, b, k, :], xT[:, k, c0:c0 + n],
                                                  start=k == 0, stop=k == KT - 1)
                        mm.then_inc(full, 1)
    return sems


def rwkv(nc, mixT, ident, pa_d, io):
    with ExitStack() as c:
        def sb(name, shape, dt=F32):
            return c.enter_context(nc.sbuf_tensor(name, shape, dt))

        sems = []

        def sem(name):
            sems.append(c.enter_context(nc.semaphore(name)))
            return sems[-1]

        vecs = sb("rwkv_vectors", [P, 6, 4])
        mu = sb("mu", [P, NB])
        w2 = sb("w2_a2", [P, D_RWKV])
        g2 = sb("g2", [P, D_RWKV])
        lnw = sb("gn_w", [P, D_RWKV])
        lnb = sb("gn_b", [P, D_RWKV])
        pair1 = sb("pair_ones", [P, P])
        hone = sb("head_ones", [P, 2])
        i64 = sb("ident_64_twice", [P, 64])
        cmask = [sb(f"causal_{n}", [P, 4, P]) for n in ("prompt", "sample")]
        lmask = sb("level_masks", [P, 6, P])
        notfirst = [sb(f"not_first_{n}", [P, HALF]) for n in ("prompt", "sample")]
        oneseq = sb("rows_of_sequence", [P, DB])
        colseq = sb("cols_of_sequence", [P, DB, P])
        x = sb("pa_tile", [P, NB, TW])
        sh = sb("shifted", [P, NB, P])
        low = sb("lora_in", [P, 2, 2, P])
        dec = sb("decay", [P, HALF])
        rate = sb("rate", [P, HALF])
        kk = sb("kk", [P, HALF])
        t1 = sb("scratch_1", [P, HALF])
        t2 = sb("scratch_2", [P, HALF])
        W = sb("decay_product", [P, 2, HALF])
        beta = sb("beta", [P, 2, 4, P])
        kap = sb("kappa", [P, 2, 4, P])
        kr = sb("khat_rho", [P, 2, 4, 2, P])
        rk = sb("bonus_products", [P, 2, HALF])
        bt = sb("beta_tok", [P, 2, RH, 64])
        kt = sb("kappa_tok", [P, 2, RH, 64])
        kv = sb("khat_tok_and_mv", [P, 2, RH, 2, 64])
        vt = sb("v_tok_rwkv", [P, 2, RH, 64])
        pg = sb("minus_p_g", [P, RH, 2, 64])
        G = sb("grams", [P, 2, 4, 4, P])
        N = sb("level_n", [P, 2, 2, 4, P])
        XT = sb("x_transposed", [P, 2, 4, P])
        X = sb("x_inverse", [P, 2, 4, P])
        Y = sb("y_level", [P, 2, 4, P])
        QT = sb("q_transposed", [P, 4, P])
        AB = sb("a_b", [P, 2, 2, 2, 2, 64])
        St = sb("state", [P, 2, 4, 64])
        ABs = kr[:, 1].rearrange("p g z t -> p (g z t)").rearrange("p (z b k) -> p z b k", z=2, b=DB)
        Qs = kv[:, 1].rearrange("p h z k -> p (h z k)").rearrange("p (b t) -> p b t", b=DB)
        ex = sb("values_by_sequence", [P, 3, DB, 64])
        Ss = sb("state_sample", [P, 4, DB, 64])
        So = sb("state_sample_new", [P, 4, DB, 64])
        o = sb("o_rwkv", [P, RH, 64])
        o2 = sb("o_scratch", [P, RH, 64])
        gn = sb("gn_stats", [P, 5, RH])

        ps = c.enter_context(nc.psum_tensor("ps_rwkv", [P, 8, HALF], F32))

        cin, masks, x_got = sem("rwkv_consts_in"), sem("masks_made"), sem("pa_tile_in")
        x_used, fch, vch, tch = sem("pa_tile_used"), sem("dve_chain_front"), sem("dve_chain_solve"), sem("dve_chain_tail")
        mixed, lora_in, lora_out, lora_used = sem("shift_mixed"), sem("lora_in_ready"), sem("lora_out_ready"), sem(
            "lora_out_used")
        sig, decays, kk_sq, nrm = sem("sigmoids"), sem("decays_ready"), sem("kk_squares"), sem("norms_summed")
        nrm_root, gn_var, gn_root = sem("norms_rooted"), sem("gn_var"), sem("gn_root")
        ch_ready, tr, tr_copied = sem("channel_values_ready"), sem("turned"), sem("turned_copied")

        def of_group(name):
            return [sem(f"{name}_{g}") for g in range(2)]

        gram, gram_used, lev = of_group("gram_ready"), of_group("gram_masked"), of_group("level_masked")
        x0, nx, y_ready = of_group("x0_ready"), of_group("n_x_product"), of_group("y_ready")
        x_mm, x_c = of_group("x_product"), of_group("x_copied")
        mv, mv_c, pgd, pg_c = of_group("mv_ready"), of_group("mv_copied"), of_group("pg_ready"), of_group("pg_copied")
        qab, qab_used = of_group("q_a_b_ready"), of_group("q_a_b_used")
        st_mm, st_new = of_group("state_product"), of_group("state_updated")
        o_mm, o_copied = of_group("o_ready"), of_group("o_copied")
        gate, o_fin, o_tr, o_mix = sem("gate_ready"), sem("o_final"), sem("o_turned"), sem("o_in_mix")
        st_out, exq, ab_mm, exv = sem("states_stored"), sem("q_expanded"), sem("ab_ready"), sem("values_expanded")
        ab_used, state_seen = sem("ab_used"), sem("state_seen")
        block = c.enter_context(nc.Block())
        CONSTS = 16 * 12
        MASKS = 82

        def bc(vec, n):
            return vec.rearrange("p (g o) -> p g o", o=1).broadcast_to([P, vec.shape[1], n])

        def g4(ap):
            return ap.rearrange("p (g t) -> p g t", g=4)

        def flat(ap):
            return ap.rearrange("p a b -> p (a b)")

        def last_level(sample):
            return 3 if sample else 5

        def first(t):
            return isinstance(t, int) and t == 0

        def after_is_sample(t):
            return int(isinstance(t, int) and t == PT - 1)

        def levels_before(t):
            return 6 * t

        def each_tile(eng, front, solve, tail):
            front(0, 0, 0)
            solve(0, 0, 0)
            with eng.Fori(0, (PT - 2) // 2) as i:
                solve(2 * i + 1, 1, 0)
                solve(2 * i + 2, 0, 0)
            solve(PT - 1, 1, 0)
            solve(PT, 0, 1)
            tail(PT, 0)

        @block.sync
        def _(sp):
            for n, name in enumerate(("w0", "a0", "k_k", "k_a", "r_k")):
                sp.dma_start(vecs[:, n, :], io[name]).then_inc(cin, 16)
            sp.dma_start(mu[:], io["mu"]).then_inc(cin, 16)
            sp.dma_start(w2[0:64, :], io["w2"]).then_inc(cin, 16)
            sp.dma_start(w2[64:P, :], io["a2"]).then_inc(cin, 16)
            sp.dma_start(g2[:], io["g2"]).then_inc(cin, 16)
            sp.dma_start(lnw[:], io["rwkv_ln_w"].broadcast_to([P, D_RWKV])).then_inc(cin, 16)
            sp.dma_start(lnb[:], io["rwkv_ln_b"].broadcast_to([P, D_RWKV])).then_inc(cin, 16)
            sp.dma_start(Ss[:], io["state"]).then_inc(cin, 16)
            with sp.Fori(0, PT) as t:
                sp.wait_ge(x_used, 1 + t)
                sp.dma_start(x[:, :, 0:P + 1], pa_d[:, :, ds(P * t, P + 1)]).then_inc(x_got, 16)
            sp.wait_ge(x_used, 1 + PT)
            sp.dma_start(x[:, :, :], pa_d[:, :, 1 + SEQ:XW]).then_inc(x_got, 16)
            for g in range(2):
                sp.wait_ge(st_new[g], 2 * PT)
            sp.dma_start(io["out_state_prompt"], St[:, 0, :, :]).then_inc(st_out, 16)
            for g in range(2):
                sp.wait_ge(st_new[g], 2 * PT + 2)
            sp.dma_start(io["out_state_sample"], So[:]).then_inc(st_out, 16)
            sp.wait_ge(st_out, 32)

        @block.gpsimd
        def _(pool):
            made = [0]

            def then(ins):
                made[0] += 1
                ins.then_inc(masks, 1)
                pool.wait_ge(masks, made[0])

            def keep(ap, pattern, base, mult, cmp=ALU.is_ge, fill=0.0):
                then(nc.gpsimd.affine_select(out=ap, in_=ap, compare_op=cmp, fill=fill, base=base, pattern=pattern,
                                             channel_multiplier=mult))

            def blocks(ap, size):
                v = ap.rearrange("p (b i) -> p b i", i=size)
                keep(v, [[-size, P // size], [0, size]], 0, 1)
                keep(v, [[size, P // size], [0, size]], size - 1, -1)

            for m, size in ((cmask[0], CHUNK), (cmask[1], DS)):
                for n, (value, strict) in enumerate(((-1.0, 1), (1.0, 0), (1.0, 1), (1.0, 0))):
                    then(nc.gpsimd.memset(m[:, n, :], value))
                    keep(m[:, n, :], [[1, P]], -strict, -1)
                    blocks(m[:, n, :], size)
            for l in range(6):
                s = 1 << l
                then(nc.gpsimd.memset(lmask[:, l, :], 1.0))
                blocks(lmask[:, l, :], 2 * s)
                v = lmask[:, l, :].rearrange("p (b i) -> p b i", i=2 * s)
                keep(v, [[2 * s, P // (2 * s)], [0, 2 * s]], s - 1, -1)
                keep(v, [[0, P // (2 * s)], [1, 2 * s]], -s, 0)
            for m, size in ((notfirst[0], CHUNK), (notfirst[1], DS)):
                then(nc.gpsimd.memset(m[:], 1.0))
                then(nc.gpsimd.memset(m[:].rearrange("p (b i) -> p b i", i=size)[:, :, 0:1], 0.0))
            then(nc.gpsimd.memset(pair1[:], 1.0))
            blocks(pair1[:], 64)
            then(nc.gpsimd.memset(hone[:], 1.0))
            keep(hone[:], [[-64, 2]], 0, 1)
            keep(hone[:], [[64, 2]], 63, -1)
            then(nc.gpsimd.memset(i64[:], 0.0))
            keep(i64[:], [[-1, 64]], 0, 1, ALU.not_equal, 1.0)
            keep(i64[:], [[-1, 64]], -64, 1, ALU.not_equal, 1.0)
            then(nc.gpsimd.memset(oneseq[:], 1.0))
            keep(oneseq[:], [[-DS, DB]], 0, 1)
            keep(oneseq[:], [[DS, DB]], DS - 1, -1)
            then(nc.gpsimd.memset(colseq[:], 1.0))
            keep(colseq[:], [[-DS, DB], [1, P]], 0, 0)
            keep(colseq[:], [[DS, DB], [-1, P]], DS - 1, 0)
            then(nc.gpsimd.memset(St[:, 0, :, :], 0.0))
            assert made[0] == MASKS, made[0]

            def levels(t, u, sample):
                for l in range(last_level(sample) + 1):
                    for g in range(2):
                        if l == 0:
                            pool.wait_ge(gram_used[g], 4 * t + 4)
                        elif l == 2:
                            pool.wait_ge(x0[g], t + 1)
                        elif l > 2:
                            pool.wait_ge(nx[g], 5 * t + l - 2)
                        nc.gpsimd.tensor_tensor(N[:, g, l % 2, :, :], G[:, g, :, 0, :],
                                                lmask[:, l:l + 1, :].broadcast_to([P, 4, P]),
                                                ALU.mult).then_inc(lev[g], 1)

            each_tile(pool, lambda t, u, s: None, levels, lambda t, u: None)

        FCH, VCH, TCH = 21, 2, 11

        @block.vector
        def _(dve):
            def chain(signal, before):
                at = [0]

                def link(ins):
                    at[0] += 1
                    ins.then_inc(signal, 1)
                    dve.wait_ge(signal, before + at[0])
                return link

            def shift(t, sample):
                link = chain(fch, 1 + FCH * t)
                if sample:
                    xv = x[:].rearrange("p c (b i) -> p c b i", i=DS + 1)
                    cur, prev = xv[:, :, :, 1:DS + 1], xv[:, :, :, 0:DS]
                    shv = sh[:].rearrange("p c (b i) -> p c b i", i=DS)
                else:
                    cur, prev, shv = x[:, :, 1:P + 1], x[:, :, 0:P], sh[:]
                dve.wait_ge(x_got, 16 * t + 16)
                dve.wait_ge(tr, 1 + 4 * t)
                if sample:
                    for n in range(NB):
                        ins = nc.vector.tensor_tensor(shv[:, n], prev[:, n], cur[:, n], ALU.subtract)
                else:
                    ins = nc.vector.tensor_tensor(shv, prev, cur, ALU.subtract)
                link(ins)
                link(nc.vector.tensor_tensor(sh[:], sh[:], bc(mu[:], P), ALU.mult))
                if sample:
                    for n in range(NB):
                        ins = nc.vector.tensor_tensor(shv[:, n], shv[:, n], cur[:, n], ALU.add)
                else:
                    ins = nc.vector.tensor_tensor(shv, shv, cur, ALU.add)
                link(ins)
                dve.nop().then_inc(mixed, 1)
                dve.nop().then_inc(x_used, 1)

            def lora_sums(t):
                link = chain(fch, 1 + FCH * t + 3)
                dve.wait_ge(lora_out, t + 1)
                nc.vector.tensor_tensor(g4(dec[:]), g4(ps[:, 3, :]), bc(vecs[:, 0, :], P), ALU.add)
                link(nc.vector.tensor_tensor(g4(rate[:]), g4(ps[:, 7, :]), bc(vecs[:, 1, :], P), ALU.add))
                dve.nop().then_inc(lora_used, 1)
                link(nc.vector.tensor_tensor(g4(kk[:]), sh[:, 4:8, :], bc(vecs[:, 2, :], P), ALU.mult))
                link(nc.vector.tensor_tensor(t1[:], kk[:], kk[:], ALU.mult))
                dve.nop().then_inc(kk_sq, 1)

            def channel_values(t, u, sample):
                link = chain(fch, 1 + FCH * t + 6)
                r, k = sh[:, 0:4, :], sh[:, 4:8, :]
                size = DS if sample else CHUNK
                dve.wait_ge(nrm_root, t + 1)
                link(nc.vector.tensor_scalar(t2[:], t2[:], 1e-12, None, ALU.max))
                link(nc.vector.reciprocal(t2[:], t2[:]))
                link(nc.vector.tensor_tensor(kk[:], kk[:], t2[:], ALU.mult))
                dve.wait_ge(sig, t + 1)
                link(nc.vector.tensor_tensor(g4(t1[:]), g4(rate[:]), bc(vecs[:, 3, :], P), ALU.mult))
                link(nc.vector.tensor_tensor(g4(t1[:]), g4(t1[:]), bc(vecs[:, 5, :], P), ALU.add))
                link(nc.vector.tensor_tensor(k, k, g4(t1[:]), ALU.mult))
                dve.wait_ge(decays, t + 1)
                link(nc.vector.tensor_tensor(t1[:], dec[:], notfirst[sample][:], ALU.mult))
                link(nc.vector.tensor_tensor(dec[:], dec[:], t1[:], ALU.subtract))
                link(nc.vector.tensor_tensor_scan(W[:, u, :], t1[:], dec[:], 0.0, ALU.mult, ALU.add))
                link(nc.vector.reciprocal(t2[:], W[:, u, :]))
                krv = kr[:, u, :, 0, :]
                nc.vector.tensor_tensor(kr[:, u, :, 1, :], r, g4(W[:, u, :]), ALU.mult)
                link(nc.vector.tensor_tensor(krv[:, :, 1:P], g4(kk[:])[:, :, 1:P], g4(W[:, u, :])[:, :, 0:P - 1],
                                             ALU.mult))
                for n in range(4):
                    ins = nc.vector.tensor_copy(krv[:, n, :].rearrange("p (b i) -> p b i", i=size)[:, :, 0],
                                                g4(kk[:])[:, n, :].rearrange("p (b i) -> p b i", i=size)[:, :, 0])
                link(ins)
                link(nc.vector.tensor_tensor(kk[:], kk[:], rate[:], ALU.mult))
                nc.vector.tensor_tensor(beta[:, u], g4(kk[:]), g4(t2[:]), ALU.mult)
                nc.vector.tensor_tensor(kap[:, u], k, g4(t2[:]), ALU.mult)
                link(nc.vector.tensor_tensor(g4(rk[:, u, :]), r, k, ALU.mult))
                link(nc.vector.tensor_tensor(g4(rk[:, u, :]), g4(rk[:, u, :]), bc(vecs[:, 4, :], P), ALU.mult))
                dve.nop().then_inc(ch_ready, 1)

            def tail(t, u):
                link = chain(tch, TCH * t)
                for g in range(2):
                    dve.wait_ge(o_copied[g], t + 1)
                bh = lambda s: s.rearrange("p (h o) -> p h o", o=1).broadcast_to([P, RH, 64])
                link(nc.vector.tensor_reduce(gn[:, 0, :], o[:], AX.X, ALU.add))
                link(nc.vector.tensor_scalar(gn[:, 1, :], gn[:, 0, :], 1.0 / 64, None, ALU.mult))
                link(nc.vector.tensor_tensor(o[:], o[:], bh(gn[:, 1, :]), ALU.subtract))
                link(nc.vector.tensor_tensor(o2[:], o[:], o[:], ALU.mult))
                link(nc.vector.tensor_reduce(gn[:, 2, :], o2[:], AX.X, ALU.add))
                link(nc.vector.tensor_scalar(gn[:, 2, :], gn[:, 2, :], 1.0 / 64, 64e-5, ALU.mult, ALU.add))
                dve.nop().then_inc(gn_var, 1)
                dve.wait_ge(gn_root, t + 1)
                link(nc.vector.reciprocal(gn[:, 4, :], gn[:, 3, :]))
                link(nc.vector.tensor_tensor(o[:], o[:], bh(gn[:, 4, :]), ALU.mult))
                link(nc.vector.tensor_tensor(flat(o[:]), flat(o[:]), lnw[:], ALU.mult))
                dve.wait_ge(gate, t + 1)
                nc.vector.tensor_tensor(flat(o[:]), flat(o[:]), lnb[:], ALU.add)
                link(nc.vector.tensor_tensor(o2[:], vt[:, u], bh(ps[:, 3, 0:RH]), ALU.mult))
                link(nc.vector.tensor_tensor(o[:], o[:], o2[:], ALU.add))
                nc.vector.tensor_tensor(flat(o[:]), flat(o[:]), ps[:, 7, :], ALU.mult).then_inc(o_fin, 1)

            idb = ident[:].rearrange("p (o t) -> p o t", o=1).broadcast_to([P, 4, P])

            def level(t, l):
                for g in range(2):
                    dve.wait_ge(nx[g], 5 * t + l)
                    nc.vector.tensor_tensor(Y[:, g], g4(ps[:, 4 * g, :]), idb, ALU.add).then_inc(y_ready[g], 1)

            def solve(t, u, sample):
                link = chain(vch, VCH * t)
                for g in range(2):
                    for h in range(4):
                        dve.wait_ge(gram[g], 4 * t + h + 1)
                        nc.vector.tensor_tensor(G[:, g, h, :, :].rearrange("p k t -> p (k t)"), ps[:, 4 * g + h, :],
                                                cmask[sample][:].rearrange("p k t -> p (k t)"),
                                                ALU.mult).then_inc(gram_used[g], 1)
                for g in range(2):
                    dve.wait_ge(lev[g], levels_before(t) + 1)
                    nc.vector.tensor_tensor(XT[:, g], N[:, g, 0, :, :], idb, ALU.add).then_inc(x0[g], 1)
                level(t, 1)
                if not first(t):
                    tail(t - 1, 1 - u)
                level(t, 2)
                if not sample:
                    shift(t + 1, after_is_sample(t))
                level(t, 3)
                if not sample:
                    level(t, 4)
                    lora_sums(t + 1)
                    level(t, 5)
                    channel_values(t + 1, 1 - u, after_is_sample(t))
                for g in range(2):
                    dve.wait_ge(qab[g], t + 1)
                    ins = nc.vector.tensor_tensor(QT[:, 2 * g:2 * g + 2, :],
                                                  ps[:, 4 * g + 2, 0:2 * P].rearrange("p (g t) -> p g t", g=2),
                                                  kr[:, u, 2 * g:2 * g + 2, 1, :], ALU.add)
                    if not sample:
                        Wc = g4(W[:, u, :])[:, 2 * g:2 * g + 2, :].rearrange("p g (c i) -> p g c i", i=CHUNK)
                        Wc = Wc[:, :, :, CHUNK - 1:CHUNK]
                        for cc in range(2):
                            nc.vector.tensor_tensor(
                                AB[:, g, 0, :, cc, :], ps[:, 4 * g + cc, 0:P].rearrange("p (g k) -> p g k", k=64),
                                i64[:].rearrange("p (o k) -> p o k", o=1).broadcast_to([P, 2, 64]), ALU.add)
                            ins = nc.vector.tensor_tensor(
                                AB[:, g, 1, :, cc, :], ps[:, 4 * g + cc, P:2 * P].rearrange("p (g k) -> p g k", k=64),
                                Wc[:, :, cc, :].broadcast_to([P, 2, 64]), ALU.mult)
                    link(ins)
                    dve.nop().then_inc(qab_used[g], 1)
                if not sample:
                    for cc in range(2):
                        for g in range(2):
                            dve.wait_ge(st_mm[g], 2 * t + cc + 1)
                            for n in range(2):
                                q = 2 * g + n
                                col = P * q + CHUNK * cc + CHUNK - 1
                                a_s = ps[:, 4 * g + 2, P * cc + 64 * n:P * cc + 64 * n + 64]
                                ins = nc.vector.scalar_tensor_tensor(
                                    St[:, 1 - cc, q, :], a_s, W[:, u, col:col + 1], AB[:, g, 1, n, cc, :],
                                    ALU.mult, ALU.add)
                            ins.then_inc(st_new[g], 1)
                else:
                    link = chain(vch, VCH * t + 2)
                    for q in range(4):
                        g, n = q // 2, q % 2
                        link(nc.vector.tensor_tensor(Qs, QT[:, q:q + 1, :].broadcast_to([P, DB, P]), colseq[:],
                                                     ALU.mult))
                        dve.nop().then_inc(exq, 1)
                        for hf in range(2):
                            h = 2 * q + hf
                            if h:
                                dve.wait_ge(ab_mm, h)
                            seq = oneseq[:].rearrange("p (b o) -> p b o", o=1).broadcast_to([P, DB, 64])
                            for z, src in enumerate((bt[:, u, h:h + 1, :], vt[:, u, h:h + 1, :], pg[:, h, 1:2, :])):
                                ins = nc.vector.tensor_tensor(ex[:, z, :, :], src.broadcast_to([P, DB, 64]), seq,
                                                              ALU.mult)
                            ins.then_inc(exv, 1)
                        dve.wait_ge(ab_mm, 2 * q + 2)
                        Wc = W[:, u, P * q:P * q + P].rearrange("p (b i) -> p b i", i=DS)[:, :, DS - 1:DS]
                        nc.vector.tensor_tensor(ABs[:, 0], ps[:, 4 * g, :].rearrange("p (b k) -> p b k", k=64),
                                                i64[:].rearrange("p (o k) -> p o k", o=1).broadcast_to([P, DB, 64]),
                                                ALU.add)
                        nc.vector.tensor_tensor(ABs[:, 1], ps[:, 4 * g + 1, :].rearrange("p (b k) -> p b k", k=64),
                                                Wc.broadcast_to([P, DB, 64]), ALU.mult).then_inc(ab_used, 1)
                        dve.wait_ge(st_mm[g], 2 * t + n + 1)
                        link(nc.vector.tensor_tensor(So[:, q, :, :], ps[:, 4 * g + 2, :].rearrange(
                            "p (b k) -> p b k", k=64), Wc.broadcast_to([P, DB, 64]), ALU.mult))
                        nc.vector.tensor_tensor(So[:, q, :, :], So[:, q, :, :], ABs[:, 1],
                                                ALU.add).then_inc(st_new[g], 1)

            def front(t, u, sample):
                shift(t, sample)
                lora_sums(t)
                channel_values(t, u, sample)

            dve.nop().then_inc(x_used, 1)
            dve.wait_ge(cin, CONSTS)
            nc.vector.tensor_scalar(vecs[:, 5, :], vecs[:, 3, :], -1.0, 1.0, ALU.mult, ALU.add).then_inc(fch, 1)
            dve.wait_ge(fch, 1)
            dve.wait_ge(masks, MASKS)
            each_tile(dve, front, solve, tail)

        @block.scalar
        def _(act):
            def lora_inputs(t, u):
                act.wait_ge(mixed, t + 1)
                nc.scalar.activation(low[0:64, u, 0, :], sh[0:64, 12, :], ACT.Tanh)
                nc.scalar.copy(low[64:P, u, 0, :], sh[64:P, 12, :])
                nc.scalar.activation(low[:, u, 1, :], sh[:, 13, :], ACT.Sigmoid).then_inc(lora_in, 1)

            def rates(t):
                act.wait_ge(lora_used, t + 1)
                nc.scalar.activation(rate[:], rate[:], ACT.Sigmoid)
                nc.scalar.activation(dec[:], dec[:], ACT.Sigmoid).then_inc(sig, 1)
                act.wait_ge(sig, t + 1)
                nc.scalar.activation(dec[:], dec[:], ACT.Exp, scale=-DECAY).then_inc(decays, 1)

            def token_values(t, u):
                for n, d in enumerate((bt[:, u], kt[:, u], kv[:, u, :, 0, :], vt[:, u])):
                    act.wait_ge(tr, 1 + 4 * t + n + 1)
                    nc.scalar.copy(d, ps[:, (7, 3)[n % 2], :].rearrange("p (h k) -> p h k", k=64)).then_inc(
                        tr_copied, 1)

            def norm_roots(t):
                act.wait_ge(nrm, t + 1)
                nc.scalar.activation(t2[:], ps[:, 3, :], ACT.Sqrt).then_inc(nrm_root, 1)

            def deviations(t):
                act.wait_ge(gn_var, t + 1)
                nc.scalar.activation(gn[:, 3, :], gn[:, 2, :], ACT.Sqrt).then_inc(gn_root, 1)

            def output(t):
                act.wait_ge(o_tr, t + 1)
                nc.scalar.copy(mixT[:, 0:4, ds(P * t, P)], g4(ps[:, 3, :])).then_inc(o_mix, 1)

            def level(t, l, sample):
                for g in range(2):
                    act.wait_ge(x_mm[g], 6 * t + l + 1)
                    if l > 0:
                        ins = nc.scalar.copy(XT[:, g].rearrange("p h t -> p (h t)"), ps[:, 4 * g + 1, :])
                    if l < last_level(sample):
                        bank = ps[:, 4 * g + 2, :] if l else ps[:, 4 * g + 1, :]
                        ins = nc.scalar.copy(X[:, g].rearrange("p h t -> p (h t)"), bank)
                    ins.then_inc(x_c[g], 1)

            def solve(t, u, sample):
                level(t, 0, sample)
                level(t, 1, sample)
                if not first(t):
                    deviations(t - 1)
                level(t, 2, sample)
                if not first(t):
                    output(t - 1)
                if not sample:
                    lora_inputs(t + 1, 1 - u)
                level(t, 3, sample)
                if not sample:
                    level(t, 4, sample)
                    rates(t + 1)
                    level(t, 5, sample)
                    norm_roots(t + 1)
                for g in range(2):
                    act.wait_ge(mv[g], t + 1)
                    nc.scalar.copy(kv[:, u, 4 * g:4 * g + 4, 1, :],
                                   ps[:, 4 * g + 2, 0:256].rearrange("p (h k) -> p h k", k=64)).then_inc(mv_c[g], 1)
                for g in range(2):
                    act.wait_ge(pgd[g], t + 1)
                    nc.scalar.mul(pg[:, 4 * g:4 * g + 4, :, :].rearrange("p h z k -> p (h z k)"), ps[:, 4 * g, :],
                                  -1.0).then_inc(pg_c[g], 1)
                if not sample:
                    token_values(t + 1, 1 - u)
                if sample:
                    for g in range(2):
                        act.wait_ge(o_mm[g], t + 1)
                    halves = o[:].rearrange("p (n z) k -> p z n k", z=2)
                    for z in range(2):
                        nc.scalar.copy(halves[:, z], ps[:, 3 + 4 * z, 0:256].rearrange(
                            "p (n k) -> p n k", k=64)).then_inc(o_copied[z], 1)
                else:
                    for g in range(2):
                        act.wait_ge(o_mm[g], t + 1)
                        nc.scalar.copy(o[:, 4 * g:4 * g + 4, :].rearrange("p (n z) k -> p z n k", z=2),
                                       ps[:, 4 * g:4 * g + 2, 0:P].rearrange("p z (n k) -> p z n k", k=64)).then_inc(
                                           o_copied[g], 1)

            def front(t, u, sample):
                lora_inputs(t, u)
                rates(t)
                norm_roots(t)
                token_values(t, u)

            act.wait_ge(masks, MASKS)
            def tail(t, u):
                deviations(t)
                output(t)

            each_tile(act, front, solve, tail)

        @block.tensor
        def _(pe):
            def lora(t, u):
                pe.wait_ge(lora_in, t + 1)
                if not isinstance(t, int) or t > 1:
                    pe.wait_ge(o_mix, t - 1)
                for q in range(4):
                    nc.tensor.matmul(ps[:, 3, P * q:P * q + P], w2[0:64, P * q:P * q + P], low[0:64, u, 0, :],
                                     start=True, stop=True)
                for q in range(4):
                    mm = nc.tensor.matmul(ps[:, 7, P * q:P * q + P], w2[64:P, P * q:P * q + P], low[64:P, u, 0, :],
                                          start=True, stop=True)
                mm.then_inc(lora_out, 1)

            def norms(t):
                pe.wait_ge(kk_sq, t + 1)
                nc.tensor.matmul(ps[:, 3, :], pair1[:], t1[:], start=True, stop=True).then_inc(nrm, 1)

            def turns(t, u):
                pe.wait_ge(ch_ready, t + 1)
                for n in range(4):
                    if n >= 2:
                        pe.wait_ge(tr_copied, 4 * t + n - 1)
                    for q in range(4):
                        src = (beta[:, u, q, :], kap[:, u, q, :], kr[:, u, q, 0, :], sh[:, 8 + q, :])[n]
                        mm = nc.tensor.transpose(ps[:, (7, 3)[n % 2], P * q:P * q + P], src, ident[:])
                    mm.then_inc(tr, 1)

            def bonus_and_gate(t, u):
                for q in range(4):
                    nc.tensor.matmul(ps[:, 3, 2 * q:2 * q + 2], rk[:, u, P * q:P * q + P], hone[:], start=True,
                                     stop=True)
                nc.tensor.matmul(ps[:, 7, :], low[:, u, 1, :], g2[:], start=True, stop=True).then_inc(gate, 1)

            def turn_output(t):
                pe.wait_ge(o_fin, t + 1)
                for q in range(4):
                    mm = nc.tensor.transpose(ps[:, 3, P * q:P * q + P],
                                             o[:, 2 * q:2 * q + 2, :].rearrange("p h k -> p (h k)"), ident[:])
                mm.then_inc(o_tr, 1)

            def level(t, l, sample):
                for g in range(2):
                    pe.wait_ge(lev[g], levels_before(t) + l + 1)
                    pe.wait_ge(x_c[g], 6 * t + l)
                    for h in range(4):
                        mm = nc.tensor.matmul(ps[:, 4 * g, P * h:P * h + P], N[:, g, l % 2, h, :], X[:, g, h, :],
                                              start=True, stop=True)
                    mm.then_inc(nx[g], 1)
                for g in range(2):
                    pe.wait_ge(y_ready[g], 5 * t + l)
                    for h in range(4):
                        mm = nc.tensor.matmul(ps[:, 4 * g + 1, P * h:P * h + P], Y[:, g, h, :], XT[:, g, h, :],
                                              start=True, stop=True)
                    if l < last_level(sample):
                        for h in range(4):
                            mm = nc.tensor.matmul(ps[:, 4 * g + 2, P * h:P * h + P], XT[:, g, h, :], Y[:, g, h, :],
                                                  start=True, stop=True)
                    mm.then_inc(x_mm[g], 1)

            def solve(t, u, sample):
                pe.wait_ge(tr_copied, 4 * t + 4)
                for g in range(2):
                    if not first(t):
                        pe.wait_ge(o_copied[g], t)
                        pe.wait_ge(st_new[g], 2 * t)
                    for h in range(4):
                        q, hf = 2 * g + h // 2, slice(64 * (h % 2), 64 * (h % 2) + 64)
                        both = kr[hf, u, q, :, :].rearrange("p z t -> p (z t)")
                        nc.tensor.matmul(ps[:, 4 * g + h, 0:256], beta[hf, u, q, :], both, start=True, stop=True)
                        nc.tensor.matmul(ps[:, 4 * g + h, 256:512], kap[hf, u, q, :], both, start=True,
                                         stop=True).then_inc(gram[g], 1)
                for g in range(2):
                    pe.wait_ge(x0[g], t + 1)
                    for h in range(4):
                        mm = nc.tensor.transpose(ps[:, 4 * g + 1, P * h:P * h + P], XT[:, g, h, :], ident[:])
                    mm.then_inc(x_mm[g], 1)
                level(t, 1, sample)
                if not first(t):
                    bonus_and_gate(t - 1, 1 - u)
                level(t, 2, sample)
                if not first(t):
                    turn_output(t - 1)
                level(t, 3, sample)
                if not sample:
                    lora(t + 1, 1 - u)
                    level(t, 4, sample)
                    level(t, 5, sample)
                    norms(t + 1)
                top = last_level(sample)
                for g in range(2):
                    for h in range(4):
                        mm = nc.tensor.matmul(ps[:, 4 * g + 2, 64 * h:64 * h + 64], G[:, g, h, 2, :],
                                              vt[:, u, 4 * g + h, :], start=True, stop=True)
                    mm.then_inc(mv[g], 1)
                for g in range(2):
                    pe.wait_ge(x_c[g], 6 * t + top + 1)
                    pe.wait_ge(mv_c[g], t + 1)
                    for h in range(4):
                        mm = nc.tensor.matmul(ps[:, 4 * g, P * h:P * h + P], XT[:, g, h, :],
                                              kv[:, u, 4 * g + h, :, :].rearrange("p z k -> p (z k)"),
                                              start=True, stop=True)
                    mm.then_inc(pgd[g], 1)
                for g in range(2):
                    pe.wait_ge(pg_c[g], t + 1)
                    for h in range(4):
                        hh, n, hf = 4 * g + h, h // 2, slice(64 * (h % 2), 64 * (h % 2) + 64)
                        mm = nc.tensor.matmul(ps[hf, 4 * g + 2, P * n:P * n + P], pg[:, hh, 0, :], G[:, g, h, 1, :],
                                              start=True, stop=True)
                    if not sample:
                        for h in range(4):
                            hh, n, hf = 4 * g + h, h // 2, slice(64 * (h % 2), 64 * (h % 2) + 64)
                            for cc in range(2):
                                rows = slice(64 * cc, 64 * cc + 64)
                                a0, b0 = slice(64 * n, 64 * n + 64), slice(P + 64 * n, P + 64 * n + 64)
                                nc.tensor.matmul(ps[hf, 4 * g + cc, a0], pg[rows, hh, 0, :], bt[rows, u, hh, :],
                                                 start=True, stop=True)
                                nc.tensor.matmul(ps[hf, 4 * g + cc, b0], kt[rows, u, hh, :], vt[rows, u, hh, :],
                                                 start=True, stop=False)
                                mm = nc.tensor.matmul(ps[hf, 4 * g + cc, b0], bt[rows, u, hh, :],
                                                      pg[rows, hh, 1, :], start=False, stop=True)
                    mm.then_inc(qab[g], 1)
                if not sample:
                    turns(t + 1, 1 - u)
                if not sample:
                    for g in range(2):
                        pe.wait_ge(qab_used[g], t + 1)
                        pe.nop().then_inc(state_seen, 1)
                        for h in range(4):
                            n, hf = h // 2, slice(64 * (h % 2), 64 * (h % 2) + 64)
                            mm = nc.tensor.matmul(ps[hf, 4 * g + 2, 64 * n:64 * n + 64], AB[hf, g, 0, n, 0, :],
                                                  St[hf, 0, 2 * g + n, :], start=True, stop=True)
                        mm.then_inc(st_mm[g], 1)
                    for g in range(2):
                        pe.wait_ge(st_new[g], 2 * t + 1)
                        pe.nop().then_inc(state_seen, 1)
                        for h in range(4):
                            hh, n, hf = 4 * g + h, h // 2, slice(64 * (h % 2), 64 * (h % 2) + 64)
                            col = slice(64 * n, 64 * n + 64)
                            oc = ps[:, 4 * g + h % 2, col]
                            nc.tensor.matmul(oc, G[:, g, h, 3, :], vt[:, u, hh, :], start=True, stop=False)
                            nc.tensor.matmul(oc, G[:, g, h, 1, :], pg[:, hh, 1, :], start=False, stop=True)
                            for cc in range(2):
                                rows = slice(64 * cc, 64 * cc + 64)
                                mm = nc.tensor.matmul(ps[rows, 4 * g + h % 2, col], QT[hf, 2 * g + n, rows],
                                                      St[hf, cc, 2 * g + n, :], start=False, stop=True,
                                                      skip_group_check=True)
                        mm.then_inc(o_mm[g], 1)
                        for h in range(4):
                            n, hf = h // 2, slice(64 * (h % 2), 64 * (h % 2) + 64)
                            mm = nc.tensor.matmul(ps[hf, 4 * g + 2, P + 64 * n:P + 64 * n + 64],
                                                  AB[hf, g, 0, n, 1, :], St[hf, 1, 2 * g + n, :], start=True,
                                                  stop=True)
                        mm.then_inc(st_mm[g], 1)
                else:
                    for q in range(4):
                        g = q // 2
                        pe.wait_ge(qab_used[g], t + 1)
                        pe.wait_ge(exq, q + 1)
                        for hf in range(2):
                            hh = 2 * q + hf
                            h = hh % 4
                            rows = slice(64 * hf, 64 * hf + 64)
                            oc = ps[:, 3 + 4 * hf, 64 * q:64 * q + 64]
                            nc.tensor.matmul(oc, G[:, g, h, 3, :], vt[:, u, hh, :], start=True, stop=False)
                            nc.tensor.matmul(oc, G[:, g, h, 1, :], pg[:, hh, 1, :], start=False, stop=False)
                            for b in range(DB):
                                mm = nc.tensor.matmul(oc, Qs[rows, b, :], Ss[rows, q, b, :], start=False,
                                                      stop=b == DB - 1)
                            if h == 3:
                                mm.then_inc(o_mm[g], 1)
                            pe.wait_ge(exv, hh + 1)
                            b0, b1 = ps[rows, 4 * g, :], ps[rows, 4 * g + 1, :]
                            nc.tensor.matmul(b0, pg[:, hh, 0, :], flat(ex[:, 0]), start=True, stop=True)
                            nc.tensor.matmul(b1, kt[:, u, hh, :], flat(ex[:, 1]), start=True, stop=False)
                            nc.tensor.matmul(b1, bt[:, u, hh, :], flat(ex[:, 2]), start=False,
                                             stop=True).then_inc(ab_mm, 1)
                        pe.wait_ge(ab_used, q + 1)
                        for b in range(DB):
                            for hf in range(2):
                                rows = slice(64 * hf, 64 * hf + 64)
                                mm = nc.tensor.matmul(ps[rows, 4 * g + 2, 64 * b:64 * b + 64], ABs[rows, 0, b, :],
                                                      Ss[rows, q, b, :], start=True, stop=True)
                        mm.then_inc(st_mm[g], 1)
                        pe.wait_ge(st_new[g], 2 * PT + q % 2 + 1)

            def front(t, u, sample):
                lora(t, u)
                norms(t)
                turns(t, u)

            def tail(t, u):
                for g in range(2):
                    pe.wait_ge(o_copied[g], t + 1)
                bonus_and_gate(t, u)
                turn_output(t)

            pe.nop().then_inc(tr, 1)
            pe.wait_ge(cin, CONSTS)
            pe.wait_ge(masks, MASKS)
            each_tile(pe, front, solve, tail)
    return sems


FFN = 512
EXPERTS = 32
GROUPS4 = 4
PER_GROUP = EXPERTS // GROUPS4
TOPK = 2
MAX_BLOCKS = 2 * T // P + EXPERTS
SLOTS = MAX_BLOCKS * P
LOGITS = GROUPS4 + EXPERTS
MH = 4
MSCALE = 1.0 / 16.0


def mix_and_norm(nc, mixT, h1_d, io):
    with ExitStack() as c:
        def sb(name, shape, dt=F32):
            return c.enter_context(nc.sbuf_tensor(name, shape, dt))

        def sem(name):
            return c.enter_context(nc.semaphore(name))

        w = sb("w_out", [P, KT, D])
        g, b = sb("ln1_g", [P, D]), sb("ln1_b", [P, D])
        ms = sb("mix_tile", [P, 3, KT, P])
        x = sb("x_tile", [P, 3, D])
        r = sb("residual", [P, 3, D])
        st = sb("ln_stats", [P, 3, 16])
        bn = sb("bn_stats", [P, 2, 6])
        ps = c.enter_context(nc.psum_tensor("ps_mix", [P, 3, D], F32))
        cin, w_got = sem("ln1_in"), sem("w_out_in")
        x_got = [sem(f"x_tile_in_{u}") for u in range(3)]
        stored = [sem(f"h1_stored_{u}") for u in range(3)]
        staged, mm_done, ch, var, root = sem("mix_staged"), sem("mix_product"), sem("dve_chain3"), sem("ln1_var"), \
            sem("ln1_sqrt")
        normed, scaled, h_ready = sem("ln1_normed"), sem("ln1_scaled"), sem("h1_ready")
        aggr_begun = sem("ln1_aggregation_begun")
        block = c.enter_context(nc.Block())

        @block.sync
        def _(sp):
            for u in range(3):
                sp.nop().then_inc(stored[u], 16)
            sp.dma_start(w[:], io["w_out"]).then_inc(w_got, 16)
            sp.dma_start(g[:], io["ln1_g"].broadcast_to([P, D])).then_inc(cin, 16)
            sp.dma_start(b[:], io["ln1_b"].broadcast_to([P, D])).then_inc(cin, 16)
            with sp.Fori(0, 3) as i:
                for u in range(3):
                    sp.wait_ge(normed, 1 + 3 * i)
                    sp.dma_start(x[:, u, :], io["x"][ds(3 * P * i + P * u, P), :]).then_inc(x_got[u], 16)
                for u in range(3):
                    sp.wait_ge(h_ready, 3 * i + u + 1)
                    sp.dma_start(h1_d[ds(3 * P * i + P * u, P), :], r[:, u, :]).then_inc(stored[u], 16)
            for u in range(3):
                sp.wait_ge(stored[u], 64)

        @block.gpsimd
        def _(pool):
            pool.wait_ge(cin, 32)
            with pool.Fori(0, 3) as i:
                for u in range(3):
                    pool.wait_ge(mm_done, 1 + 3 * i)
                    nc.gpsimd.tensor_copy(ms[:, u, :, :], mixT[:, :, ds(3 * P * i + P * u, P)]).then_inc(staged, 1)
                for u in range(3):
                    pool.wait_ge(normed, 1 + 3 * i + u + 1)
                    nc.gpsimd.tensor_tensor(r[:, u, :], r[:, u, :], g[:], ALU.mult).then_inc(scaled, 1)
                    pool.wait_ge(scaled, 3 * i + u + 1)
                    nc.gpsimd.tensor_tensor(r[:, u, :], r[:, u, :], b[:], ALU.add).then_inc(h_ready, 1)

        @block.tensor
        def _(pe):
            pe.nop().then_inc(mm_done, 1)
            pe.wait_ge(w_got, 16)
            with pe.Fori(0, 3) as i:
                for u in range(3):
                    pe.wait_ge(staged, 3 * i + u + 1)
                    pe.wait_ge(normed, 1 + 3 * i)
                    for n in range(2):
                        for k in range(KT):
                            mm = nc.tensor.matmul(ps[:, u, HALF * n:HALF * n + HALF], ms[:, u, k, :],
                                                  w[:, k, HALF * n:HALF * n + HALF], start=k == 0, stop=k == KT - 1)
                    mm.then_inc(mm_done, 1)

        @block.scalar
        def _(act):
            with act.Fori(0, 3) as i:
                for u in range(3):
                    act.wait_ge(var, 3 * i + u + 1)
                    nc.scalar.activation(st[:, u, 3:4], st[:, u, 2:3], ACT.Sqrt).then_inc(root, 1)

        @block.vector
        def _(dve):
            dve.nop().then_inc(normed, 1)
            with dve.Fori(0, 3) as i:
                at = [0]

                def link(ins):
                    at[0] += 1
                    ins.then_inc(ch, 1)
                    dve.wait_ge(ch, 15 * i + at[0])

                for u in range(3):
                    dve.wait_ge(x_got[u], 16 * i + 16)
                    dve.wait_ge(mm_done, 1 + 3 * i + u + 1)
                    dve.wait_ge(stored[u], 16 * i + 16)
                    link(nc.vector.scalar_tensor_tensor(r[:, u, :], x[:, u, :], ALPHA, ps[:, u, :], ALU.mult, ALU.add))
                    for n in range(2):
                        ins = nc.vector.bn_stats(bn[:, n, :], r[:, u, HALF * n:HALF * n + HALF])
                    link(ins)
                    dve.nop().then_inc(aggr_begun, 1)
                    link(nc.vector.bn_aggr(st[:, u, 0:2], bn[:].rearrange("p n s -> p (n s)")))
                    link(nc.vector.tensor_scalar(st[:, u, 2:3], st[:, u, 1:2], LN_EPS, None, ALU.add))
                    dve.nop().then_inc(var, 1)
                    dve.wait_ge(root, 3 * i + u + 1)
                    link(nc.vector.reciprocal(st[:, u, 4:5], st[:, u, 3:4]))
                    nc.vector.tensor_scalar(r[:, u, :], r[:, u, :], st[:, u, 0:1], st[:, u, 4:5], ALU.subtract,
                                            ALU.mult).then_inc(normed, 1)


def memory_and_router(nc, ident, L, h1_d, h2_d, io):
    with ExitStack() as c:
        def sb(name, shape, dt=F32):
            return c.enter_context(nc.sbuf_tensor(name, shape, dt))

        def sem(name):
            return c.enter_context(nc.semaphore(name))

        wq, wo = sb("mem_wq", [P, KT, D]), sb("mem_wo", [P, KT, D])
        mkT, mv = sb("mem_kT", [P, KT, N_MEM]), sb("mem_v", [P, 2, D])
        g, b = sb("ln2_g", [P, D]), sb("ln2_b", [P, D])
        wr = sb("w_router", [P, KT, LOGITS])
        h1 = sb("h1", [P, D])
        hT = sb("h_T", [P, KT, P])
        q = sb("mem_q", [P, D])
        qT = sb("mem_qT", [P, KT, P + DS])
        S = sb("mem_probs", [P, 2 * D])
        PT_ = sb("mem_probs_T", [P, 16, P])
        oT = sb("mem_oT", [P, KT, P])
        r = sb("h2", [P, D])
        ck, cv = sb("cache_mem_kT", [P, 2, KT, N_MEM]), sb("cache_mem_v", [P, 2, 2, D])
        st = sb("mem_stats", [P, 4, 8])
        bn = sb("bn_stats2", [P, 2, 6])
        zero = sb("zero_row", [1, D])
        pT = c.enter_context(nc.psum_tensor("pT", [P, D], F32))
        pM = c.enter_context(nc.psum_tensor("pM", [P, D], F32))
        pS = c.enter_context(nc.psum_tensor("pS", [P, 2 * D], F32))

        kv_done, kv_copied, kv_out = sem("mem_product"), sem("mem_copied"), sem("mem_stored")
        kv_in, w_in_ = sem("mem_weights_in"), sem("attention_weights_in")
        with nc.Block() as block:
            @block.sync
            def _(sp):
                for k in range(4):
                    sp.dma_start(S[:, 512 * k:512 * k + 512].rearrange("p (a t) -> p a t", a=2),
                                 io["memT"][:, 2 * k:2 * k + 2, :]).then_inc(kv_in, 16)
                sp.dma_start(wq[:], io["mem_wk"]).then_inc(kv_in, 16)
                sp.dma_start(wo[:], io["mem_wv"]).then_inc(kv_in, 16)
                sp.dma_start(g[:], io["ln2_g"].broadcast_to([P, D])).then_inc(w_in_, 16)
                sp.dma_start(b[:], io["ln2_b"].broadcast_to([P, D])).then_inc(w_in_, 16)
                sp.dma_start(wr[:, :, 0:GROUPS4], io["w_group"]).then_inc(w_in_, 16)
                sp.dma_start(wr[:, :, GROUPS4:LOGITS], io["w_expert"]).then_inc(w_in_, 16)
                sp.wait_ge(kv_copied, 4)
                sp.dma_start(io["out_mem_k"], cv[:, 0, :, :]).then_inc(kv_out, 16)
                sp.wait_ge(kv_copied, 8)
                sp.dma_start(io["out_mem_v"], mv[:]).then_inc(kv_out, 16)
                sp.wait_ge(kv_done, 8)
                sp.dma_start(wq[:], io["mem_wq"]).then_inc(w_in_, 16)
                sp.dma_start(wo[:], io["mem_wo"]).then_inc(w_in_, 16)
                sp.wait_ge(kv_out, 32)
                sp.wait_ge(w_in_, 96)

            @block.tensor
            def _(pe):
                pe.wait_ge(kv_in, 96)
                mT = S[:].rearrange("p (k t) -> p k t", k=KT)
                for n in range(8):
                    wgt, m, h = (wq, wo)[n // 4], n // 2 % 2, n % 2
                    if n >= 2:
                        pe.wait_ge(kv_copied, n - 1)
                    for k in range(KT):
                        mm = nc.tensor.matmul(pM[:, HALF * (n % 2):HALF * (n % 2) + HALF], mT[:, k, P * m:P * m + P],
                                              wgt[:, k, HALF * h:HALF * h + HALF], start=k == 0, stop=k == KT - 1)
                    mm.then_inc(kv_done, 1)
                pe.wait_ge(kv_copied, 4)
                for n in range(4):
                    for j in range(4):
                        kt, m = (4 * n + j) // 2, j % 2
                        mm = nc.tensor.transpose(pS[:, HALF * n + P * j:HALF * n + P * j + P],
                                                 cv[:, 0, m, P * kt:P * kt + P], ident[:])
                    mm.then_inc(kv_done, 1)

            @block.scalar
            def _(act):
                for n in range(8):
                    m, h = n // 2 % 2, n % 2
                    act.wait_ge(kv_done, n + 1)
                    dst = (cv[:, 0, m, HALF * h:HALF * h + HALF], mv[:, m, HALF * h:HALF * h + HALF])[n // 4]
                    nc.scalar.copy(dst, pM[:, HALF * (n % 2):HALF * (n % 2) + HALF]).then_inc(kv_copied, 1)
                for n in range(4):
                    act.wait_ge(kv_done, 9 + n)
                    nc.scalar.copy(mkT[:, 2 * n:2 * n + 2, :].rearrange("p k t -> p (k t)"),
                                   pS[:, HALF * n:HALF * n + HALF]).then_inc(kv_copied, 1)
                act.wait_ge(kv_copied, 12)

        h_in, h_turned, hT_c = sem("h1_in"), sem("h_turned"), sem("h_T_copied")
        q_mm, q_c, q_turned, qT_c = sem("q_product"), sem("q_copied"), sem("q_turned"), sem("qT_copied")
        s_mm, s_max, s_exp, s_norm = sem("mem_scores"), sem("mem_max"), sem("mem_exp"), sem("mem_normed")
        p_turned, p_c, o_mm, o_c = sem("probs_turned"), sem("probs_T_copied"), sem("mem_o"), sem("mem_o_copied")
        y_mm, ch, var, root, h_out = sem("wo_product"), sem("dve_chain4"), sem("ln2_var"), sem("ln2_sqrt"), sem("h2_out")
        r_ready, lg_mm, lg_c, pad = sem("h2_ready"), sem("logits_ready"), sem("logits_copied"), sem("pads_zero")
        scaled, normed = sem("ln2_scaled"), sem("ln2_normed")
        aggr_begun = sem("ln2_aggregation_begun")
        k_in = [sem("cache_k_in_0"), sem("cache_k_in_1")]
        v_in = [sem("cache_v_in_0"), sem("cache_v_in_1")]
        block = c.enter_context(nc.Block())
        VCH = 11

        @block.sync
        def _(sp):
            sp.nop().then_inc(h_out, 16)
            for n in range(2):
                sp.dma_start(ck[:, n, :, :], io["cache_mem_kT"][n]).then_inc(k_in[n], 16)
                sp.dma_start(cv[:, n, :, :], io["cache_mem_v"][n]).then_inc(v_in[n], 16)

            def load(t):
                sp.wait_ge(r_ready, 1 + t)
                sp.dma_start(h1[:], h1_d[ds(P * t, P), :]).then_inc(h_in, 16)

            def store(t):
                sp.wait_ge(r_ready, 1 + t + 1)
                sp.dma_start(h2_d[ds(P * t, P), :], r[:]).then_inc(h_out, 16)

            with sp.Fori(0, PT) as t:
                load(t)
                store(t)
            load(PT)
            for s in range(2, DB):
                sp.wait_ge(s_mm, PT + s - 1)
                sp.dma_start(ck[:, s % 2, :, :], io["cache_mem_kT"][s]).then_inc(k_in[s % 2], 16)
            for s in range(2, DB):
                sp.wait_ge(o_mm, PT + s - 1)
                sp.dma_start(cv[:, s % 2, :, :], io["cache_mem_v"][s]).then_inc(v_in[s % 2], 16)
            store(PT)
            sp.wait_ge(pad, 2)
            sp.dma_start(h2_d[T:T + 1, :], zero[:]).then_inc(h_out, 16)
            sp.wait_ge(h_out, 16 * (NT + 2))

        @block.gpsimd
        def _(pool):
            pool.nop().then_inc(r_ready, 1)
            nc.gpsimd.memset(qT[:, :, P:P + DS], 0.0).then_inc(pad, 1)
            nc.gpsimd.memset(zero[:], 0.0).then_inc(pad, 1)
            with pool.Fori(0, NT) as t:
                pool.wait_ge(normed, t + 1)
                nc.gpsimd.tensor_tensor(r[:], r[:], g[:], ALU.mult).then_inc(scaled, 1)
                pool.wait_ge(scaled, t + 1)
                nc.gpsimd.tensor_tensor(r[:], r[:], b[:], ALU.add).then_inc(r_ready, 1)

        @block.tensor
        def _(pe):
            def tile(t, sample):
                pe.wait_ge(h_in, 16 * t + 16)
                for k in range(KT):
                    mm = nc.tensor.transpose(pT[:, P * k:P * k + P], h1[:, P * k:P * k + P], ident[:])
                mm.then_inc(h_turned, 1)
                pe.wait_ge(hT_c, 2 * t + 1)
                for n in range(2):
                    for k in range(KT):
                        mm = nc.tensor.matmul(pM[:, HALF * n:HALF * n + HALF], hT[:, k, :],
                                              wq[:, k, HALF * n:HALF * n + HALF], start=k == 0, stop=k == KT - 1)
                mm.then_inc(q_mm, 1)
                pe.wait_ge(q_c, t + 1)
                for k in range(KT):
                    mm = nc.tensor.transpose(pT[:, P * k:P * k + P], q[:, P * k:P * k + P], ident[:])
                mm.then_inc(q_turned, 1)
                pe.wait_ge(qT_c, t + 1)
                if not sample:
                    for h in range(MH):
                        for k in range(2):
                            mm = nc.tensor.matmul(pS[:, N_MEM * h:N_MEM * h + N_MEM], qT[:, 2 * h + k, 0:P],
                                                  mkT[:, 2 * h + k, :], start=k == 0, stop=k == 1)
                    mm.then_inc(s_mm, 1)
                    pe.wait_ge(s_norm, t + 1)
                    for n in range(2):
                        for j in range(4):
                            mm = nc.tensor.transpose(pT[:, HALF * n + P * j:HALF * n + P * j + P],
                                                     S[:, HALF * n + P * j:HALF * n + P * j + P], ident[:])
                    mm.then_inc(p_turned, 1)
                    pe.wait_ge(p_c, t + 1)
                    for cb in range(KT):
                        for k in range(2):
                            mm = nc.tensor.matmul(pM[:, P * cb:P * cb + P], mv[:, k, P * cb:P * cb + P],
                                                  PT_[:, 2 * (cb // 2) + k, :], start=k == 0, stop=k == 1)
                    mm.then_inc(o_mm, 1)
                else:
                    pe.wait_ge(pad, 1)
                    for s in range(DB):
                        pe.wait_ge(k_in[s % 2], 16 * (s // 2) + 16)
                        for h in range(MH):
                            for k in range(2):
                                mm = nc.tensor.matmul(pS[32 * h:32 * h + 32, N_MEM * s:N_MEM * s + N_MEM],
                                                      qT[:, 2 * h + k, DS * s:DS * s + 32],
                                                      ck[:, s % 2, 2 * h + k, :], start=k == 0, stop=k == 1)
                        mm.then_inc(s_mm, 1)
                    pe.wait_ge(s_norm, t + 1)
                    for n in range(2):
                        if n:
                            pe.wait_ge(p_c, t + 1)
                        for j in range(8):
                            mm = nc.tensor.transpose(pT[:, P * j:P * j + P],
                                                     S[:, P * (8 * n + j):P * (8 * n + j) + P], ident[:])
                        mm.then_inc(p_turned, 1)
                    pe.wait_ge(p_c, t + 2)
                    for s in range(DB):
                        pe.wait_ge(v_in[s % 2], 16 * (s // 2) + 16)
                        for cb in range(KT):
                            for k in range(2):
                                mm = nc.tensor.matmul(pM[:, P * cb + DS * s:P * cb + DS * s + DS],
                                                      cv[:, s % 2, k, P * cb:P * cb + P],
                                                      PT_[:, 2 * s + k, 32 * (cb // 2):32 * (cb // 2) + DS],
                                                      start=k == 0, stop=k == 1)
                        mm.then_inc(o_mm, 1)
                pe.wait_ge(o_c, t + 1)
                for n in range(2):
                    for k in range(KT):
                        mm = nc.tensor.matmul(pS[:, HALF * n:HALF * n + HALF], oT[:, k, :],
                                              wo[:, k, HALF * n:HALF * n + HALF], start=k == 0, stop=k == KT - 1)
                mm.then_inc(y_mm, 1)
                pe.wait_ge(r_ready, 1 + t + 1)
                for k in range(KT):
                    mm = nc.tensor.transpose(pT[:, P * k:P * k + P], r[:, P * k:P * k + P], ident[:])
                mm.then_inc(h_turned, 1)
                pe.wait_ge(hT_c, 2 * t + 2)
                for k in range(KT):
                    mm = nc.tensor.matmul(pM[:, 0:LOGITS], hT[:, k, :], wr[:, k, :], start=k == 0, stop=k == KT - 1)
                mm.then_inc(lg_mm, 1)
                pe.wait_ge(lg_c, t + 1)

            with pe.Fori(0, PT) as t:
                tile(t, 0)
            tile(PT, 1)

        @block.scalar
        def _(act):
            def copy_T(dst, src):
                for n in range(2):
                    ins = nc.scalar.copy(dst[:, 4 * n:4 * n + 4, 0:P],
                                         src[:, HALF * n:HALF * n + HALF].rearrange("p (k t) -> p k t", k=4))
                return ins

            def tile(t, sample):
                act.wait_ge(h_turned, 2 * t + 1)
                copy_T(hT, pT).then_inc(hT_c, 1)
                act.wait_ge(q_turned, t + 1)
                copy_T(qT, pT).then_inc(qT_c, 1)
                act.wait_ge(s_max, t + 1)
                parts = DB if sample else MH
                for h in range(parts):
                    ins = nc.scalar.activation(S[:, N_MEM * h:N_MEM * h + N_MEM], pS[:, N_MEM * h:N_MEM * h + N_MEM],
                                               ACT.Exp, bias=st[:, 1, h:h + 1], scale=MSCALE,
                                               accum_out=st[:, 2, h:h + 1])
                ins.then_inc(s_exp, 1)
                for n in range(2 if sample else 1):
                    act.wait_ge(p_turned, t + n + 1)
                    copy_T(PT_[:, 8 * n:8 * n + 8, :], pT).then_inc(p_c, 1)
                act.wait_ge(var, t + 1)
                nc.scalar.activation(st[:, 3, 3:4], st[:, 3, 2:3], ACT.Sqrt).then_inc(root, 1)
                act.wait_ge(h_turned, 2 * t + 2)
                copy_T(hT, pT).then_inc(hT_c, 1)

            with act.Fori(0, PT) as t:
                tile(t, 0)
            tile(PT, 1)

        @block.vector
        def _(dve):
            def tile(t, sample):
                at = [0]

                def link(ins):
                    at[0] += 1
                    ins.then_inc(ch, 1)
                    dve.wait_ge(ch, VCH * t + at[0])

                dve.wait_ge(q_mm, t + 1)
                nc.vector.tensor_copy(q[:], pM[:]).then_inc(q_c, 1)
                parts = DB if sample else MH
                w = N_MEM * parts
                dve.wait_ge(s_mm, t + parts if sample else t + 1)
                link(nc.vector.tensor_reduce(st[:, 0, 0:parts], pS[:, 0:w].rearrange("p (h m) -> p h m", m=N_MEM),
                                             AX.X, ALU.max))
                link(nc.vector.tensor_scalar(st[:, 1, 0:parts], st[:, 0, 0:parts], -MSCALE, None, ALU.mult))
                dve.nop().then_inc(s_max, 1)
                dve.wait_ge(s_exp, t + 1)
                link(nc.vector.reciprocal(st[:, 0, 0:parts], st[:, 2, 0:parts]))
                for h in range(parts):
                    ins = nc.vector.tensor_scalar(S[:, N_MEM * h:N_MEM * h + N_MEM], S[:, N_MEM * h:N_MEM * h + N_MEM],
                                                  st[:, 0, h:h + 1], None, ALU.mult)
                ins.then_inc(s_norm, 1)
                dve.wait_ge(o_mm, t + DB if sample else t + 1)
                nc.vector.tensor_copy(oT[:].rearrange("p k t -> p (k t)"), pM[:]).then_inc(o_c, 1)
                dve.wait_ge(y_mm, t + 1)
                dve.wait_ge(h_out, 16 * t + 16)
                link(nc.vector.scalar_tensor_tensor(r[:], h1[:], ALPHA, pS[:, 0:D], ALU.mult, ALU.add))
                for n in range(2):
                    ins = nc.vector.bn_stats(bn[:, n, :], r[:, HALF * n:HALF * n + HALF])
                link(ins)
                dve.nop().then_inc(aggr_begun, 1)
                link(nc.vector.bn_aggr(st[:, 3, 0:2], bn[:].rearrange("p n s -> p (n s)")))
                link(nc.vector.tensor_scalar(st[:, 3, 2:3], st[:, 3, 1:2], LN_EPS, None, ALU.add))
                dve.nop().then_inc(var, 1)
                dve.wait_ge(root, t + 1)
                link(nc.vector.reciprocal(st[:, 3, 4:5], st[:, 3, 3:4]))
                nc.vector.tensor_scalar(r[:], r[:], st[:, 3, 0:1], st[:, 3, 4:5], ALU.subtract,
                                        ALU.mult).then_inc(normed, 1)
                dve.wait_ge(lg_mm, t + 1)
                while at[0] < VCH - 1:
                    link(dve.nop())
                dst = L[:, ds(t, 1), :].rearrange("p o e -> p (o e)") if not sample else L[:, PT, :]
                link(nc.vector.tensor_copy(dst, pM[:, 0:LOGITS]))
                dve.nop().then_inc(lg_c, 1)

            with dve.Fori(0, PT) as t:
                tile(t, 0)
            tile(PT, 1)


def route(nc, L, rt, pool_dmas, io):
    with ExitStack() as c:
        def sb(name, shape, dt=F32):
            return c.enter_context(nc.sbuf_tensor(name, shape, dt))

        def sem(name):
            return c.enter_context(nc.semaphore(name))

        bias = sb("router_bias", [P, LOGITS])
        gl, eg = sb("group_logits", [P, NT, 4]), sb("group_hot", [P, NT, 4])
        gt, io4 = sb("group_tmp", [P, NT, 4]), sb("iota_4", [P, 4])
        el, tmp, pos = sb("expert_logits", [P, NT, EXPERTS]), sb("expert_tmp", [P, NT, EXPERTS]), sb(
            "positions", [P, NT, EXPERTS])
        oh = sb("expert_hot", [P, 2, NT, EXPERTS])
        both = sb("both_hot", [P, NT, EXPERTS])
        io32, ioi = sb("iota_32", [P, EXPERTS]), sb("iota_int", [P, MAX_BLOCKS + 2], I32)
        s = sb("route_scalars", [P, 10, NT])
        m2 = sb("slots_float", [P, 2, NT])
        upper, ones = sb("strict_upper", [P, P]), sb("all_ones", [P, P])
        cnt, cnti = sb("expert_counts", [P, 6, EXPERTS]), sb("expert_counts_int", [P, EXPERTS], I32)
        cmp_ = sb("block_compare", [P, MAX_BLOCKS + 2, EXPERTS])
        iob, be = sb("iota_blocks", [P, MAX_BLOCKS + 2]), sb("block_expert_float", [P, MAX_BLOCKS + 2])
        tok = sb("token_numbers", [P, NT], I32)
        pair = sb("slot_values", [P, 2, NT, 3], I32)
        fill = sb("empty_rows", [P, MAX_BLOCKS + 2, 3], I32)
        pr = c.enter_context(nc.psum_tensor("ps_rank", [P, HALF], F32))
        pc = c.enter_context(nc.psum_tensor("ps_count", [P, HALF], F32))
        b_in, io_done, ch, ex_in, ex = sem("router_bias_in"), sem("iotas"), sem("dve_chain5"), sem("exp_args"), sem("exps")
        hots, ranks, out, filled = sem("choices_ready"), sem("ranks_ready"), sem("slots_ready"), sem("slots_cleared")
        scat = pool_dmas["slots_scattered"]
        fills = sem("fill_made")
        block = c.enter_context(nc.Block())
        W = MAX_BLOCKS + 2

        @block.sync
        def _(sp):
            sp.dma_start(bias[:, 0:4], io["b_group"].broadcast_to([P, 4])).then_inc(b_in, 16)
            sp.dma_start(bias[:, 4:LOGITS], io["b_expert"].broadcast_to([P, EXPERTS])).then_inc(b_in, 16)
            sp.wait_ge(fills, 3)
            sp.dma_start(io["slots"].rearrange("(b p) z -> p b z", p=P), fill[:]).then_inc(filled, 16)
            sp.wait_ge(filled, 16)

        @block.gpsimd
        def _(pool):
            nc.gpsimd.iota(ioi[:], pattern=[[1, W]], base=0, channel_multiplier=0).then_inc(io_done, 1)
            nc.gpsimd.iota(tok[:], pattern=[[P, NT]], base=0, channel_multiplier=1).then_inc(io_done, 1)
            nc.gpsimd.memset(upper[:], 1.0).then_inc(io_done, 1)
            nc.gpsimd.memset(ones[:], 1.0).then_inc(io_done, 1)
            pool.wait_ge(io_done, 4)
            nc.gpsimd.affine_select(out=upper[:], in_=upper[:], compare_op=ALU.is_ge, fill=0.0, base=-1,
                                    pattern=[[1, P]], channel_multiplier=-1).then_inc(io_done, 1)
            nc.gpsimd.memset(fill[:, :, 0:1], T).then_inc(fills, 1)
            nc.gpsimd.memset(fill[:, :, 1:2], 0).then_inc(fills, 1)
            nc.gpsimd.iota(fill[:, :, 2], pattern=[[P, W]], base=2 * T, channel_multiplier=1).then_inc(fills, 1)
            pool.wait_ge(filled, 16)
            pool.wait_ge(out, 1)
            for t in range(NT):
                for z in range(2):
                    nc.gpsimd.indirect_dma_start(
                        out=io["slots"], out_offset=bass.IndirectOffsetOnAxis(ap=rt["slot"][:, z, t:t + 1], axis=0),
                        in_=pair[:, z, t, :], in_offset=None).then_inc(scat, 16)
            pool.wait_ge(scat, 16 * 2 * NT)

        @block.tensor
        def _(pe):
            pe.wait_ge(io_done, 5)
            pe.wait_ge(hots, 1)
            flat = both[:].rearrange("p t e -> p (t e)")
            nc.tensor.matmul(pr[:, 0:NT * EXPERTS], upper[:], flat, start=True, stop=True)
            nc.tensor.matmul(pc[:, 0:NT * EXPERTS], ones[:], flat, start=True, stop=True).then_inc(ranks, 1)

        @block.scalar
        def _(act):
            act.wait_ge(ex_in, 1)
            nc.scalar.activation(gt[:], gt[:], ACT.Exp)
            nc.scalar.activation(s[:, 5, :], s[:, 5, :], ACT.Exp).then_inc(ex, 1)

        @block.vector
        def _(dve):
            n = [0]

            def link(ins):
                n[0] += 1
                ins.then_inc(ch, 1)
                dve.wait_ge(ch, n[0])

            V = nc.vector

            def across(vec, k):
                return vec.rearrange("p (t o) -> p t o", o=1).broadcast_to([P, NT, k])

            def over(row, k):
                return row.rearrange("p (o k) -> p o k", o=1).broadcast_to([P, NT, k])

            def first_of_max(x, hot, scratch, io_row, k, mx, idx):
                link(V.tensor_reduce(mx, x, AX.X, ALU.max))
                link(V.tensor_tensor(hot, x, across(mx, k), ALU.is_equal))
                link(V.tensor_scalar(hot, hot, -1.0, -1000.0, ALU.add, ALU.mult))
                link(V.tensor_tensor(scratch, hot, over(io_row, k), ALU.add))
                link(V.tensor_reduce(idx, scratch, AX.X, ALU.min))
                link(V.tensor_tensor(hot, over(io_row, k), across(idx, k), ALU.is_equal))

            dve.wait_ge(b_in, 32)
            dve.wait_ge(io_done, 4)
            link(V.tensor_copy(iob[:], ioi[:]))
            link(V.tensor_copy(io4[:], iob[:, 0:4]))
            link(V.tensor_copy(io32[:], iob[:, 0:EXPERTS]))
            link(V.tensor_tensor(gl[:], L[:, :, 0:4], over(bias[:, 0:4], 4), ALU.add))
            link(V.tensor_tensor(el[:], L[:, :, 4:LOGITS], over(bias[:, 4:LOGITS], EXPERTS), ALU.add))
            first_of_max(gl[:], eg[:], gt[:], io4[:], 4, s[:, 0, :], s[:, 1, :])
            link(V.tensor_tensor(gt[:], gl[:], across(s[:, 0, :], 4), ALU.subtract))
            hot8 = eg[:].rearrange("p t (g o) -> p (t g) o", o=1).broadcast_to([P, NT * 4, PER_GROUP])
            e8 = lambda a: a.rearrange("p t (g e) -> p (t g) e", g=4)
            link(V.tensor_tensor(e8(tmp[:]), e8(el[:]), hot8, ALU.mult))
            link(V.tensor_scalar(eg[:], eg[:], -1.0, -NEG, ALU.add, ALU.mult))
            link(V.tensor_tensor(e8(el[:]), e8(tmp[:]), hot8, ALU.add))
            first_of_max(el[:], oh[:, 0], tmp[:], io32[:], EXPERTS, s[:, 2, :], s[:, 3, :])
            link(V.tensor_scalar(tmp[:], oh[:, 0], 3 * NEG, None, ALU.mult))
            link(V.tensor_tensor(el[:], el[:], tmp[:], ALU.add))
            first_of_max(el[:], oh[:, 1], tmp[:], io32[:], EXPERTS, s[:, 4, :], s[:, 3, :])
            link(V.tensor_tensor(s[:, 5, :], s[:, 4, :], s[:, 2, :], ALU.subtract))
            dve.nop().then_inc(ex_in, 1)
            link(V.tensor_tensor(both[:], oh[:, 0], oh[:, 1], ALU.add))
            dve.nop().then_inc(hots, 1)
            dve.wait_ge(ex, 1)
            link(V.tensor_reduce(s[:, 6, :], gt[:], AX.X, ALU.add))
            link(V.tensor_scalar(s[:, 7, :], s[:, 5, :], 1.0, None, ALU.add))
            link(V.tensor_tensor(s[:, 6, :], s[:, 6, :], s[:, 7, :], ALU.mult))
            link(V.reciprocal(s[:, 8, :], s[:, 6, :]))
            link(V.tensor_tensor(s[:, 9, :], s[:, 8, :], s[:, 5, :], ALU.mult))
            dve.wait_ge(ranks, 1)
            link(V.tensor_copy(pos[:].rearrange("p t e -> p (t e)"), pr[:, 0:NT * EXPERTS]))
            link(V.tensor_copy(cnt[:, 0, :], pc[:, 0:EXPERTS]))
            for t in range(1, NT):
                link(V.tensor_tensor(pos[:, t, :], pos[:, t, :], cnt[:, 0, :], ALU.add))
                link(V.tensor_tensor(cnt[:, 0, :], cnt[:, 0, :], pc[:, EXPERTS * t:EXPERTS * t + EXPERTS], ALU.add))
            link(V.tensor_scalar(cnt[:, 1, :], cnt[:, 0, :], float(P - 1), None, ALU.add))
            link(V.tensor_copy(cnti[:], cnt[:, 1, :]))
            link(V.tensor_scalar(cnti[:], cnti[:], 7, None, ALU.arith_shift_right))
            link(V.tensor_copy(cnt[:, 1, :], cnti[:]))
            link(V.memset(cnt[:, 2, :], 1.0))
            link(V.tensor_tensor_scan(cnt[:, 3, :], cnt[:, 2, :], cnt[:, 1, :], 0.0, ALU.mult, ALU.add))
            link(V.tensor_tensor(cnt[:, 4, :], cnt[:, 3, :], cnt[:, 1, :], ALU.subtract))
            link(V.tensor_scalar(cnt[:, 4, :], cnt[:, 4, :], float(P), None, ALU.mult))
            link(V.tensor_tensor(pos[:], pos[:], over(cnt[:, 4, :], EXPERTS), ALU.add))
            for z in range(2):
                link(V.tensor_tensor(tmp[:], pos[:], oh[:, z], ALU.mult))
                link(V.tensor_reduce(m2[:, z, :], tmp[:], AX.X, ALU.add))
                link(V.tensor_copy(pair[:, z, :, 0], tok[:]))
                link(V.tensor_copy(pair[:, z, :, 1].bitcast(F32), s[:, 8 + z, :]))
                link(V.tensor_scalar(pair[:, z, :, 2], tok[:], 2, z, ALU.mult, ALU.add))
            link(V.tensor_copy(rt["slot"][:], m2[:]))
            dve.nop().then_inc(out, 1)
            wide = lambda a: a.rearrange("p (b o) -> p b o", o=1).broadcast_to([P, W, EXPERTS])
            link(V.tensor_tensor(cmp_[:], wide(iob[:]),
                                 cnt[:, 3, :].rearrange("p (o e) -> p o e", o=1).broadcast_to([P, W, EXPERTS]),
                                 ALU.is_ge))
            link(V.tensor_reduce(be[:], cmp_[:], AX.X, ALU.add))
            link(V.tensor_scalar(be[:], be[:], float(EXPERTS - 1), None, ALU.min))
            link(V.tensor_copy(rt["block_expert"][:], be[:]))
            link(V.tensor_scalar(cnt[:, 5, 0:1], cnt[:, 3, EXPERTS - 1:EXPERTS], 1.0, None, ALU.add))
            link(V.tensor_copy(rt["pairs"][:], cnt[:, 5, 0:1]))
            link(V.tensor_scalar(rt["pairs"][:], rt["pairs"][:], 1, None, ALU.arith_shift_right))


def experts(nc, ident, rt, pool_dmas, h2_d, y_d, io):
    with ExitStack() as c:
        def sb(name, shape, dt=F32):
            return c.enter_context(nc.sbuf_tensor(name, shape, dt))

        def sem(name):
            return c.enter_context(nc.semaphore(name))

        w1, w3, w2 = sb("w1", [P, 2, KT, FFN]), sb("w3", [P, 2, KT, FFN]), sb("w2", [P, 2, FFN // P, D])
        tk, gt = sb("slots_to_gather", [P, 2, 3], I32), sb("slots_to_scatter", [P, 2, 3], I32)
        xg = sb("gathered", [P, 2, D])
        xT = sb("gathered_T", [P, 2, KT, P])
        sg, hb, hT = sb("sigmoid", [P, 2, FFN]), sb("hidden", [P, 2, FFN]), sb("hidden_T", [P, 2, FFN // P, P])
        y = sb("expert_out", [P, 2, D])
        pT = c.enter_context(nc.psum_tensor("pT2", [P, 2, HALF], F32))
        pH = c.enter_context(nc.psum_tensor("pH", [P, 2, 2, HALF], F32))
        pY = c.enter_context(nc.psum_tensor("pY", [P, 2, HALF], F32))
        w13_in = [sem(f"w1_w3_in_{u}") for u in range(2)]
        w2_in = [sem(f"w2_in_{u}") for u in range(2)]
        tk_in = [pool_dmas[f"tokens_in_{u}"] for u in range(2)]
        gt_in = [sem(f"gates_in_{u}") for u in range(2)]
        xg_in = [pool_dmas[f"rows_in_{u}"] for u in range(2)]
        y_out = [pool_dmas[f"outputs_scattered_{u}"] for u in range(2)]
        turned, xT_c, h_mm, sig, hid, h_turned, hT_c, y_mm, y_c, ch = (sem(n) for n in (
            "rows_turned", "rows_T_copied", "hidden_product", "sigmoid_ready", "hidden_ready", "hidden_turned",
            "hidden_T_copied", "out_product", "out_gated", "hidden_chain"))
        gather_begun, y_free = sem("gather_begun_moe"), sem("outputs_stored")
        block = c.enter_context(nc.Block())

        def passes(eng):
            return eng.value_load(rt["pairs"][0:1, 0:1], min_val=1, max_val=(MAX_BLOCKS + 1) // 2)

        @block.sync
        def _(sp):
            with sp.Fori(0, passes(sp)) as i:
                for u in range(2):
                    e = sp.value_load(rt["block_expert"][0:1, ds(2 * i + u, 1)], min_val=0, max_val=EXPERTS - 1)
                    sp.wait_ge(h_mm, 2 * i + u + 1)
                    sp.dma_start(w1[:, u, :, :].rearrange("p k (o n) -> p o k n", o=1),
                                 io["moe_w1"][:, ds(e, 1), :, :]).then_inc(w13_in[u], 16)
                    sp.dma_start(w3[:, u, :, :].rearrange("p k (o n) -> p o k n", o=1),
                                 io["moe_w3"][:, ds(e, 1), :, :]).then_inc(w13_in[u], 16)
                    sp.wait_ge(y_mm, 2 * i + u + 1)
                    sp.dma_start(w2[:, u, :, :].rearrange("p k (o n) -> p o k n", o=1),
                                 io["moe_w2"][:, ds(e, 1), :, :]).then_inc(w2_in[u], 16)
                for u in range(2):
                    sp.wait_ge(y_free, 1 + 2 * i)
                    sp.dma_start(gt[:, u, :], io["slots"][ds(2 * P * i + P * u, P), :]).then_inc(gt_in[u], 16)

        @block.gpsimd
        def _(pool):
            def gather(i, u):
                pool.dma_start(tk[:, u, :], io["slots"][ds(2 * P * i + P * u, P), :]).then_inc(tk_in[u], 16)
                pool.wait_ge(tk_in[u], 16 * i + 16)
                pool.nop().then_inc(gather_begun, 1)
                nc.gpsimd.indirect_dma_start(
                    out=xg[:, u, :], out_offset=None, in_=h2_d,
                    in_offset=bass.IndirectOffsetOnAxis(ap=tk[:, u, 0:1], axis=0)).then_inc(xg_in[u], 16)

            pool.nop().then_inc(y_free, 1)
            gather(0, 0)
            gather(0, 1)
            n = passes(pool)
            with pool.Fori(0, n) as i:
                for u in range(2):
                    pool.wait_ge(turned, 1 + 4 * i + 2 * u + 2)
                    pool.nop().then_inc(gather_begun, 1)
                    gather(i + 1, u)
                for u in range(2):
                    pool.wait_ge(y_c, 1 + 2 * i + u + 1)
                    pool.nop().then_inc(gather_begun, 1)
                    nc.gpsimd.indirect_dma_start(
                        out=y_d, out_offset=bass.IndirectOffsetOnAxis(ap=gt[:, u, 2:3], axis=0),
                        in_=y[:, u, :], in_offset=None).then_inc(y_out[u], 16)
                for u in range(2):
                    pool.wait_ge(y_out[u], 16 * i + 16)
                    pool.nop().then_inc(y_free, 1)
            for u in range(2):
                pool.wait_ge(xg_in[u], 16 * n + 16)
                pool.nop().then_inc(gather_begun, 1)

        @block.tensor
        def _(pe):
            pe.nop().then_inc(h_mm, 2)
            pe.nop().then_inc(y_mm, 2)
            pe.nop().then_inc(turned, 1)
            with pe.Fori(0, passes(pe)) as i:
                def hidden(u):
                    pe.wait_ge(xg_in[u], 16 * i + 16)
                    for z in range(2):
                        pe.wait_ge(xT_c, 1 + 4 * i + 2 * u + z)
                        for k in range(4):
                            c0 = P * (4 * z + k)
                            mm = nc.tensor.transpose(pT[:, 0, P * k:P * k + P], xg[:, u, c0:c0 + P], ident[:])
                        mm.then_inc(turned, 1)
                    pe.wait_ge(xT_c, 1 + 4 * i + 2 * u + 2)
                    pe.wait_ge(w13_in[u], 32 * i + 32)
                    pe.wait_ge(hid, 1 + 2 * i)
                    for z, w in enumerate((w1, w3)):
                        for k in range(KT):
                            mm = nc.tensor.matmul(pH[:, u, z, :], xT[:, u, k, :], w[:, u, k, :], start=k == 0,
                                                  stop=k == KT - 1)
                    mm.then_inc(h_mm, 1)

                def output(u):
                    pe.wait_ge(hid, 1 + 2 * i + u + 1)
                    pe.wait_ge(hT_c, 1 + 2 * i + u)
                    for k in range(4):
                        mm = nc.tensor.transpose(pT[:, 1, P * k:P * k + P], hb[:, u, P * k:P * k + P], ident[:])
                    mm.then_inc(h_turned, 1)
                    pe.wait_ge(hT_c, 1 + 2 * i + u + 1)
                    pe.wait_ge(w2_in[u], 16 * i + 16)
                    pe.wait_ge(y_c, 1 + 2 * i + u)
                    for z in range(2):
                        for k in range(4):
                            mm = nc.tensor.matmul(pY[:, z, :], hT[:, u, k, :], w2[:, u, k, HALF * z:HALF * z + HALF],
                                                  start=k == 0, stop=k == 3)
                    mm.then_inc(y_mm, 1)

                hidden(0)
                hidden(1)
                output(0)
                output(1)

        @block.scalar
        def _(act):
            for s in (xT_c, hT_c):
                act.nop().then_inc(s, 1)
            with act.Fori(0, passes(act)) as i:
                def rows(u):
                    for z in range(2):
                        act.wait_ge(turned, 1 + 4 * i + 2 * u + z + 1)
                        nc.scalar.copy(xT[:, u, 4 * z:4 * z + 4, :].rearrange("p k t -> p (k t)"),
                                       pT[:, 0, :]).then_inc(xT_c, 1)

                def sigmoid(u):
                    act.wait_ge(h_mm, 2 + 2 * i + u + 1)
                    nc.scalar.activation(sg[:, u, :], pH[:, u, 0, :], ACT.Sigmoid).then_inc(sig, 1)

                rows(0)
                rows(1)
                sigmoid(0)
                sigmoid(1)
                for u in range(2):
                    act.wait_ge(h_turned, 2 * i + u + 1)
                    nc.scalar.copy(hT[:, u, :, :].rearrange("p k t -> p (k t)"), pT[:, 1, :]).then_inc(hT_c, 1)

        @block.vector
        def _(dve):
            for s in (hid, y_c):
                dve.nop().then_inc(s, 1)
            with dve.Fori(0, passes(dve)) as i:
                for u in range(2):
                    dve.wait_ge(sig, 2 * i + u + 1)
                    nc.vector.tensor_tensor(sg[:, u, :], sg[:, u, :], pH[:, u, 0, :], ALU.mult).then_inc(ch, 1)
                    dve.wait_ge(ch, 2 * i + u + 1)
                    nc.vector.tensor_tensor(hb[:, u, :], sg[:, u, :], pH[:, u, 1, :], ALU.mult).then_inc(hid, 1)
                for u in range(2):
                    dve.wait_ge(y_mm, 2 + 2 * i + u + 1)
                    dve.wait_ge(gt_in[u], 16 * i + 16)
                    dve.wait_ge(y_free, 1 + 2 * i)
                    nc.vector.tensor_scalar(y[:, u, :], pY[:].rearrange("p z n -> p (z n)"),
                                            gt[:, u, 1:2].bitcast(F32), None, ALU.mult).then_inc(y_c, 1)


def combine(nc, h2_d, y_d, io):
    with ExitStack() as c:
        def sb(name, shape, dt=F32):
            return c.enter_context(nc.sbuf_tensor(name, shape, dt))

        def sem(name):
            return c.enter_context(nc.semaphore(name))

        g, b = sb("ln3_g", [P, D]), sb("ln3_b", [P, D])
        h, r = sb("h2_rows", [P, 3, D]), sb("out_rows", [P, 3, D])
        ya = sb("expert_rows", [P, 3, 2, D])
        st, bn = sb("ln3_stats", [P, 3, 16]), sb("bn_stats3", [P, 2, 6])
        cin = sem("ln3_in")
        h_in = [sem(f"h2_in_{u}") for u in range(3)]
        y_in = [sem(f"expert_rows_in_{u}") for u in range(3)]
        stored = [sem(f"y_stored_{u}") for u in range(3)]
        ch, var, root, normed, scaled, ready = (sem(n) for n in (
            "dve_chain6", "ln3_var", "ln3_sqrt", "ln3_normed", "ln3_scaled", "y_ready"))
        aggr_begun = sem("ln3_aggregation_begun")
        block = c.enter_context(nc.Block())

        @block.sync
        def _(sp):
            for u in range(3):
                sp.nop().then_inc(stored[u], 16)
            sp.dma_start(g[:], io["ln3_g"].broadcast_to([P, D])).then_inc(cin, 16)
            sp.dma_start(b[:], io["ln3_b"].broadcast_to([P, D])).then_inc(cin, 16)
            with sp.Fori(0, 3) as i:
                for u in range(3):
                    sp.wait_ge(normed, 1 + 3 * i)
                    sp.dma_start(h[:, u, :], h2_d[ds(3 * P * i + P * u, P), :]).then_inc(h_in[u], 16)
                    sp.dma_start(ya[:, u, :, :], y_d[ds(6 * P * i + 2 * P * u, 2 * P), :].rearrange(
                        "(p z) n -> p z n", z=2)).then_inc(y_in[u], 16)
                for u in range(3):
                    sp.wait_ge(ready, 3 * i + u + 1)
                    sp.dma_start(io["out_y"][ds(3 * P * i + P * u, P), :], r[:, u, :]).then_inc(stored[u], 16)
            for u in range(3):
                sp.wait_ge(stored[u], 64)

        @block.scalar
        def _(act):
            with act.Fori(0, 3) as i:
                for u in range(3):
                    act.wait_ge(var, 3 * i + u + 1)
                    nc.scalar.activation(st[:, u, 3:4], st[:, u, 2:3], ACT.Sqrt).then_inc(root, 1)

        @block.vector
        def _(dve):
            dve.nop().then_inc(normed, 1)
            dve.wait_ge(cin, 32)
            with dve.Fori(0, 3) as i:
                at = [0]

                def link(ins):
                    at[0] += 1
                    ins.then_inc(ch, 1)
                    dve.wait_ge(ch, 24 * i + at[0])

                for u in range(3):
                    dve.wait_ge(h_in[u], 16 * i + 16)
                    dve.wait_ge(y_in[u], 16 * i + 16)
                    dve.wait_ge(stored[u], 16 * i + 16)
                    link(nc.vector.scalar_tensor_tensor(r[:, u, :], h[:, u, :], ALPHA, ya[:, u, 0, :], ALU.mult,
                                                        ALU.add))
                    link(nc.vector.tensor_tensor(r[:, u, :], r[:, u, :], ya[:, u, 1, :], ALU.add))
                    for n in range(2):
                        ins = nc.vector.bn_stats(bn[:, n, :], r[:, u, HALF * n:HALF * n + HALF])
                    link(ins)
                    dve.nop().then_inc(aggr_begun, 1)
                    link(nc.vector.bn_aggr(st[:, u, 0:2], bn[:].rearrange("p n s -> p (n s)")))
                    link(nc.vector.tensor_scalar(st[:, u, 2:3], st[:, u, 1:2], LN_EPS, None, ALU.add))
                    dve.nop().then_inc(var, 1)
                    dve.wait_ge(root, 3 * i + u + 1)
                    link(nc.vector.reciprocal(st[:, u, 4:5], st[:, u, 3:4]))
                    link(nc.vector.tensor_scalar(r[:, u, :], r[:, u, :], st[:, u, 0:1], st[:, u, 4:5], ALU.subtract,
                                                 ALU.mult))
                    dve.nop().then_inc(normed, 1)
                    link(nc.vector.tensor_tensor(r[:, u, :], r[:, u, :], g[:], ALU.mult))
                    nc.vector.tensor_tensor(r[:, u, :], r[:, u, :], b[:], ALU.add).then_inc(ready, 1)


def setup(nc, xT, ident, io):
    with nc.semaphore("x_in") as x_in, nc.semaphore("zeroed") as zeroed, nc.semaphore("ident_made") as made:
        sems = [x_in, zeroed, made]
        with nc.Block() as block:
            @block.sync
            def _(sp):
                sp.dma_start(xT[:], io["xT"]).then_inc(x_in, 16)
                sp.wait_ge(x_in, 16)

            @block.gpsimd
            def _(pool):
                nc.gpsimd.memset(ident[:], 0.0).then_inc(zeroed, 1)
                pool.wait_ge(zeroed, 1)
                nc.gpsimd.affine_select(out=ident[:], in_=ident[:], compare_op=ALU.not_equal, fill=1.0, base=0,
                                        pattern=[[-1, P]], channel_multiplier=1).then_inc(made, 1)
                pool.wait_ge(made, 1)
    return sems


def clear(nc, sems):
    with nc.Block() as block:
        @block.gpsimd
        def _(pool):
            for s in sems:
                pool.sem_clear(s)


def program(nc, io):
    with ExitStack() as c:
        ident = c.enter_context(nc.sbuf_tensor("ident", [P, P], F32))
        L = c.enter_context(nc.sbuf_tensor("router_logits", [P, NT, LOGITS], F32))
        rt = {
            "slot": c.enter_context(nc.sbuf_tensor("choice_slots", [P, 2, NT], I32)),
            "block_expert": c.enter_context(nc.sbuf_tensor("block_expert", [P, MAX_BLOCKS + 2], I32)),
            "pairs": c.enter_context(nc.sbuf_tensor("block_pairs", [P, 1], I32)),
        }
        pool_dmas = {n: c.enter_context(nc.semaphore(n)) for n in (
            "w_even_in", "w_odd_in", "shift_loaded", "slots_scattered", "tokens_in_0", "tokens_in_1", "rows_in_0", "rows_in_1",
            "outputs_scattered_0", "outputs_scattered_1")}
        with nc.sbuf_tensor("mixT", [P, KT, T], F32) as mixT:
            with nc.sbuf_tensor("xT", [P, KT, T], F32) as xT:
                sems = setup(nc, xT, ident, io)
                sems += attention_heads(nc, xT, mixT, ident, io)
                sems += rwkv_projection(nc, xT, pool_dmas, io["pa"], io)
            sems += rwkv(nc, mixT, ident, io["pa"], io)
            clear(nc, sems)
            mix_and_norm(nc, mixT, io["h1"], io)
        memory_and_router(nc, ident, L, io["h1"], io["h2"], io)
        route(nc, L, rt, pool_dmas, io)
        experts(nc, ident, rt, pool_dmas, io["h2"], io["y_rows"], io)
        combine(nc, io["h2"], io["y_rows"], io)


def kernel(**inputs):
    import numpy as np
    import concourse.bacc as bacc
    from concourse.bass_utils import run_bass_kernel_spmd

    nc = bacc.Bacc("TRN2", target_bir_lowering=False, num_devices=1)
    a = {k: np.ascontiguousarray(v) for k, v in inputs.items()}
    arrays, io = {}, {}

    def give(name, array):
        array = np.ascontiguousarray(array)
        arrays["in_" + name] = array
        io[name] = nc.dram_tensor("in_" + name, array.shape, mybir.dt.from_np(array.dtype), kind="ExternalInput").ap()
        return io[name]

    def take(name, shape):
        io[name] = nc.dram_tensor(name, shape, F32, kind="ExternalOutput").ap()

    x_all = np.concatenate([a["x_prompt"].reshape(SEQ, D), a["x_sample"].reshape(DB * DS, D)])
    io["xT"] = give("xT_", x_all.T).rearrange("(k p) t -> p k t", p=P)
    give("w_in", a["w_in"][0])
    io["w_in_diff"] = io["w_in"][:, C_RWKV:C_IN].rearrange("(k p) (s n) -> p k s n", p=P, s=3)
    give("cache_kT", a["cache_diff_k"][0].transpose(1, 0, 3, 2))
    give("cache_diff_v", a["cache_diff_v"])
    for n in ("diff_lq1", "diff_lk1", "diff_lq2", "diff_lk2"):
        give(n, a[n])
    give("subln", a["diff_subln"].reshape(P, 1))
    per_block = lambda v, n: v.reshape(n, P).T
    per_pair = lambda v: per_block(v, 4)
    io["w_in_rwkv"] = io["w_in"][:, 0:C_RWKV].rearrange("(k p) (c n) -> p k c n", p=P, n=P)
    give("shiftT", a["state_shift"].reshape(DB, NB, P).transpose(2, 1, 0))
    for n in ("w0", "a0", "k_k", "k_a", "r_k"):
        give(n, per_pair(a["rwkv_" + n]))
    give("mu", per_block(a["rwkv_mu"], NB))
    for n in ("w2", "a2", "g2"):
        give(n, a["rwkv_" + n][0])
    give("rwkv_ln_w", a["rwkv_ln_w"])
    give("rwkv_ln_b", a["rwkv_ln_b"])
    give("state", a["state_rwkv"].reshape(DB, 4, 2, 64, 64).transpose(2, 4, 1, 0, 3).reshape(P, 4, DB, 64))
    io["pa"] = nc.dram_tensor("pa_rows", (P, NB, XW), F32, kind="Internal").ap()
    give("x", x_all)
    rows = lambda w: w.rearrange("(k p) n -> p k n", p=P)
    for n in ("w_out", "mem_wq", "mem_wk", "mem_wv", "mem_wo"):
        io[n] = rows(give(n, a[n][0]))
    for n in ("ln1_g", "ln1_b", "ln2_g", "ln2_b", "ln3_g", "ln3_b"):
        give(n, a[n])
    io["memT"] = rows(give("memT", a["mem_prompt"][0].T))
    io["w_group"] = rows(give("w_group", a["moe_w_group"][0]))
    io["w_expert"] = rows(give("w_expert", a["moe_w_expert"][0]))
    give("b_group", a["moe_b_group"])
    give("b_expert", a["moe_b_expert"])
    io["cache_mem_kT"] = give("cache_mem_kT", a["cache_mem_k"][0].transpose(0, 2, 1)).rearrange(
        "b (k p) m -> b p k m", p=P)
    io["cache_mem_v"] = give("cache_mem_v", a["cache_mem_v"][0]).rearrange("b (m p) n -> b p m n", p=P)
    for n in ("w1", "w3", "w2"):
        io["moe_" + n] = give("moe_" + n, a["moe_" + n][0]).rearrange("e (k p) n -> p e k n", p=P)
    io["h1"] = nc.dram_tensor("h1_rows", (T, D), F32, kind="Internal").ap()
    io["h2"] = nc.dram_tensor("h2_rows_and_zero", (T + 1, D), F32, kind="Internal").ap()
    io["y_rows"] = nc.dram_tensor("y_rows", (2 * T + SLOTS + 2 * P, D), F32, kind="Internal").ap()
    io["slots"] = nc.dram_tensor("slots", (SLOTS + 2 * P, 3), I32, kind="Internal").ap()
    take("out_y", (T, D))
    take("out_mem_k_rows", (N_MEM, D))
    take("out_mem_v_rows", (N_MEM, D))
    for n in ("out_mem_k", "out_mem_v"):
        io[n] = io[n + "_rows"].rearrange("(m p) n -> p m n", p=P)
    take("out_shift", (P, NB, DB + 1))
    take("out_state_prompt", (P, 4, 64))
    take("out_state_sample", (P, 4, DB, 64))
    take("out_diff_k_prompt", (HEADS, SEQ, P))
    take("out_diff_v_prompt", (HEADS, SEQ, P))
    take("out_diff_k_sample", (HEADS, P, P))
    take("out_diff_v_sample", (HEADS, P, P))
    program(nc, io)
    r = run_bass_kernel_spmd(nc, [arrays], core_ids=[0]).results[0]
    sample = lambda o: o.reshape(HEADS, DB, DS, P).transpose(1, 0, 2, 3)[None]
    shift = r["out_shift"].transpose(2, 1, 0).reshape(DB + 1, C_RWKV)
    st_p = r["out_state_prompt"].reshape(2, 64, 4, 64).transpose(2, 0, 3, 1).reshape(1, 1, RH, 64, 64)
    st_s = r["out_state_sample"].reshape(2, 64, 4, DB, 64).transpose(3, 2, 0, 4, 1).reshape(1, DB, RH, 64, 64)
    return (r["out_y"][None, 0:SEQ], r["out_y"][SEQ:T].reshape(DB, DS, D), r["out_diff_k_prompt"][None, None], r["out_diff_v_prompt"][None, None],
            r["out_mem_k_rows"][None, None], r["out_mem_v_rows"][None, None], st_p, shift[None, None, 0:1],
            sample(r["out_diff_k_sample"]), sample(r["out_diff_v_sample"]), st_s, shift[None, 1:, None])
```

```python
from contextlib import ExitStack

import concourse.bass as bass
from concourse import mybir

F32 = mybir.dt.float32
I32 = mybir.dt.int32
ALU = mybir.AluOpType
ACT = mybir.ActivationFunctionType
AX = mybir.AxisListType
ds = bass.ds

P = 128
D = 1024
KT = D // P
SEQ = 1024
PT = SEQ // P
DB, DS = 8, 16
T = SEQ + DB * DS
NT = T // P
CHUNK = 64
HEADS = 4
QK = 64
C_RWKV = 1792
D_RWKV = 512
C_IN = 3328
PAST = 256
N_MEM = 256
NEG = -1e30
LAM_INIT = 0.2
ALPHA = 2.0 ** 0.25
LN_EPS = 1e-5
HALF = 512


def rwkv_masks(nc, pool, masks, fixed):
    pair1, hone, i64, cmask, lmask, notfirst, oneseq, colseq = (fixed[n] for n in (
        "pair1", "hone", "i64", "cmask", "lmask", "notfirst", "oneseq", "colseq"))
    made = [0]

    def then(ins):
        made[0] += 1
        ins.then_inc(masks, 1)
        pool.wait_ge(masks, made[0])

    def keep(ap, pattern, base, mult, cmp=ALU.is_ge, fill=0.0):
        then(nc.gpsimd.affine_select(out=ap, in_=ap, compare_op=cmp, fill=fill, base=base, pattern=pattern,
                                     channel_multiplier=mult))

    def blocks(ap, size):
        v = ap.rearrange("p (b i) -> p b i", i=size)
        keep(v, [[-size, P // size], [0, size]], 0, 1)
        keep(v, [[size, P // size], [0, size]], size - 1, -1)

    for m, size in ((cmask[0], CHUNK), (cmask[1], DS)):
        for n, (value, strict) in enumerate(((-1.0, 1), (1.0, 0), (1.0, 1), (1.0, 0))):
            then(nc.gpsimd.memset(m[:, n, :], value))
            keep(m[:, n, :], [[1, P]], -strict, -1)
            blocks(m[:, n, :], size)
    for l in range(6):
        s = 1 << l
        then(nc.gpsimd.memset(lmask[:, l, :], 1.0))
        blocks(lmask[:, l, :], 2 * s)
        v = lmask[:, l, :].rearrange("p (b i) -> p b i", i=2 * s)
        keep(v, [[2 * s, P // (2 * s)], [0, 2 * s]], s - 1, -1)
        keep(v, [[0, P // (2 * s)], [1, 2 * s]], -s, 0)
    for m, size in ((notfirst[0], CHUNK), (notfirst[1], DS)):
        then(nc.gpsimd.memset(m[:], 1.0))
        then(nc.gpsimd.memset(m[:].rearrange("p (b i) -> p b i", i=size)[:, :, 0:1], 0.0))
    then(nc.gpsimd.memset(pair1[:], 1.0))
    blocks(pair1[:], 64)
    then(nc.gpsimd.memset(hone[:], 1.0))
    keep(hone[:], [[-64, 2]], 0, 1)
    keep(hone[:], [[64, 2]], 63, -1)
    then(nc.gpsimd.memset(i64[:], 0.0))
    keep(i64[:], [[-1, 64]], 0, 1, ALU.not_equal, 1.0)
    keep(i64[:], [[-1, 64]], -64, 1, ALU.not_equal, 1.0)
    then(nc.gpsimd.memset(oneseq[:], 1.0))
    keep(oneseq[:], [[-DS, DB]], 0, 1)
    keep(oneseq[:], [[DS, DB]], DS - 1, -1)
    then(nc.gpsimd.memset(colseq[:], 1.0))
    keep(colseq[:], [[-DS, DB], [1, P]], 0, 0)
    keep(colseq[:], [[DS, DB], [-1, P]], DS - 1, 0)


def attention_heads(nc, xT, mixT, ident, fixed, io):
    c = ExitStack()
    with c:
        def sb(name, shape, dt=F32):
            return c.enter_context(nc.sbuf_tensor(name, shape, dt))

        sems = []

        def sem(name):
            sems.append(c.enter_context(nc.semaphore(name)))
            return sems[-1]

        wh = sb("w_head", [P, KT, 3, P])
        qT = sb("qT", [P, T + DS])
        kT = sb("kT", [P, T])
        v = sb("v_tok", [P, NT, P])
        ktok = sb("k_tok", [P, NT, P])
        kc = sb("k_cache_T", [P, 2, 4, PAST])
        vc = sb("v_cache", [P, 2, 4, 2, P])
        S = sb("scores", [P, 2, 2, SEQ])
        at = sb("attn", [P, 2, SEQ])
        aT = sb("attn_T", [P, 8, P])
        osb = sb("o_units", [P, 10, P])
        tabP = sb("bias_prompt", [P, SEQ])
        tabS = sb("bias_sample", [P, 2, 384])
        itmp = sb("iota_tmp", [P, SEQ], I32)
        stat = sb("softmax_stats", [P, 2, 8])
        ss = sb("o_square_sums", [P, 10])
        rst = sb("o_rstd", [P, 2, 10])
        sq = sb("square_scratch", [P, P])
        sub = sb("subln", [P, 1])
        lqk = sb("lambda_vectors", [P, 4, QK])
        lam = sb("lambda_terms", [P, 8])
        psS = c.enter_context(nc.psum_tensor("psS", [P, 2, SEQ], F32))
        psT = c.enter_context(nc.psum_tensor("psT", [P, 2, HALF], F32))
        psO = c.enter_context(nc.psum_tensor("psO", [P, HALF], F32))

        consts_in, w_in_, caches_in = sem("consts_in"), sem("w_head_in"), sem("caches_in")
        iota_done, tables = sem("iota_done"), sem("tables_done")
        pj_full, pj_evac = sem("transposed_ready"), sem("transposed_copied")
        s_ready, s_biased, s_exp = sem("scores_ready"), sem("scores_biased"), sem("scores_exp")
        at_ready, pv_done, o_saved = sem("attn_ready"), sem("pv_done"), sem("o_saved")
        dvec, actc = sem("dve_chain"), sem("lambda_exps")
        rms_var, rms_sqrt, o_scaled = sem("rms_var"), sem("rms_sqrt"), sem("o_scaled")
        bias_begun, scores_begun = sem("bias_begun"), sem("scores_begun")
        proj_done, kv_out, masks = sem("projections_done"), sem("kv_stored"), sem("rwkv_masks_made")

        width = [P * (u + 1) for u in range(PT)] + [384, 384]
        groups = [-(-w // HALF) for w in width]
        NPROJ = 12
        JOBS = NPROJ + sum(groups) + 3
        first_job = [NPROJ + sum(groups[:u]) for u in range(10)]
        CH = T // 3

        block = c.enter_context(nc.Block())

        @block.sync
        def _(sp):
            sp.nop().then_inc(kv_out, 16)
            sp.dma_start(sub[:], io["subln"]).then_inc(consts_in, 16)
            for n, name in enumerate(("diff_lq1", "diff_lk1", "diff_lq2", "diff_lk2")):
                sp.dma_start(lqk[:, n, :], io[name].broadcast_to([P, QK])).then_inc(consts_in, 16)
            with sp.Fori(0, HEADS) as h:
                sp.wait_ge(proj_done, 1 + h)
                for n in range(3):
                    sp.dma_start(wh[:, :, n, :], io["w_in_diff"][:, :, n, ds(h * P, P)]).then_inc(w_in_, 16)
                sp.wait_ge(pv_done, 1 + 10 * h)
                for g in range(2):
                    sp.dma_start(kc[:, g, :, :], io["cache_kT"][ds(h, 1), 4 * g:4 * g + 4, :, :].rearrange(
                        "o b d k -> d (o b) k")).then_inc(caches_in, 16)
                    for b in range(4):
                        sp.dma_start(vc[:, g, b, :, :], io["cache_diff_v"][0, 4 * g + b, ds(h, 1), :, :].rearrange(
                            "o (t p) d -> p (o t) d", p=P)).then_inc(caches_in, 16)
                sp.wait_ge(pj_evac, 1 + JOBS * h + NPROJ)
                sp.dma_start(io["out_diff_k_prompt"][ds(h, 1), :, :].rearrange("o (t p) d -> p (o t) d", p=P),
                             ktok[:, 0:PT, :]).then_inc(kv_out, 16)
                sp.dma_start(io["out_diff_v_prompt"][ds(h, 1), :, :].rearrange("o (t p) d -> p (o t) d", p=P),
                             v[:, 0:PT, :]).then_inc(kv_out, 16)
                sp.dma_start(io["out_diff_k_sample"][ds(h, 1), :, :].rearrange("o p d -> p (o d)"),
                             ktok[:, PT, :]).then_inc(kv_out, 16)
                sp.dma_start(io["out_diff_v_sample"][ds(h, 1), :, :].rearrange("o p d -> p (o d)"),
                             v[:, PT, :]).then_inc(kv_out, 16)
            sp.wait_ge(kv_out, 16 + 64 * HEADS)

        @block.gpsimd
        def _(pool):
            nc.gpsimd.iota(itmp[:, :], pattern=[[-1, SEQ]], base=SEQ - P, channel_multiplier=1).then_inc(iota_done, 1)
            pool.wait_ge(tables, 1)
            for r in range(4):
                q = slice(32 * r, 32 * r + 32)
                nc.gpsimd.iota(itmp[q, 0:PAST], pattern=[[-1, PAST]], base=PAST, channel_multiplier=1)
                nc.gpsimd.iota(itmp[q, PAST:PAST + DS], pattern=[[-1, DS]], base=0,
                               channel_multiplier=1).then_inc(iota_done, 1)
            pool.wait_ge(iota_done, 5)
            rwkv_masks(nc, pool, masks, fixed)

        @block.vector
        def _(dve):
            chained = [0]

            def then(ins):
                chained[0] += 1
                ins.then_inc(dvec, 1)
                dve.wait_ge(dvec, chained[0])

            dve.nop().then_inc(s_biased, 1)
            slope = 8.0 * 2.0 ** -2
            dve.wait_ge(iota_done, 1)
            then(nc.vector.tensor_copy(tabP[:], itmp[:]))
            then(nc.vector.scalar_tensor_tensor(S[:, 0, 0, :], tabP[:], -1.0, tabP[:], ALU.mult, ALU.max))
            ins = nc.vector.tensor_scalar(tabP[:], S[:, 0, 0, :], -slope, None, ALU.mult)
            then(ins)
            nc.vector.memset(tabP[0:CHUNK, SEQ - CHUNK:SEQ], NEG).then_inc(tables, 1)
            dve.wait_ge(iota_done, 5)
            then(nc.vector.tensor_copy(S[:, 0, 0, 0:PAST + DS], itmp[:, 0:PAST + DS]))
            then(nc.vector.scalar_tensor_tensor(S[:, 1, 0, 0:PAST + DS], S[:, 0, 0, 0:PAST + DS], -1.0,
                                                S[:, 0, 0, 0:PAST + DS], ALU.mult, ALU.max))
            then(nc.vector.memset(tabS[:], NEG))
            for g in range(2):
                nc.vector.tensor_scalar(tabS[:, g, 0:PAST], S[:, 1, 0, 0:PAST], -slope, None, ALU.mult)
                for r in range(4):
                    q = slice(32 * r, 32 * r + 32)
                    o = PAST + DS * (4 * g + r)
                    ins = nc.vector.tensor_scalar(tabS[q, g, o:o + DS], S[q, 1, 0, PAST:PAST + DS], -slope, None,
                                                  ALU.mult)
            then(ins)
            then(nc.vector.memset(qT[:, T:T + DS], 0.0))
            dve.wait_ge(consts_in, 80)
            for n in range(2):
                then(nc.vector.tensor_tensor_reduce(sq[:, 0:QK], lqk[:, 2 * n, :], lqk[:, 2 * n + 1, :], 1.0, 0.0,
                                                    ALU.mult, ALU.add, lam[:, n:n + 1]))
            then(nc.vector.tensor_scalar(sub[:], sub[:], 1.0 - LAM_INIT, None, ALU.mult))
            dve.nop().then_inc(tables, 1)
            dve.wait_ge(actc, 1)
            then(nc.vector.tensor_tensor(lam[:, 4:5], lam[:, 3:4], lam[:, 2:3], ALU.subtract))
            then(nc.vector.tensor_scalar(lam[:, 5:6], lam[:, 4:5], -LAM_INIT, None, ALU.add))
            SETUP = chained[0]
            CHAIN = 10 * 2 + 10 * 3 + 3

            with dve.Fori(0, HEADS) as h:
                at_link = [0]

                def link(ins):
                    at_link[0] += 1
                    ins.then_inc(dvec, 1)
                    dve.wait_ge(dvec, CHAIN * h + SETUP + at_link[0])

                def bias_and_max(u):
                    dve.wait_ge(s_ready, 10 * h + u + 1)
                    dve.nop().then_inc(bias_begun, 1)
                    w = width[u]
                    tab = tabP[:, SEQ - w:SEQ] if u < PT else tabS[:, u - PT, :]
                    st = stat[:, u % 2, :]
                    for k in range(2):
                        ins = nc.vector.tensor_tensor_reduce(S[:, u % 2, k, 0:w], psS[:, k, 0:w], tab, 1.0, -3e38,
                                                             ALU.add, ALU.max, st[:, k:k + 1])
                    link(ins)
                    link(nc.vector.tensor_scalar(st[:, 2:4], st[:, 0:2], -0.125, None, ALU.mult))
                    dve.nop().then_inc(s_biased, 1)

                def combine(u):
                    dve.wait_ge(s_exp, 20 * h + 2 * u + 2)
                    w = width[u]
                    st = stat[:, u % 2, :]
                    link(nc.vector.reciprocal(st[:, 6:8], st[:, 4:6]))
                    link(nc.vector.tensor_scalar(st[:, 7:8], st[:, 7:8], lam[:, 5:6], st[:, 4:5], ALU.mult, ALU.mult))
                    if u >= 2:
                        dve.wait_ge(pj_full, JOBS * h + first_job[u - 2] + groups[u - 2])
                    link(nc.vector.scalar_tensor_tensor(at[:, u % 2, 0:w], S[:, u % 2, 1, 0:w], st[:, 7:8],
                                                        S[:, u % 2, 0, 0:w], ALU.mult, ALU.add))
                    dve.nop().then_inc(at_ready, 1)

                bias_and_max(0)
                for u in range(10):
                    combine(u)
                    if u < 9:
                        bias_and_max(u + 1)
                nc.vector.tensor_scalar(tabP[:], tabP[:], 0.25, None, ALU.mult)
                nc.vector.tensor_scalar(tabS[:], tabS[:], 0.25, None, ALU.mult)
                dve.wait_ge(o_saved, 10 * h + 10)
                link(nc.vector.tensor_scalar(rst[:, 0, :], ss[:], 1.0 / P, 1e-5, ALU.mult, ALU.add))
                dve.nop().then_inc(rms_var, 1)
                dve.wait_ge(rms_sqrt, h + 1)
                link(nc.vector.reciprocal(rst[:, 0, :], rst[:, 1, :]))
                for u in range(10):
                    ins = nc.vector.tensor_scalar(osb[:, u, :], osb[:, u, :], rst[:, 0, u:u + 1], None, ALU.mult)
                link(ins)
                dve.nop().then_inc(o_scaled, 1)
                assert at_link[0] == CHAIN

        @block.scalar
        def _(act):
            act.nop().then_inc(pj_evac, 1)
            act.wait_ge(tables, 2)
            nc.scalar.activation(lam[:, 2:4], lam[:, 0:2], ACT.Exp).then_inc(actc, 1)
            with act.Fori(0, HEADS) as h:
                job = [0]

                def bank():
                    j = job[0]
                    job[0] += 1
                    act.wait_ge(pj_full, JOBS * h + j + 1)
                    return psT[:, j % 2, :]

                act.wait_ge(kv_out, 16 + 64 * h)
                for n in range(3):
                    nc.scalar.copy(qT[:, CH * n:CH * n + CH], bank()[:, 0:CH]).then_inc(pj_evac, 1)
                for n in range(3):
                    nc.scalar.copy(kT[:, CH * n:CH * n + CH], bank()[:, 0:CH]).then_inc(pj_evac, 1)
                for dst in (v, ktok):
                    for n in range(3):
                        k = min(4, NT - 4 * n)
                        nc.scalar.copy(dst[:, 4 * n:4 * n + k, :].rearrange("p t d -> p (t d)"),
                                       bank()[:, 0:k * P]).then_inc(pj_evac, 1)

                def exponentials(u):
                    act.wait_ge(s_biased, 1 + 10 * h + u + 1)
                    w, st = width[u], stat[:, u % 2, :]
                    for k in range(2):
                        nc.scalar.activation(S[:, u % 2, k, 0:w], S[:, u % 2, k, 0:w], ACT.Exp, bias=st[:, 2 + k:3 + k],
                                             scale=0.125, accum_out=st[:, 4 + k:5 + k]).then_inc(s_exp, 1)

                exponentials(0)
                for u in range(10):
                    for g in range(groups[u]):
                        k = min(HALF, width[u] - HALF * g)
                        nc.scalar.copy(aT[:, 4 * g:4 * g + k // P, :].rearrange("p t d -> p (t d)"),
                                       bank()[:, 0:k]).then_inc(pj_evac, 1)
                    if u < 9:
                        exponentials(u + 1)
                    act.wait_ge(pv_done, 1 + 10 * h + u + 1)
                    share = stat[:, u % 2, 6:7]
                    nc.scalar.activation(osb[:, u, :], psO[:, 0:P], ACT.Copy, scale=share)
                    nc.scalar.activation(sq[:], psO[:, 0:P], ACT.Square, scale=share,
                                         accum_out=ss[:, u:u + 1]).then_inc(o_saved, 1)
                act.wait_ge(rms_var, h + 1)
                nc.scalar.activation(rst[:, 1, :], rst[:, 0, :], ACT.Sqrt).then_inc(rms_sqrt, 1)
                for n in range(2):
                    nc.scalar.activation(mixT[:, ds(4 + h, 1), HALF * n:HALF * n + HALF].rearrange("p o t -> p (o t)"),
                                         bank(), ACT.Copy, scale=sub[:, 0:1]).then_inc(pj_evac, 1)
                src = bank()[:, 0:2 * P].rearrange("p (b i) -> p b i", i=32)[:, :, 0:DS]
                dst = mixT[:, ds(4 + h, 1), SEQ:T].rearrange("p o (b i) -> p (o b) i", i=DS)
                nc.scalar.activation(dst, src, ACT.Copy, scale=sub[:, 0:1]).then_inc(pj_evac, 1)
                assert job[0] == JOBS

        @block.tensor
        def _(pe):
            pe.nop().then_inc(proj_done, 1)
            pe.nop().then_inc(pv_done, 1)
            pe.wait_ge(tables, 2)
            with pe.Fori(0, HEADS) as h:
                job = [0]

                def bank():
                    j = job[0]
                    job[0] += 1
                    pe.wait_ge(pj_evac, 1 + JOBS * h + max(j - 1, 0))
                    return psT[:, j % 2, :]

                pe.wait_ge(w_in_, 48 * h + 48)
                for n in range(2):
                    for q in range(3):
                        o = bank()
                        for k in range(KT):
                            mm = nc.tensor.matmul(o[:, 0:CH], wh[:, k, n, :], xT[:, k, CH * q:CH * q + CH],
                                                  start=k == 0, stop=k == KT - 1)
                        mm.then_inc(pj_full, 1)
                for q in range(3):
                    o = bank()
                    for t in range(4 * q, min(4 * q + 4, NT)):
                        for k in range(KT):
                            mm = nc.tensor.matmul(o[:, (t % 4) * P:(t % 4) * P + P], xT[:, k, P * t:P * t + P],
                                                  wh[:, k, 2, :], start=k == 0, stop=k == KT - 1)
                    mm.then_inc(pj_full, 1)
                pe.wait_ge(pj_evac, 1 + JOBS * h + 6)
                for q in range(3):
                    o = bank()
                    for t in range(4 * q, min(4 * q + 4, NT)):
                        mm = nc.tensor.transpose(o[:, (t % 4) * P:(t % 4) * P + P], kT[:, P * t:P * t + P], ident[:])
                        if t == 0:
                            mm.then_inc(proj_done, 1)
                    mm.then_inc(pj_full, 1)

                def scores(u):
                    pe.wait_ge(s_biased, 1 + 10 * h + u)
                    pe.nop().then_inc(scores_begun, 1)
                    for k in range(2):
                        r = slice(QK * k, QK * k + QK)
                        if u < PT:
                            for c0 in range(0, width[u], HALF):
                                n = min(HALF, width[u] - c0)
                                mm = nc.tensor.matmul(psS[:, k, c0:c0 + n], qT[r, P * u:P * u + P], kT[r, c0:c0 + n],
                                                      start=True, stop=True)
                        else:
                            g = u - PT
                            for j in range(4):
                                o = SEQ + DS * (4 * g + j)
                                rows = slice(32 * j, 32 * j + 32)
                                nc.tensor.matmul(psS[rows, k, 0:PAST], qT[r, o:o + 32], kc[r, g, j, :],
                                                 start=True, stop=True)
                                mm = nc.tensor.matmul(psS[rows, k, PAST:384], qT[r, o:o + 32], kT[r, SEQ:T],
                                                      start=True, stop=True)
                    mm.then_inc(s_ready, 1)

                def weighted_values(u):
                    pe.wait_ge(at_ready, 10 * h + u + 1)
                    nb = width[u] // P
                    for g in range(groups[u]):
                        o = bank()
                        for b in range(4 * g, min(4 * g + 4, nb)):
                            mm = nc.tensor.transpose(o[:, (b % 4) * P:(b % 4) * P + P],
                                                     at[:, u % 2, P * b:P * b + P], ident[:])
                        mm.then_inc(pj_full, 1)
                    pe.wait_ge(pj_evac, 1 + JOBS * h + first_job[u] + groups[u])
                    if u < PT:
                        for b in range(nb):
                            mm = nc.tensor.matmul(psO[:, 0:P], aT[:, b, :], v[:, b, :], start=b == 0, stop=b == nb - 1)
                    else:
                        g = u - PT
                        for j in range(4):
                            rows = slice(32 * j, 32 * j + 32)
                            for b in range(3):
                                rhs = vc[:, g, j, b, :] if b < 2 else v[:, PT, :]
                                mm = nc.tensor.matmul(psO[rows, 0:P], aT[:, b, rows], rhs, start=b == 0, stop=b == 2)
                    mm.then_inc(pv_done, 1)

                pe.wait_ge(pj_evac, 1 + JOBS * h + NPROJ)
                pe.wait_ge(caches_in, 160 * h + 160)
                scores(0)
                for u in range(10):
                    if u < 9:
                        scores(u + 1)
                    weighted_values(u)
                pe.wait_ge(o_scaled, h + 1)
                for q in range(3):
                    o = bank()
                    for u in range(4 * q, min(4 * q + 4, 10)):
                        mm = nc.tensor.transpose(o[:, (u % 4) * P:(u % 4) * P + P], osb[:, u, :], ident[:])
                    mm.then_inc(pj_full, 1)
                assert job[0] == JOBS
            pe.wait_ge(pj_evac, 1 + JOBS * HEADS)
    return sems


RH = 8
NB = C_RWKV // P
XW = 1 + SEQ + DB * (DS + 1)
TW = DB * (DS + 1)
DECAY = 0.6065306597126334


def rwkv_projection(nc, xT, pool_dmas, pa_d, io):
    with ExitStack() as c:
        def sb(name, shape, dt=F32):
            return c.enter_context(nc.sbuf_tensor(name, shape, dt))

        sems = []

        def sem(name):
            sems.append(c.enter_context(nc.semaphore(name)))
            return sems[-1]

        w = sb("w_block", [P, 2, KT, P])
        row = sb("pa_row", [P, 2, XW])
        shift = sb("shift_in", [P, NB, DB])
        last = sb("shift_out", [P, NB, DB + 1])
        ps = c.enter_context(nc.psum_tensor("ps_proj", [P, 6, HALF], F32))
        w_got, s_in = [pool_dmas["w_even_in"], pool_dmas["w_odd_in"]], pool_dmas["shift_loaded"]
        full, copied, zero = sem("proj_full"), sem("proj_copied"), sem("row_zeroed")
        row_ready, row_out, last_out = sem("row_ready"), sem("row_stored"), sem("shift_stored")
        block = c.enter_context(nc.Block())
        GROUPS = [(0, HALF), (HALF, HALF), (SEQ, P)]

        @block.sync
        def _(sp):
            sp.nop().then_inc(row_out, 16)
            sp.wait_ge(zero, 1)
            with sp.Fori(0, NB // 2) as i:
                for b in range(2):
                    sp.wait_ge(row_ready, 1 + 2 * i + b + 1)
                    sp.dma_start(pa_d[:, ds(2 * i + b, 1), :].rearrange("p o x -> p (o x)"),
                                   row[:, b, :]).then_inc(row_out, 16)
            sp.wait_ge(row_ready, 1 + NB)
            sp.dma_start(io["out_shift"], last[:]).then_inc(last_out, 16)
            sp.wait_ge(row_out, 16 + 16 * NB)
            sp.wait_ge(last_out, 16)

        @block.gpsimd
        def _(pool):
            nc.gpsimd.memset(row[:, :, 0:1], 0.0).then_inc(zero, 1)
            pool.dma_start(shift[:], io["shiftT"]).then_inc(s_in, 16)
            with pool.Fori(0, NB // 2) as i:
                for b in range(2):
                    pool.wait_ge(full, 1 + 6 * i)
                    pool.dma_start(w[:, b, :, :].rearrange("p k (o n) -> p k o n", o=1),
                                 io["w_in_rwkv"][:, :, ds(2 * i + b, 1), :]).then_inc(w_got[b], 16)

        @block.scalar
        def _(act):
            act.nop().then_inc(row_ready, 1)
            act.wait_ge(s_in, 16)
            with act.Fori(0, NB // 2) as i:
                for b in range(2):
                    act.wait_ge(row_out, 16 + 32 * i)
                    for q, (c0, n) in enumerate(GROUPS):
                        act.wait_ge(full, 1 + 6 * i + 3 * b + q + 1)
                        if q < 2:
                            nc.scalar.copy(row[:, b, 1 + c0:1 + c0 + n], ps[:, 3 * b + q, 0:n]).then_inc(copied, 1)
                        else:
                            dst = row[:, b, 1 + SEQ:XW].rearrange("p (b i) -> p b i", i=DS + 1)
                            src = ps[:, 3 * b + q, 0:n].rearrange("p (b i) -> p b i", i=DS)
                            nc.scalar.copy(dst[:, :, 1:DS + 1], src).then_inc(copied, 1)
                            nc.scalar.copy(last[:, ds(2 * i + b, 1), 1:DB + 1].rearrange("p o b -> p (o b)"),
                                           src[:, :, DS - 1])
                            nc.scalar.copy(dst[:, :, 0],
                                           shift[:, ds(2 * i + b, 1), :].rearrange("p o b -> p (o b)"))
                            nc.scalar.copy(last[:, ds(2 * i + b, 1), 0:1].rearrange("p o b -> p (o b)"),
                                           ps[:, 3 * b + 1, HALF - 1:HALF]).then_inc(row_ready, 1)

        @block.tensor
        def _(pe):
            pe.nop().then_inc(full, 1)
            with pe.Fori(0, NB // 2) as i:
                for b in range(2):
                    pe.wait_ge(w_got[b], 16 * i + 16)
                    for q, (c0, n) in enumerate(GROUPS):
                        pe.wait_ge(row_ready, 1 + 2 * i)
                        for k in range(KT):
                            mm = nc.tensor.matmul(ps[:, 3 * b + q, 0:n], w[:, b, k, :], xT[:, k, c0:c0 + n],
                                                  start=k == 0, stop=k == KT - 1)
                        mm.then_inc(full, 1)
    return sems


def rwkv(nc, mixT, ident, fixed, pa_d, io):
    with ExitStack() as c:
        def sb(name, shape, dt=F32):
            return c.enter_context(nc.sbuf_tensor(name, shape, dt))

        sems = []

        def sem(name):
            sems.append(c.enter_context(nc.semaphore(name)))
            return sems[-1]

        vecs = sb("rwkv_vectors", [P, 6, 4])
        mu = sb("mu", [P, NB])
        w2 = sb("w2_a2", [P, D_RWKV])
        g2 = sb("g2", [P, D_RWKV])
        lnw = sb("gn_w", [P, D_RWKV])
        lnb = sb("gn_b", [P, D_RWKV])
        pair1, hone, i64, cmask, lmask, notfirst, oneseq, colseq = (fixed[n] for n in (
            "pair1", "hone", "i64", "cmask", "lmask", "notfirst", "oneseq", "colseq"))
        x = sb("pa_tile", [P, NB, TW])
        sh = sb("shifted", [P, NB, P])
        low = sb("lora_in", [P, 2, 2, P])
        dec = sb("decay", [P, HALF])
        rate = sb("rate", [P, HALF])
        kk = sb("kk", [P, HALF])
        t1 = sb("scratch_1", [P, HALF])
        t2 = sb("scratch_2", [P, HALF])
        W = sb("decay_product", [P, 2, HALF])
        beta = sb("beta", [P, 2, 4, P])
        kap = sb("kappa", [P, 2, 4, P])
        kr = sb("khat_rho", [P, 2, 4, 2, P])
        rk = sb("bonus_products", [P, 2, HALF])
        bt = sb("beta_tok", [P, 2, RH, 64])
        kt = sb("kappa_tok", [P, 2, RH, 64])
        kv = sb("khat_tok_and_mv", [P, 2, RH, 2, 64])
        vt = sb("v_tok_rwkv", [P, 2, RH, 64])
        pg = sb("minus_p_g", [P, RH, 2, 64])
        G = sb("grams", [P, 2, 4, 4, P])
        N = sb("level_n", [P, 2, 2, 4, P])
        XT = sb("x_transposed", [P, 2, 4, P])
        X = sb("x_inverse", [P, 2, 4, P])
        Y = sb("y_level", [P, 2, 4, P])
        QT = sb("q_transposed", [P, 4, P])
        AB = sb("a_b", [P, 2, 2, 2, 2, 64])
        St = sb("state", [P, 2, 4, 64])
        ABs = kr[:, 1].rearrange("p g z t -> p (g z t)").rearrange("p (z b k) -> p z b k", z=2, b=DB)
        Qs = kv[:, 1].rearrange("p h z k -> p (h z k)").rearrange("p (b t) -> p b t", b=DB)
        ex = sb("values_by_sequence", [P, 3, DB, 64])
        Ss = sb("state_sample", [P, 4, DB, 64])
        So = sb("state_sample_new", [P, 4, DB, 64])
        o = sb("o_rwkv", [P, RH, 64])
        o2 = sb("o_scratch", [P, RH, 64])
        gn = sb("gn_stats", [P, 5, RH])

        ps = c.enter_context(nc.psum_tensor("ps_rwkv", [P, 8, HALF], F32))

        cin, masks, x_got = sem("rwkv_consts_in"), sem("masks_made"), sem("pa_tile_in")
        x_used, fch, vch, tch = sem("pa_tile_used"), sem("dve_chain_front"), sem("dve_chain_solve"), sem("dve_chain_tail")
        mixed, lora_in, lora_out, lora_used = sem("shift_mixed"), sem("lora_in_ready"), sem("lora_out_ready"), sem(
            "lora_out_used")
        sig, decays, kk_sq, nrm = sem("sigmoids"), sem("decays_ready"), sem("kk_squares"), sem("norms_summed")
        nrm_root, gn_var, gn_root = sem("norms_rooted"), sem("gn_var"), sem("gn_root")
        ch_ready, tr, tr_copied = sem("channel_values_ready"), sem("turned"), sem("turned_copied")

        def of_group(name):
            return [sem(f"{name}_{g}") for g in range(2)]

        gram, gram_used, lev = of_group("gram_ready"), of_group("gram_masked"), of_group("level_masked")
        x0, nx, y_ready = of_group("x0_ready"), of_group("n_x_product"), of_group("y_ready")
        x_mm, x_c = of_group("x_product"), of_group("x_copied")
        mv, mv_c, pgd, pg_c = of_group("mv_ready"), of_group("mv_copied"), of_group("pg_ready"), of_group("pg_copied")
        qab, qab_used = of_group("q_a_b_ready"), of_group("q_a_b_used")
        st_mm, st_new = of_group("state_product"), of_group("state_updated")
        o_mm, o_copied = of_group("o_ready"), of_group("o_copied")
        gate, o_fin, o_tr, o_mix = sem("gate_ready"), sem("o_final"), sem("o_turned"), sem("o_in_mix")
        st_out, exq, ab_mm, exv = sem("states_stored"), sem("q_expanded"), sem("ab_ready"), sem("values_expanded")
        ab_used, state_seen = sem("ab_used"), sem("state_seen")
        block = c.enter_context(nc.Block())
        CONSTS = 16 * 12
        MASKS = 1

        def bc(vec, n):
            return vec.rearrange("p (g o) -> p g o", o=1).broadcast_to([P, vec.shape[1], n])

        def g4(ap):
            return ap.rearrange("p (g t) -> p g t", g=4)

        def flat(ap):
            return ap.rearrange("p a b -> p (a b)")

        def last_level(sample):
            return 3 if sample else 5

        def first(t):
            return isinstance(t, int) and t == 0

        def after_is_sample(t):
            return int(isinstance(t, int) and t == PT - 1)

        def levels_before(t):
            return 6 * t

        def each_tile(eng, front, solve, tail):
            front(0, 0, 0)
            solve(0, 0, 0)
            with eng.Fori(0, (PT - 2) // 2) as i:
                solve(2 * i + 1, 1, 0)
                solve(2 * i + 2, 0, 0)
            solve(PT - 1, 1, 0)
            solve(PT, 0, 1)
            tail(PT, 0)

        @block.sync
        def _(sp):
            for n, name in enumerate(("w0", "a0", "k_k", "k_a", "r_k")):
                sp.dma_start(vecs[:, n, :], io[name]).then_inc(cin, 16)
            sp.dma_start(mu[:], io["mu"]).then_inc(cin, 16)
            sp.dma_start(w2[0:64, :], io["w2"]).then_inc(cin, 16)
            sp.dma_start(w2[64:P, :], io["a2"]).then_inc(cin, 16)
            sp.dma_start(g2[:], io["g2"]).then_inc(cin, 16)
            sp.dma_start(lnw[:], io["rwkv_ln_w"].broadcast_to([P, D_RWKV])).then_inc(cin, 16)
            sp.dma_start(lnb[:], io["rwkv_ln_b"].broadcast_to([P, D_RWKV])).then_inc(cin, 16)
            sp.dma_start(Ss[:], io["state"]).then_inc(cin, 16)
            with sp.Fori(0, PT) as t:
                sp.wait_ge(x_used, 1 + t)
                sp.dma_start(x[:, :, 0:P + 1], pa_d[:, :, ds(P * t, P + 1)]).then_inc(x_got, 16)
            sp.wait_ge(x_used, 1 + PT)
            sp.dma_start(x[:, :, :], pa_d[:, :, 1 + SEQ:XW]).then_inc(x_got, 16)
            for g in range(2):
                sp.wait_ge(st_new[g], 2 * PT)
            sp.dma_start(io["out_state_prompt"], St[:, 0, :, :]).then_inc(st_out, 16)
            for g in range(2):
                sp.wait_ge(st_new[g], 2 * PT + 2)
            sp.dma_start(io["out_state_sample"], So[:]).then_inc(st_out, 16)
            sp.wait_ge(st_out, 32)

        @block.gpsimd
        def _(pool):
            nc.gpsimd.memset(St[:, 0, :, :], 0.0).then_inc(masks, 1)

            def levels(t, u, sample):
                for l in range(last_level(sample) + 1):
                    for g in range(2):
                        if l == 0:
                            pool.wait_ge(gram_used[g], 4 * t + 4)
                        elif l == 2:
                            pool.wait_ge(x0[g], t + 1)
                        elif l > 2:
                            pool.wait_ge(nx[g], 5 * t + l - 2)
                        nc.gpsimd.tensor_tensor(N[:, g, l % 2, :, :], G[:, g, :, 0, :],
                                                lmask[:, l:l + 1, :].broadcast_to([P, 4, P]),
                                                ALU.mult).then_inc(lev[g], 1)

            each_tile(pool, lambda t, u, s: None, levels, lambda t, u: None)

        FCH, VCH, TCH = 21, 2, 11

        @block.vector
        def _(dve):
            def chain(signal, before):
                at = [0]

                def link(ins):
                    at[0] += 1
                    ins.then_inc(signal, 1)
                    dve.wait_ge(signal, before + at[0])
                return link

            def shift(t, sample):
                link = chain(fch, 1 + FCH * t)
                if sample:
                    xv = x[:].rearrange("p c (b i) -> p c b i", i=DS + 1)
                    cur, prev = xv[:, :, :, 1:DS + 1], xv[:, :, :, 0:DS]
                    shv = sh[:].rearrange("p c (b i) -> p c b i", i=DS)
                else:
                    cur, prev, shv = x[:, :, 1:P + 1], x[:, :, 0:P], sh[:]
                dve.wait_ge(x_got, 16 * t + 16)
                dve.wait_ge(tr, 1 + 4 * t)
                if sample:
                    for n in range(NB):
                        ins = nc.vector.tensor_tensor(shv[:, n], prev[:, n], cur[:, n], ALU.subtract)
                else:
                    ins = nc.vector.tensor_tensor(shv, prev, cur, ALU.subtract)
                link(ins)
                link(nc.vector.tensor_tensor(sh[:], sh[:], bc(mu[:], P), ALU.mult))
                if sample:
                    for n in range(NB):
                        ins = nc.vector.tensor_tensor(shv[:, n], shv[:, n], cur[:, n], ALU.add)
                else:
                    ins = nc.vector.tensor_tensor(shv, shv, cur, ALU.add)
                link(ins)
                dve.nop().then_inc(mixed, 1)
                dve.nop().then_inc(x_used, 1)

            def lora_sums(t):
                link = chain(fch, 1 + FCH * t + 3)
                dve.wait_ge(lora_out, t + 1)
                nc.vector.tensor_tensor(g4(dec[:]), g4(ps[:, 3, :]), bc(vecs[:, 0, :], P), ALU.add)
                link(nc.vector.tensor_tensor(g4(rate[:]), g4(ps[:, 7, :]), bc(vecs[:, 1, :], P), ALU.add))
                dve.nop().then_inc(lora_used, 1)
                link(nc.vector.tensor_tensor(g4(kk[:]), sh[:, 4:8, :], bc(vecs[:, 2, :], P), ALU.mult))
                link(nc.vector.tensor_tensor(t1[:], kk[:], kk[:], ALU.mult))
                dve.nop().then_inc(kk_sq, 1)

            def keys(t):
                link = chain(fch, 1 + FCH * t + 6)
                k = sh[:, 4:8, :]
                dve.wait_ge(nrm_root, t + 1)
                link(nc.vector.tensor_scalar(t2[:], t2[:], 1e-12, None, ALU.max))
                link(nc.vector.reciprocal(t2[:], t2[:]))
                link(nc.vector.tensor_tensor(kk[:], kk[:], t2[:], ALU.mult))
                dve.wait_ge(sig, t + 1)
                link(nc.vector.tensor_tensor(g4(t1[:]), g4(rate[:]), bc(vecs[:, 3, :], P), ALU.mult))
                link(nc.vector.tensor_tensor(g4(t1[:]), g4(t1[:]), bc(vecs[:, 5, :], P), ALU.add))
                link(nc.vector.tensor_tensor(k, k, g4(t1[:]), ALU.mult))

            def channel_values(t, u, sample):
                link = chain(fch, 1 + FCH * t + 12)
                r, k = sh[:, 0:4, :], sh[:, 4:8, :]
                size = DS if sample else CHUNK
                dve.wait_ge(decays, t + 1)
                link(nc.vector.tensor_tensor(t1[:], dec[:], notfirst[sample][:], ALU.mult))
                link(nc.vector.tensor_tensor(dec[:], dec[:], t1[:], ALU.subtract))
                link(nc.vector.tensor_tensor_scan(W[:, u, :], t1[:], dec[:], 0.0, ALU.mult, ALU.add))
                link(nc.vector.reciprocal(t2[:], W[:, u, :]))
                krv = kr[:, u, :, 0, :]
                nc.vector.tensor_tensor(kr[:, u, :, 1, :], r, g4(W[:, u, :]), ALU.mult)
                link(nc.vector.tensor_tensor(krv[:, :, 1:P], g4(kk[:])[:, :, 1:P], g4(W[:, u, :])[:, :, 0:P - 1],
                                             ALU.mult))
                for n in range(4):
                    ins = nc.vector.tensor_copy(krv[:, n, :].rearrange("p (b i) -> p b i", i=size)[:, :, 0],
                                                g4(kk[:])[:, n, :].rearrange("p (b i) -> p b i", i=size)[:, :, 0])
                link(ins)
                link(nc.vector.tensor_tensor(kk[:], kk[:], rate[:], ALU.mult))
                nc.vector.tensor_tensor(beta[:, u], g4(kk[:]), g4(t2[:]), ALU.mult)
                nc.vector.tensor_tensor(kap[:, u], k, g4(t2[:]), ALU.mult)
                link(nc.vector.tensor_tensor(g4(rk[:, u, :]), r, k, ALU.mult))
                link(nc.vector.tensor_tensor(g4(rk[:, u, :]), g4(rk[:, u, :]), bc(vecs[:, 4, :], P), ALU.mult))
                dve.nop().then_inc(ch_ready, 1)

            def tail(t, u):
                link = chain(tch, TCH * t)
                for g in range(2):
                    dve.wait_ge(o_copied[g], t + 1)
                bh = lambda s: s.rearrange("p (h o) -> p h o", o=1).broadcast_to([P, RH, 64])
                link(nc.vector.tensor_reduce(gn[:, 0, :], o[:], AX.X, ALU.add))
                link(nc.vector.tensor_scalar(gn[:, 1, :], gn[:, 0, :], 1.0 / 64, None, ALU.mult))
                link(nc.vector.tensor_tensor(o[:], o[:], bh(gn[:, 1, :]), ALU.subtract))
                link(nc.vector.tensor_tensor(o2[:], o[:], o[:], ALU.mult))
                link(nc.vector.tensor_reduce(gn[:, 2, :], o2[:], AX.X, ALU.add))
                link(nc.vector.tensor_scalar(gn[:, 2, :], gn[:, 2, :], 1.0 / 64, 64e-5, ALU.mult, ALU.add))
                dve.nop().then_inc(gn_var, 1)
                dve.wait_ge(gn_root, t + 1)
                link(nc.vector.reciprocal(gn[:, 4, :], gn[:, 3, :]))
                link(nc.vector.tensor_tensor(o[:], o[:], bh(gn[:, 4, :]), ALU.mult))
                link(nc.vector.tensor_tensor(flat(o[:]), flat(o[:]), lnw[:], ALU.mult))
                dve.wait_ge(gate, t + 1)
                nc.vector.tensor_tensor(flat(o[:]), flat(o[:]), lnb[:], ALU.add)
                link(nc.vector.tensor_tensor(o2[:], vt[:, u], bh(ps[:, 3, 0:RH]), ALU.mult))
                link(nc.vector.tensor_tensor(o[:], o[:], o2[:], ALU.add))
                nc.vector.tensor_tensor(flat(o[:]), flat(o[:]), ps[:, 7, :], ALU.mult).then_inc(o_fin, 1)

            idb = ident[:].rearrange("p (o t) -> p o t", o=1).broadcast_to([P, 4, P])

            def level(t, l):
                for g in range(2):
                    dve.wait_ge(nx[g], 5 * t + l)
                    nc.vector.tensor_tensor(Y[:, g], g4(ps[:, 4 * g, :]), idb, ALU.add).then_inc(y_ready[g], 1)

            def solve(t, u, sample):
                link = chain(vch, VCH * t)
                for g in range(2):
                    for h in range(4):
                        dve.wait_ge(gram[g], 4 * t + h + 1)
                        nc.vector.tensor_tensor(G[:, g, h, :, :].rearrange("p k t -> p (k t)"), ps[:, 4 * g + h, :],
                                                cmask[sample][:].rearrange("p k t -> p (k t)"),
                                                ALU.mult).then_inc(gram_used[g], 1)
                for g in range(2):
                    dve.wait_ge(lev[g], levels_before(t) + 1)
                    nc.vector.tensor_tensor(XT[:, g], N[:, g, 0, :, :], idb, ALU.add).then_inc(x0[g], 1)
                level(t, 1)
                if not first(t):
                    tail(t - 1, 1 - u)
                level(t, 2)
                if not sample:
                    shift(t + 1, after_is_sample(t))
                level(t, 3)
                if not sample:
                    lora_sums(t + 1)
                    level(t, 4)
                    keys(t + 1)
                    level(t, 5)
                    channel_values(t + 1, 1 - u, after_is_sample(t))
                for g in range(2):
                    dve.wait_ge(qab[g], t + 1)
                    ins = nc.vector.tensor_tensor(QT[:, 2 * g:2 * g + 2, :],
                                                  ps[:, 4 * g + 2, 0:2 * P].rearrange("p (g t) -> p g t", g=2),
                                                  kr[:, u, 2 * g:2 * g + 2, 1, :], ALU.add)
                    if not sample:
                        Wc = g4(W[:, u, :])[:, 2 * g:2 * g + 2, :].rearrange("p g (c i) -> p g c i", i=CHUNK)
                        Wc = Wc[:, :, :, CHUNK - 1:CHUNK]
                        for cc in range(2):
                            nc.vector.tensor_tensor(
                                AB[:, g, 0, :, cc, :], ps[:, 4 * g + cc, 0:P].rearrange("p (g k) -> p g k", k=64),
                                i64[:].rearrange("p (o k) -> p o k", o=1).broadcast_to([P, 2, 64]), ALU.add)
                            ins = nc.vector.tensor_tensor(
                                AB[:, g, 1, :, cc, :], ps[:, 4 * g + cc, P:2 * P].rearrange("p (g k) -> p g k", k=64),
                                Wc[:, :, cc, :].broadcast_to([P, 2, 64]), ALU.mult)
                    link(ins)
                    dve.nop().then_inc(qab_used[g], 1)
                if not sample:
                    for cc in range(2):
                        for g in range(2):
                            dve.wait_ge(st_mm[g], 2 * t + cc + 1)
                            for n in range(2):
                                q = 2 * g + n
                                col = P * q + CHUNK * cc + CHUNK - 1
                                a_s = ps[:, 4 * g + 2, P * cc + 64 * n:P * cc + 64 * n + 64]
                                ins = nc.vector.scalar_tensor_tensor(
                                    St[:, 1 - cc, q, :], a_s, W[:, u, col:col + 1], AB[:, g, 1, n, cc, :],
                                    ALU.mult, ALU.add)
                            ins.then_inc(st_new[g], 1)
                else:
                    link = chain(vch, VCH * t + 2)
                    for q in range(4):
                        g, n = q // 2, q % 2
                        link(nc.vector.tensor_tensor(Qs, QT[:, q:q + 1, :].broadcast_to([P, DB, P]), colseq[:],
                                                     ALU.mult))
                        dve.nop().then_inc(exq, 1)
                        for hf in range(2):
                            h = 2 * q + hf
                            if h:
                                dve.wait_ge(ab_mm, h)
                            seq = oneseq[:].rearrange("p (b o) -> p b o", o=1).broadcast_to([P, DB, 64])
                            for z, src in enumerate((bt[:, u, h:h + 1, :], vt[:, u, h:h + 1, :], pg[:, h, 1:2, :])):
                                ins = nc.vector.tensor_tensor(ex[:, z, :, :], src.broadcast_to([P, DB, 64]), seq,
                                                              ALU.mult)
                            ins.then_inc(exv, 1)
                        dve.wait_ge(ab_mm, 2 * q + 2)
                        Wc = W[:, u, P * q:P * q + P].rearrange("p (b i) -> p b i", i=DS)[:, :, DS - 1:DS]
                        nc.vector.tensor_tensor(ABs[:, 0], ps[:, 4 * g, :].rearrange("p (b k) -> p b k", k=64),
                                                i64[:].rearrange("p (o k) -> p o k", o=1).broadcast_to([P, DB, 64]),
                                                ALU.add)
                        nc.vector.tensor_tensor(ABs[:, 1], ps[:, 4 * g + 1, :].rearrange("p (b k) -> p b k", k=64),
                                                Wc.broadcast_to([P, DB, 64]), ALU.mult).then_inc(ab_used, 1)
                        dve.wait_ge(st_mm[g], 2 * t + n + 1)
                        link(nc.vector.tensor_tensor(So[:, q, :, :], ps[:, 4 * g + 2, :].rearrange(
                            "p (b k) -> p b k", k=64), Wc.broadcast_to([P, DB, 64]), ALU.mult))
                        nc.vector.tensor_tensor(So[:, q, :, :], So[:, q, :, :], ABs[:, 1],
                                                ALU.add).then_inc(st_new[g], 1)

            def front(t, u, sample):
                shift(t, sample)
                lora_sums(t)
                keys(t)
                channel_values(t, u, sample)

            dve.nop().then_inc(x_used, 1)
            dve.wait_ge(cin, CONSTS)
            nc.vector.tensor_scalar(vecs[:, 5, :], vecs[:, 3, :], -1.0, 1.0, ALU.mult, ALU.add).then_inc(fch, 1)
            dve.wait_ge(fch, 1)
            dve.wait_ge(masks, MASKS)
            each_tile(dve, front, solve, tail)

        @block.scalar
        def _(act):
            def lora_inputs(t, u):
                act.wait_ge(mixed, t + 1)
                nc.scalar.activation(low[0:64, u, 0, :], sh[0:64, 12, :], ACT.Tanh)
                nc.scalar.copy(low[64:P, u, 0, :], sh[64:P, 12, :])
                nc.scalar.activation(low[:, u, 1, :], sh[:, 13, :], ACT.Sigmoid).then_inc(lora_in, 1)

            def rates(t):
                act.wait_ge(lora_used, t + 1)
                nc.scalar.activation(rate[:], rate[:], ACT.Sigmoid)
                nc.scalar.activation(dec[:], dec[:], ACT.Sigmoid).then_inc(sig, 1)
                act.wait_ge(sig, t + 1)
                nc.scalar.activation(dec[:], dec[:], ACT.Exp, scale=-DECAY).then_inc(decays, 1)

            def token_values(t, u):
                for n, d in enumerate((bt[:, u], kt[:, u], kv[:, u, :, 0, :], vt[:, u])):
                    act.wait_ge(tr, 1 + 4 * t + n + 1)
                    nc.scalar.copy(d, ps[:, (7, 3)[n % 2], :].rearrange("p (h k) -> p h k", k=64)).then_inc(
                        tr_copied, 1)

            def norm_roots(t):
                act.wait_ge(nrm, t + 1)
                nc.scalar.activation(t2[:], ps[:, 3, :], ACT.Sqrt).then_inc(nrm_root, 1)

            def deviations(t):
                act.wait_ge(gn_var, t + 1)
                nc.scalar.activation(gn[:, 3, :], gn[:, 2, :], ACT.Sqrt).then_inc(gn_root, 1)

            def output(t):
                act.wait_ge(o_tr, t + 1)
                nc.scalar.copy(mixT[:, 0:4, ds(P * t, P)], g4(ps[:, 3, :])).then_inc(o_mix, 1)

            def level(t, l, sample):
                for g in range(2):
                    act.wait_ge(x_mm[g], 6 * t + l + 1)
                    if l > 0:
                        ins = nc.scalar.copy(XT[:, g].rearrange("p h t -> p (h t)"), ps[:, 4 * g + 1, :])
                    if l < last_level(sample):
                        bank = ps[:, 4 * g + 2, :] if l else ps[:, 4 * g + 1, :]
                        ins = nc.scalar.copy(X[:, g].rearrange("p h t -> p (h t)"), bank)
                    ins.then_inc(x_c[g], 1)

            def solve(t, u, sample):
                level(t, 0, sample)
                level(t, 1, sample)
                if not first(t):
                    deviations(t - 1)
                level(t, 2, sample)
                if not first(t):
                    output(t - 1)
                if not sample:
                    lora_inputs(t + 1, 1 - u)
                level(t, 3, sample)
                if not sample:
                    rates(t + 1)
                    level(t, 4, sample)
                    norm_roots(t + 1)
                    level(t, 5, sample)
                for g in range(2):
                    act.wait_ge(mv[g], t + 1)
                    nc.scalar.copy(kv[:, u, 4 * g:4 * g + 4, 1, :],
                                   ps[:, 4 * g + 2, 0:256].rearrange("p (h k) -> p h k", k=64)).then_inc(mv_c[g], 1)
                for g in range(2):
                    act.wait_ge(pgd[g], t + 1)
                    nc.scalar.mul(pg[:, 4 * g:4 * g + 4, :, :].rearrange("p h z k -> p (h z k)"), ps[:, 4 * g, :],
                                  -1.0).then_inc(pg_c[g], 1)
                if not sample:
                    token_values(t + 1, 1 - u)
                if sample:
                    for g in range(2):
                        act.wait_ge(o_mm[g], t + 1)
                    halves = o[:].rearrange("p (n z) k -> p z n k", z=2)
                    for z in range(2):
                        nc.scalar.copy(halves[:, z], ps[:, 3 + 4 * z, 0:256].rearrange(
                            "p (n k) -> p n k", k=64)).then_inc(o_copied[z], 1)
                else:
                    for g in range(2):
                        act.wait_ge(o_mm[g], t + 1)
                        nc.scalar.copy(o[:, 4 * g:4 * g + 4, :].rearrange("p (n z) k -> p z n k", z=2),
                                       ps[:, 4 * g:4 * g + 2, 0:P].rearrange("p z (n k) -> p z n k", k=64)).then_inc(
                                           o_copied[g], 1)

            def front(t, u, sample):
                lora_inputs(t, u)
                rates(t)
                norm_roots(t)
                token_values(t, u)

            act.wait_ge(masks, MASKS)
            def tail(t, u):
                deviations(t)
                output(t)

            each_tile(act, front, solve, tail)

        @block.tensor
        def _(pe):
            def lora(t, u):
                pe.wait_ge(lora_in, t + 1)
                if not isinstance(t, int) or t > 1:
                    pe.wait_ge(o_mix, t - 1)
                for q in range(4):
                    nc.tensor.matmul(ps[:, 3, P * q:P * q + P], w2[0:64, P * q:P * q + P], low[0:64, u, 0, :],
                                     start=True, stop=True)
                for q in range(4):
                    mm = nc.tensor.matmul(ps[:, 7, P * q:P * q + P], w2[64:P, P * q:P * q + P], low[64:P, u, 0, :],
                                          start=True, stop=True)
                mm.then_inc(lora_out, 1)

            def norms(t):
                pe.wait_ge(kk_sq, t + 1)
                nc.tensor.matmul(ps[:, 3, :], pair1[:], t1[:], start=True, stop=True).then_inc(nrm, 1)

            def turns(t, u):
                pe.wait_ge(ch_ready, t + 1)
                for n in range(4):
                    if n >= 2:
                        pe.wait_ge(tr_copied, 4 * t + n - 1)
                    for q in range(4):
                        src = (beta[:, u, q, :], kap[:, u, q, :], kr[:, u, q, 0, :], sh[:, 8 + q, :])[n]
                        mm = nc.tensor.transpose(ps[:, (7, 3)[n % 2], P * q:P * q + P], src, ident[:])
                    mm.then_inc(tr, 1)

            def bonus_and_gate(t, u):
                for q in range(4):
                    nc.tensor.matmul(ps[:, 3, 2 * q:2 * q + 2], rk[:, u, P * q:P * q + P], hone[:], start=True,
                                     stop=True)
                nc.tensor.matmul(ps[:, 7, :], low[:, u, 1, :], g2[:], start=True, stop=True).then_inc(gate, 1)

            def turn_output(t):
                pe.wait_ge(o_fin, t + 1)
                for q in range(4):
                    mm = nc.tensor.transpose(ps[:, 3, P * q:P * q + P],
                                             o[:, 2 * q:2 * q + 2, :].rearrange("p h k -> p (h k)"), ident[:])
                mm.then_inc(o_tr, 1)

            def level(t, l, sample):
                for g in range(2):
                    pe.wait_ge(lev[g], levels_before(t) + l + 1)
                    pe.wait_ge(x_c[g], 6 * t + l)
                    for h in range(4):
                        mm = nc.tensor.matmul(ps[:, 4 * g, P * h:P * h + P], N[:, g, l % 2, h, :], X[:, g, h, :],
                                              start=True, stop=True)
                    mm.then_inc(nx[g], 1)
                for g in range(2):
                    pe.wait_ge(y_ready[g], 5 * t + l)
                    for h in range(4):
                        mm = nc.tensor.matmul(ps[:, 4 * g + 1, P * h:P * h + P], Y[:, g, h, :], XT[:, g, h, :],
                                              start=True, stop=True)
                    if l < last_level(sample):
                        for h in range(4):
                            mm = nc.tensor.matmul(ps[:, 4 * g + 2, P * h:P * h + P], XT[:, g, h, :], Y[:, g, h, :],
                                                  start=True, stop=True)
                    mm.then_inc(x_mm[g], 1)

            def solve(t, u, sample):
                pe.wait_ge(tr_copied, 4 * t + 4)
                for g in range(2):
                    if not first(t):
                        pe.wait_ge(o_copied[g], t)
                        pe.wait_ge(st_new[g], 2 * t)
                    for h in range(4):
                        q, hf = 2 * g + h // 2, slice(64 * (h % 2), 64 * (h % 2) + 64)
                        both = kr[hf, u, q, :, :].rearrange("p z t -> p (z t)")
                        nc.tensor.matmul(ps[:, 4 * g + h, 0:256], beta[hf, u, q, :], both, start=True, stop=True)
                        nc.tensor.matmul(ps[:, 4 * g + h, 256:512], kap[hf, u, q, :], both, start=True,
                                         stop=True).then_inc(gram[g], 1)
                for g in range(2):
                    pe.wait_ge(x0[g], t + 1)
                    for h in range(4):
                        mm = nc.tensor.transpose(ps[:, 4 * g + 1, P * h:P * h + P], XT[:, g, h, :], ident[:])
                    mm.then_inc(x_mm[g], 1)
                level(t, 1, sample)
                if not first(t):
                    bonus_and_gate(t - 1, 1 - u)
                level(t, 2, sample)
                if not first(t):
                    turn_output(t - 1)
                level(t, 3, sample)
                if not sample:
                    lora(t + 1, 1 - u)
                    level(t, 4, sample)
                    norms(t + 1)
                    level(t, 5, sample)
                top = last_level(sample)
                for g in range(2):
                    for h in range(4):
                        mm = nc.tensor.matmul(ps[:, 4 * g + 2, 64 * h:64 * h + 64], G[:, g, h, 2, :],
                                              vt[:, u, 4 * g + h, :], start=True, stop=True)
                    mm.then_inc(mv[g], 1)
                for g in range(2):
                    pe.wait_ge(x_c[g], 6 * t + top + 1)
                    pe.wait_ge(mv_c[g], t + 1)
                    for h in range(4):
                        mm = nc.tensor.matmul(ps[:, 4 * g, P * h:P * h + P], XT[:, g, h, :],
                                              kv[:, u, 4 * g + h, :, :].rearrange("p z k -> p (z k)"),
                                              start=True, stop=True)
                    mm.then_inc(pgd[g], 1)
                for g in range(2):
                    pe.wait_ge(pg_c[g], t + 1)
                    for h in range(4):
                        hh, n, hf = 4 * g + h, h // 2, slice(64 * (h % 2), 64 * (h % 2) + 64)
                        mm = nc.tensor.matmul(ps[hf, 4 * g + 2, P * n:P * n + P], pg[:, hh, 0, :], G[:, g, h, 1, :],
                                              start=True, stop=True)
                    if not sample:
                        for h in range(4):
                            hh, n, hf = 4 * g + h, h // 2, slice(64 * (h % 2), 64 * (h % 2) + 64)
                            for cc in range(2):
                                rows = slice(64 * cc, 64 * cc + 64)
                                a0, b0 = slice(64 * n, 64 * n + 64), slice(P + 64 * n, P + 64 * n + 64)
                                nc.tensor.matmul(ps[hf, 4 * g + cc, a0], pg[rows, hh, 0, :], bt[rows, u, hh, :],
                                                 start=True, stop=True)
                                nc.tensor.matmul(ps[hf, 4 * g + cc, b0], kt[rows, u, hh, :], vt[rows, u, hh, :],
                                                 start=True, stop=False)
                                mm = nc.tensor.matmul(ps[hf, 4 * g + cc, b0], bt[rows, u, hh, :],
                                                      pg[rows, hh, 1, :], start=False, stop=True)
                    mm.then_inc(qab[g], 1)
                if not sample:
                    turns(t + 1, 1 - u)
                if not sample:
                    for g in range(2):
                        pe.wait_ge(qab_used[g], t + 1)
                        pe.nop().then_inc(state_seen, 1)
                        for h in range(4):
                            n, hf = h // 2, slice(64 * (h % 2), 64 * (h % 2) + 64)
                            mm = nc.tensor.matmul(ps[hf, 4 * g + 2, 64 * n:64 * n + 64], AB[hf, g, 0, n, 0, :],
                                                  St[hf, 0, 2 * g + n, :], start=True, stop=True)
                        mm.then_inc(st_mm[g], 1)
                    for g in range(2):
                        pe.wait_ge(st_new[g], 2 * t + 1)
                        pe.nop().then_inc(state_seen, 1)
                        for h in range(4):
                            hh, n, hf = 4 * g + h, h // 2, slice(64 * (h % 2), 64 * (h % 2) + 64)
                            col = slice(64 * n, 64 * n + 64)
                            oc = ps[:, 4 * g + h % 2, col]
                            nc.tensor.matmul(oc, G[:, g, h, 3, :], vt[:, u, hh, :], start=True, stop=False)
                            nc.tensor.matmul(oc, G[:, g, h, 1, :], pg[:, hh, 1, :], start=False, stop=True)
                            for cc in range(2):
                                rows = slice(64 * cc, 64 * cc + 64)
                                mm = nc.tensor.matmul(ps[rows, 4 * g + h % 2, col], QT[hf, 2 * g + n, rows],
                                                      St[hf, cc, 2 * g + n, :], start=False, stop=True,
                                                      skip_group_check=True)
                        mm.then_inc(o_mm[g], 1)
                        for h in range(4):
                            n, hf = h // 2, slice(64 * (h % 2), 64 * (h % 2) + 64)
                            mm = nc.tensor.matmul(ps[hf, 4 * g + 2, P + 64 * n:P + 64 * n + 64],
                                                  AB[hf, g, 0, n, 1, :], St[hf, 1, 2 * g + n, :], start=True,
                                                  stop=True)
                        mm.then_inc(st_mm[g], 1)
                else:
                    for q in range(4):
                        g = q // 2
                        pe.wait_ge(qab_used[g], t + 1)
                        pe.wait_ge(exq, q + 1)
                        for hf in range(2):
                            hh = 2 * q + hf
                            h = hh % 4
                            rows = slice(64 * hf, 64 * hf + 64)
                            oc = ps[:, 3 + 4 * hf, 64 * q:64 * q + 64]
                            nc.tensor.matmul(oc, G[:, g, h, 3, :], vt[:, u, hh, :], start=True, stop=False)
                            nc.tensor.matmul(oc, G[:, g, h, 1, :], pg[:, hh, 1, :], start=False, stop=False)
                            for b in range(DB):
                                mm = nc.tensor.matmul(oc, Qs[rows, b, :], Ss[rows, q, b, :], start=False,
                                                      stop=b == DB - 1)
                            if h == 3:
                                mm.then_inc(o_mm[g], 1)
                            pe.wait_ge(exv, hh + 1)
                            b0, b1 = ps[rows, 4 * g, :], ps[rows, 4 * g + 1, :]
                            nc.tensor.matmul(b0, pg[:, hh, 0, :], flat(ex[:, 0]), start=True, stop=True)
                            nc.tensor.matmul(b1, kt[:, u, hh, :], flat(ex[:, 1]), start=True, stop=False)
                            nc.tensor.matmul(b1, bt[:, u, hh, :], flat(ex[:, 2]), start=False,
                                             stop=True).then_inc(ab_mm, 1)
                        pe.wait_ge(ab_used, q + 1)
                        for b in range(DB):
                            for hf in range(2):
                                rows = slice(64 * hf, 64 * hf + 64)
                                mm = nc.tensor.matmul(ps[rows, 4 * g + 2, 64 * b:64 * b + 64], ABs[rows, 0, b, :],
                                                      Ss[rows, q, b, :], start=True, stop=True)
                        mm.then_inc(st_mm[g], 1)
                        pe.wait_ge(st_new[g], 2 * PT + q % 2 + 1)

            def front(t, u, sample):
                lora(t, u)
                norms(t)
                turns(t, u)

            def tail(t, u):
                for g in range(2):
                    pe.wait_ge(o_copied[g], t + 1)
                bonus_and_gate(t, u)
                turn_output(t)

            pe.nop().then_inc(tr, 1)
            pe.wait_ge(cin, CONSTS)
            pe.wait_ge(masks, MASKS)
            each_tile(pe, front, solve, tail)
    return sems


FFN = 512
EXPERTS = 32
GROUPS4 = 4
PER_GROUP = EXPERTS // GROUPS4
MAX_BLOCKS = 2 * T // P + EXPERTS
SLOTS = MAX_BLOCKS * P
LOGITS = GROUPS4 + EXPERTS
MH = 4
MSCALE = 1.0 / 16.0


def mix_and_norm(nc, mixT, wq, wo, h1_d, io):
    with ExitStack() as c:
        def sb(name, shape, dt=F32):
            return c.enter_context(nc.sbuf_tensor(name, shape, dt))

        def sem(name):
            return c.enter_context(nc.semaphore(name))

        w = sb("w_out", [P, KT, D])
        g, b = sb("ln1_g", [P, D]), sb("ln1_b", [P, D])
        ms = sb("mix_tile", [P, 3, KT, P])
        x = sb("x_tile", [P, 3, D])
        r = sb("residual", [P, 3, D])
        st = sb("ln_stats", [P, 3, 16])
        bn = sb("bn_stats", [P, 2, 6])
        ps = c.enter_context(nc.psum_tensor("ps_mix", [P, 3, D], F32))
        cin, w_got, kv_got = sem("ln1_in"), sem("w_out_in"), sem("mem_kv_weights_in")
        x_got = [sem(f"x_tile_in_{u}") for u in range(3)]
        stored = [sem(f"h1_stored_{u}") for u in range(3)]
        staged, mm_done, ch, var, root = sem("mix_staged"), sem("mix_product"), sem("dve_chain3"), sem("ln1_var"), \
            sem("ln1_sqrt")
        normed, scaled, h_ready = sem("ln1_normed"), sem("ln1_scaled"), sem("h1_ready")
        aggr_begun, summed = sem("ln1_aggregation_begun"), sem("residual_summed")
        block = c.enter_context(nc.Block())

        @block.sync
        def _(sp):
            for u in range(3):
                sp.nop().then_inc(stored[u], 16)
            sp.dma_start(w[:], io["w_out"]).then_inc(w_got, 16)
            sp.dma_start(g[:], io["ln1_g"].broadcast_to([P, D])).then_inc(cin, 16)
            sp.dma_start(b[:], io["ln1_b"].broadcast_to([P, D])).then_inc(cin, 16)
            for u in range(3):
                sp.dma_start(x[:, u, :], io["x"][P * u:P * u + P, :]).then_inc(x_got[u], 16)
            sp.dma_start(wq[:], io["mem_wk"]).then_inc(kv_got, 16)
            sp.dma_start(wo[:], io["mem_wv"]).then_inc(kv_got, 16)
            with sp.Fori(0, 2) as i:
                for u in range(3):
                    sp.wait_ge(h_ready, 3 * i + u + 1)
                    sp.dma_start(h1_d[ds(3 * P * i + P * u, P), :], r[:, u, :]).then_inc(stored[u], 16)
                    sp.wait_ge(normed, 3 * i + u + 1)
                    sp.dma_start(x[:, u, :], io["x"][ds(3 * P * i + P * u + 3 * P, P), :]).then_inc(x_got[u], 16)
            for u in range(3):
                sp.wait_ge(h_ready, 6 + u + 1)
                sp.dma_start(h1_d[6 * P + P * u:7 * P + P * u, :], r[:, u, :]).then_inc(stored[u], 16)
            for u in range(3):
                sp.wait_ge(stored[u], 64)
            sp.wait_ge(kv_got, 32)

        @block.gpsimd
        def _(pool):
            def stage(i, u):
                nc.gpsimd.tensor_copy(ms[:, u, :, :], mixT[:, :, ds(3 * P * i + P * u, P)]).then_inc(staged, 1)

            def scale(i, u):
                pool.wait_ge(normed, 3 * i + u + 1)
                nc.gpsimd.tensor_tensor(r[:, u, :], r[:, u, :], g[:], ALU.mult).then_inc(scaled, 1)
                pool.wait_ge(scaled, 3 * i + u + 1)
                nc.gpsimd.tensor_tensor(r[:, u, :], r[:, u, :], b[:], ALU.add).then_inc(h_ready, 1)

            for u in range(3):
                stage(0, u)
            pool.wait_ge(cin, 32)
            with pool.Fori(0, 2) as i:
                for u in range(3):
                    pool.wait_ge(mm_done, 3 * i + u + 1)
                    stage(i + 1, u)
                    scale(i, u)
            for u in range(3):
                scale(2, u)

        @block.tensor
        def _(pe):
            pe.wait_ge(w_got, 16)
            with pe.Fori(0, 3) as i:
                for u in range(3):
                    pe.wait_ge(staged, 3 * i + u + 1)
                    pe.wait_ge(summed, 3 * i + u + 1)
                    for n in range(2):
                        for k in range(KT):
                            mm = nc.tensor.matmul(ps[:, u, HALF * n:HALF * n + HALF], ms[:, u, k, :],
                                                  w[:, k, HALF * n:HALF * n + HALF], start=k == 0, stop=k == KT - 1)
                    mm.then_inc(mm_done, 1)

        @block.scalar
        def _(act):
            with act.Fori(0, 3) as i:
                for u in range(3):
                    act.wait_ge(var, 3 * i + u + 1)
                    nc.scalar.activation(st[:, u, 3:4], st[:, u, 2:3], ACT.Sqrt).then_inc(root, 1)

        @block.vector
        def _(dve):
            dve.nop().then_inc(summed, 3)
            with dve.Fori(0, 3) as i:
                at = [0]

                def link(ins):
                    at[0] += 1
                    ins.then_inc(ch, 1)
                    dve.wait_ge(ch, 15 * i + at[0])

                for u in range(3):
                    dve.wait_ge(x_got[u], 16 * i + 16)
                    dve.wait_ge(mm_done, 3 * i + u + 1)
                    dve.wait_ge(stored[u], 16 * i + 16)
                    link(nc.vector.scalar_tensor_tensor(r[:, u, :], x[:, u, :], ALPHA, ps[:, u, :], ALU.mult, ALU.add))
                    dve.nop().then_inc(summed, 1)
                    for n in range(2):
                        ins = nc.vector.bn_stats(bn[:, n, :], r[:, u, HALF * n:HALF * n + HALF])
                    link(ins)
                    dve.nop().then_inc(aggr_begun, 1)
                    link(nc.vector.bn_aggr(st[:, u, 0:2], bn[:].rearrange("p n s -> p (n s)")))
                    link(nc.vector.tensor_scalar(st[:, u, 2:3], st[:, u, 1:2], LN_EPS, None, ALU.add))
                    dve.nop().then_inc(var, 1)
                    dve.wait_ge(root, 3 * i + u + 1)
                    link(nc.vector.reciprocal(st[:, u, 4:5], st[:, u, 3:4]))
                    nc.vector.tensor_scalar(r[:, u, :], r[:, u, :], st[:, u, 0:1], st[:, u, 4:5], ALU.subtract,
                                            ALU.mult).then_inc(normed, 1)


def memory_and_router(nc, ident, L, wq, wo, mixT, h1_d, h2_d, io):
    with ExitStack() as c:
        def sb(name, shape, dt=F32):
            return c.enter_context(nc.sbuf_tensor(name, shape, dt))

        def sem(name):
            return c.enter_context(nc.semaphore(name))

        BUFS, VBUFS = 4, 2
        mkT, mv = sb("mem_kT", [P, KT, N_MEM]), sb("mem_v", [P, 2, D])
        g, b = sb("ln2_g", [P, D]), sb("ln2_b", [P, D])
        wr = sb("w_router", [P, KT, LOGITS])
        h1 = sb("h1", [P, 2, D])
        hT, rT = sb("h1_T", [P, KT, P]), sb("h2_T", [P, KT, P])
        qT = sb("mem_qT", [P, KT, P + DS])
        S = sb("mem_probs", [P, 2 * D])
        PT_ = sb("mem_probs_T", [P, 16, P])
        oT = sb("mem_oT", [P, KT, P])
        r = sb("h2", [P, D])
        ck = mixT[:].rearrange("p k t -> p (k t)")[:, 0:BUFS * KT * N_MEM].rearrange(
            "p (s k m) -> p s k m", s=BUFS, k=KT)
        cv = sb("cache_mem_v", [P, VBUFS, 2, D])
        st = sb("mem_stats", [P, 4, 8])
        bn = sb("bn_stats2", [P, 2, 6])
        zero = sb("zero_row", [1, D])
        pT = c.enter_context(nc.psum_tensor("pT", [P, D], F32))
        pM = c.enter_context(nc.psum_tensor("pM", [P, D], F32))
        pS = c.enter_context(nc.psum_tensor("pS", [P, 2 * D], F32))

        kv_done, kv_copied, kv_out = sem("mem_product"), sem("mem_copied"), sem("mem_stored")
        kv_in, w_in_, wo_in = sem("mem_weights_in"), sem("attention_weights_in"), sem("wo_in")
        with nc.Block() as block:
            @block.sync
            def _(sp):
                for k in range(4):
                    sp.dma_start(S[:, 512 * k:512 * k + 512].rearrange("p (a t) -> p a t", a=2),
                                 io["memT"][:, 2 * k:2 * k + 2, :]).then_inc(kv_in, 16)
                sp.dma_start(g[:], io["ln2_g"].broadcast_to([P, D])).then_inc(w_in_, 16)
                sp.dma_start(b[:], io["ln2_b"].broadcast_to([P, D])).then_inc(w_in_, 16)
                sp.dma_start(wr[:, :, 0:GROUPS4], io["w_group"]).then_inc(w_in_, 16)
                sp.dma_start(wr[:, :, GROUPS4:LOGITS], io["w_expert"]).then_inc(w_in_, 16)
                sp.wait_ge(kv_done, 4)
                sp.dma_start(wq[:], io["mem_wq"]).then_inc(w_in_, 16)
                sp.wait_ge(kv_copied, 4)
                sp.dma_start(io["out_mem_k"], cv[:, 0, :, :]).then_inc(kv_out, 16)
                sp.wait_ge(kv_copied, 8)
                sp.dma_start(io["out_mem_v"], mv[:]).then_inc(kv_out, 16)
                sp.wait_ge(kv_done, 8)
                sp.dma_start(wo[:], io["mem_wo"]).then_inc(wo_in, 16)
                sp.wait_ge(kv_out, 32)
                sp.wait_ge(w_in_, 80)

            @block.tensor
            def _(pe):
                pe.wait_ge(kv_in, 64)
                mT = S[:].rearrange("p (k t) -> p k t", k=KT)
                for n in range(8):
                    wgt, m, h = (wq, wo)[n // 4], n // 2 % 2, n % 2
                    if n >= 2:
                        pe.wait_ge(kv_copied, n - 1)
                    for k in range(KT):
                        mm = nc.tensor.matmul(pM[:, HALF * (n % 2):HALF * (n % 2) + HALF], mT[:, k, P * m:P * m + P],
                                              wgt[:, k, HALF * h:HALF * h + HALF], start=k == 0, stop=k == KT - 1)
                    mm.then_inc(kv_done, 1)
                pe.wait_ge(kv_copied, 4)
                for n in range(4):
                    for j in range(4):
                        kt, m = (4 * n + j) // 2, j % 2
                        mm = nc.tensor.transpose(pS[:, HALF * n + P * j:HALF * n + P * j + P],
                                                 cv[:, 0, m, P * kt:P * kt + P], ident[:])
                    mm.then_inc(kv_done, 1)

            @block.scalar
            def _(act):
                for n in range(8):
                    m, h = n // 2 % 2, n % 2
                    act.wait_ge(kv_done, n + 1)
                    dst = (cv[:, 0, m, HALF * h:HALF * h + HALF], mv[:, m, HALF * h:HALF * h + HALF])[n // 4]
                    nc.scalar.copy(dst, pM[:, HALF * (n % 2):HALF * (n % 2) + HALF]).then_inc(kv_copied, 1)
                for n in range(4):
                    act.wait_ge(kv_done, 9 + n)
                    nc.scalar.copy(mkT[:, 2 * n:2 * n + 2, :].rearrange("p k t -> p (k t)"),
                                   pS[:, HALF * n:HALF * n + HALF]).then_inc(kv_copied, 1)
                act.wait_ge(kv_copied, 12)

        h_in = [sem("h1_in_even"), sem("h1_in_odd")]
        h_turned, hT_c, r_turned, rT_c = sem("h1_turned"), sem("h1_T_copied"), sem("h2_turned"), sem("h2_T_copied")
        q_mm, qT_c, h1_used = sem("q_product"), sem("qT_copied"), sem("h1_used")
        s_mm, s_max, s_exp, s_norm = sem("mem_scores"), sem("mem_max"), sem("mem_exp"), sem("mem_normed")
        p_turned, p_c, o_mm, o_c = sem("probs_turned"), sem("probs_T_copied"), sem("mem_o"), sem("mem_o_copied")
        y_mm, ch, var, root, h_out = sem("wo_product"), sem("dve_chain4"), sem("ln2_var"), sem("ln2_sqrt"), sem("h2_out")
        r_ready, lg_mm, lg_c, pad = sem("h2_ready"), sem("logits_ready"), sem("logits_copied"), sem("pads_zero")
        scaled, normed = sem("ln2_scaled"), sem("ln2_normed")
        aggr_begun = sem("ln2_aggregation_begun")
        k_in = [sem(f"cache_k_in_{n}") for n in range(BUFS)]
        v_in = [sem(f"cache_v_in_{n}") for n in range(VBUFS)]
        block = c.enter_context(nc.Block())
        VCH = 8

        def first(t):
            return isinstance(t, int) and t == 0

        def each_tile(eng, front, attend, router):
            front(0, 0)
            attend(0, 0, 0)
            with eng.Fori(0, (PT - 2) // 2) as i:
                attend(2 * i + 1, 1, 0)
                attend(2 * i + 2, 0, 0)
            attend(PT - 1, 1, 0)
            attend(PT, 0, 1)
            router(PT)

        @block.sync
        def _(sp):
            def load(t, u):
                sp.dma_start(h1[:, u, :], h1_d[ds(P * t, P), :]).then_inc(h_in[u], 16)

            def store(t):
                sp.wait_ge(r_ready, t + 1)
                sp.dma_start(h2_d[ds(P * t, P), :], r[:]).then_inc(h_out, 16)

            def attend(t, u, sample):
                if not first(t) and not sample:
                    sp.wait_ge(h1_used, t)
                    load(t + 1, 1 - u)
                if not first(t):
                    store(t - 1)
                if sample:
                    for s in range(BUFS, DB):
                        sp.wait_ge(s_mm, PT + s - BUFS + 1)
                        sp.dma_start(ck[:, s % BUFS, :, :], io["cache_mem_kT"][s]).then_inc(k_in[s % BUFS], 16)
                    for s in range(VBUFS, DB):
                        sp.wait_ge(o_mm, PT + s - VBUFS + 1)
                        sp.dma_start(cv[:, s % VBUFS, :, :], io["cache_mem_v"][s]).then_inc(v_in[s % VBUFS], 16)

            load(0, 0)
            load(1, 1)
            for n in range(BUFS):
                sp.dma_start(ck[:, n, :, :], io["cache_mem_kT"][n]).then_inc(k_in[n], 16)
            for n in range(VBUFS):
                sp.dma_start(cv[:, n, :, :], io["cache_mem_v"][n]).then_inc(v_in[n], 16)
            each_tile(sp, lambda t, u: None, attend, store)
            sp.wait_ge(pad, 2)
            sp.dma_start(h2_d[T:T + 1, :], zero[:]).then_inc(h_out, 16)
            sp.wait_ge(h_out, 16 * (NT + 1))

        @block.gpsimd
        def _(pool):
            nc.gpsimd.memset(qT[:, :, P:P + DS], 0.0).then_inc(pad, 1)
            nc.gpsimd.memset(zero[:], 0.0).then_inc(pad, 1)
            with pool.Fori(0, NT) as t:
                pool.wait_ge(normed, t + 1)
                nc.gpsimd.tensor_tensor(r[:], r[:], g[:], ALU.mult).then_inc(scaled, 1)
                pool.wait_ge(scaled, t + 1)
                nc.gpsimd.tensor_tensor(r[:], r[:], b[:], ALU.add).then_inc(r_ready, 1)

        @block.tensor
        def _(pe):
            def turn_h1(t, u):
                pe.wait_ge(h_in[u], 8 * (t - u) + 16)
                if not first(t):
                    if not isinstance(t, int) or t > 1:
                        pe.wait_ge(p_c, t - 1)
                for k in range(KT):
                    mm = nc.tensor.transpose(pT[:, P * k:P * k + P], h1[:, u, P * k:P * k + P], ident[:])
                mm.then_inc(h_turned, 1)

            def queries(t):
                pe.wait_ge(hT_c, t + 1)
                if not isinstance(t, int) or t > 1:
                    pe.wait_ge(lg_c, 1 + t - 2)
                for cb in range(KT):
                    for k in range(KT):
                        mm = nc.tensor.matmul(pS[:, D + P * cb:D + P * cb + P], wq[:, k, P * cb:P * cb + P],
                                              hT[:, k, :], start=k == 0, stop=k == KT - 1)
                mm.then_inc(q_mm, 1)

            def turn_h2(t):
                pe.wait_ge(r_ready, t + 1)
                for k in range(KT):
                    mm = nc.tensor.transpose(pM[:, P * k:P * k + P], r[:, P * k:P * k + P], ident[:])
                mm.then_inc(r_turned, 1)

            def logits(t):
                pe.wait_ge(rT_c, t + 1)
                for k in range(KT):
                    mm = nc.tensor.matmul(pS[:, D:D + LOGITS], rT[:, k, :], wr[:, k, :], start=k == 0,
                                          stop=k == KT - 1)
                mm.then_inc(lg_mm, 1)

            def front(t, u):
                turn_h1(t, u)
                queries(t)

            def attend(t, u, sample):
                pe.wait_ge(qT_c, t + 1)
                if not first(t):
                    pe.wait_ge(h1_used, t)
                if not sample:
                    for h in range(MH):
                        for k in range(2):
                            mm = nc.tensor.matmul(pS[:, N_MEM * h:N_MEM * h + N_MEM], qT[:, 2 * h + k, 0:P],
                                                  mkT[:, 2 * h + k, :], start=k == 0, stop=k == 1)
                    mm.then_inc(s_mm, 1)
                    turn_h1(t + 1, 1 - u)
                    queries(t + 1)
                else:
                    pe.wait_ge(pad, 1)
                    pe.wait_ge(lg_c, 1 + t - 1)
                    for s in range(DB):
                        pe.wait_ge(k_in[s % BUFS], 16 * (s // BUFS) + 16)
                        for h in range(MH):
                            for k in range(2):
                                mm = nc.tensor.matmul(pS[32 * h:32 * h + 32, N_MEM * s:N_MEM * s + N_MEM],
                                                      qT[:, 2 * h + k, DS * s:DS * s + 32],
                                                      ck[:, s % BUFS, 2 * h + k, :], start=k == 0, stop=k == 1)
                        mm.then_inc(s_mm, 1)
                if not first(t):
                    turn_h2(t - 1)
                pe.wait_ge(s_norm, t + 1)
                if not sample:
                    pe.wait_ge(hT_c, t + 2)
                for n in range(2 if sample else 1):
                    if n:
                        pe.wait_ge(p_c, t + 1)
                    for j in range(8):
                        mm = nc.tensor.transpose(pT[:, P * j:P * j + P], S[:, P * (8 * n + j):P * (8 * n + j) + P],
                                                 ident[:])
                    mm.then_inc(p_turned, 1)
                if not first(t):
                    if not sample:
                        pe.wait_ge(qT_c, t + 2)
                    logits(t - 1)
                pe.wait_ge(p_c, t + 2 if sample else t + 1)
                if not sample:
                    for cb in range(KT):
                        for k in range(2):
                            mm = nc.tensor.matmul(pM[:, P * cb:P * cb + P], mv[:, k, P * cb:P * cb + P],
                                                  PT_[:, 2 * (cb // 2) + k, :], start=k == 0, stop=k == 1)
                    mm.then_inc(o_mm, 1)
                else:
                    for s in range(DB):
                        pe.wait_ge(v_in[s % VBUFS], 16 * (s // VBUFS) + 16)
                        for cb in range(KT):
                            for k in range(2):
                                mm = nc.tensor.matmul(pM[:, P * cb + DS * s:P * cb + DS * s + DS],
                                                      cv[:, s % VBUFS, k, P * cb:P * cb + P],
                                                      PT_[:, 2 * s + k, 32 * (cb // 2):32 * (cb // 2) + DS],
                                                      start=k == 0, stop=k == 1)
                        mm.then_inc(o_mm, 1)
                pe.wait_ge(o_c, t + 1)
                if first(t):
                    pe.wait_ge(wo_in, 16)
                for n in range(2):
                    for k in range(KT):
                        mm = nc.tensor.matmul(pS[:, HALF * n:HALF * n + HALF], oT[:, k, :],
                                              wo[:, k, HALF * n:HALF * n + HALF], start=k == 0, stop=k == KT - 1)
                mm.then_inc(y_mm, 1)

            def router(t):
                turn_h2(t)
                pe.wait_ge(lg_c, 1 + t)
                logits(t)

            each_tile(pe, front, attend, router)

        @block.scalar
        def _(act):
            def copy_T(dst, src):
                for n in range(2):
                    ins = nc.scalar.copy(dst[:, 4 * n:4 * n + 4, 0:P],
                                         src[:, HALF * n:HALF * n + HALF].rearrange("p (k t) -> p k t", k=4))
                return ins

            def turned_h1(t):
                act.wait_ge(h_turned, t + 1)
                copy_T(hT, pT).then_inc(hT_c, 1)

            def queries(t):
                act.wait_ge(q_mm, t + 1)
                copy_T(qT, pS[:, D:2 * D]).then_inc(qT_c, 1)

            def turned_h2(t):
                act.wait_ge(r_turned, t + 1)
                copy_T(rT, pM).then_inc(rT_c, 1)

            def front(t, u):
                turned_h1(t)
                queries(t)

            def attend(t, u, sample):
                parts = DB if sample else MH
                if not sample:
                    turned_h1(t + 1)
                act.wait_ge(s_max, t + 1)
                for h in range(parts):
                    ins = nc.scalar.activation(S[:, N_MEM * h:N_MEM * h + N_MEM], pS[:, N_MEM * h:N_MEM * h + N_MEM],
                                               ACT.Exp, bias=st[:, 1, h:h + 1], scale=MSCALE,
                                               accum_out=st[:, 2, h:h + 1])
                ins.then_inc(s_exp, 1)
                if not sample:
                    queries(t + 1)
                if not first(t):
                    turned_h2(t - 1)
                for n in range(2 if sample else 1):
                    act.wait_ge(p_turned, t + n + 1)
                    copy_T(PT_[:, 8 * n:8 * n + 8, :], pT).then_inc(p_c, 1)
                act.wait_ge(var, t + 1)
                nc.scalar.activation(st[:, 3, 3:4], st[:, 3, 2:3], ACT.Sqrt).then_inc(root, 1)

            each_tile(act, front, attend, turned_h2)

        @block.vector
        def _(dve):
            def router(t):
                dve.wait_ge(lg_mm, t + 1)
                dst = L[:, ds(t, 1), :].rearrange("p o e -> p (o e)")
                nc.vector.tensor_copy(dst, pS[:, D:D + LOGITS]).then_inc(lg_c, 1)

            def attend(t, u, sample):
                at = [0]

                def link(ins):
                    at[0] += 1
                    ins.then_inc(ch, 1)
                    dve.wait_ge(ch, VCH * t + at[0])

                parts = DB if sample else MH
                w = N_MEM * parts
                dve.wait_ge(s_mm, t + parts if sample else t + 1)
                link(nc.vector.tensor_reduce(st[:, 0, 0:parts], pS[:, 0:w].rearrange("p (h m) -> p h m", m=N_MEM),
                                             AX.X, ALU.max))
                link(nc.vector.tensor_scalar(st[:, 1, 0:parts], st[:, 0, 0:parts], -MSCALE, None, ALU.mult))
                dve.nop().then_inc(s_max, 1)
                dve.wait_ge(s_exp, t + 1)
                link(nc.vector.reciprocal(st[:, 0, 0:parts], st[:, 2, 0:parts]))
                for h in range(parts):
                    ins = nc.vector.tensor_scalar(S[:, N_MEM * h:N_MEM * h + N_MEM], S[:, N_MEM * h:N_MEM * h + N_MEM],
                                                  st[:, 0, h:h + 1], None, ALU.mult)
                ins.then_inc(s_norm, 1)
                if not first(t):
                    router(t - 1)
                dve.wait_ge(o_mm, t + DB if sample else t + 1)
                nc.vector.tensor_copy(oT[:].rearrange("p k t -> p (k t)"), pM[:]).then_inc(o_c, 1)
                dve.wait_ge(y_mm, t + 1)
                if not first(t):
                    dve.wait_ge(h_out, 16 * t)
                link(nc.vector.scalar_tensor_tensor(r[:], h1[:, u, :], ALPHA, pS[:, 0:D], ALU.mult, ALU.add))
                dve.nop().then_inc(h1_used, 1)
                for n in range(2):
                    ins = nc.vector.bn_stats(bn[:, n, :], r[:, HALF * n:HALF * n + HALF])
                link(ins)
                dve.nop().then_inc(aggr_begun, 1)
                link(nc.vector.bn_aggr(st[:, 3, 0:2], bn[:].rearrange("p n s -> p (n s)")))
                link(nc.vector.tensor_scalar(st[:, 3, 2:3], st[:, 3, 1:2], LN_EPS, None, ALU.add))
                dve.nop().then_inc(var, 1)
                dve.wait_ge(root, t + 1)
                link(nc.vector.reciprocal(st[:, 3, 4:5], st[:, 3, 3:4]))
                nc.vector.tensor_scalar(r[:], r[:], st[:, 3, 0:1], st[:, 3, 4:5], ALU.subtract,
                                        ALU.mult).then_inc(normed, 1)
                assert at[0] == VCH

            dve.nop().then_inc(lg_c, 1)
            each_tile(dve, lambda t, u: None, attend, router)


def route(nc, L, rt, pool_dmas, io):
    with ExitStack() as c:
        def sb(name, shape, dt=F32):
            return c.enter_context(nc.sbuf_tensor(name, shape, dt))

        def sem(name):
            return c.enter_context(nc.semaphore(name))

        bias = sb("router_bias", [P, LOGITS])
        gl, eg = sb("group_logits", [P, NT, 4]), sb("group_hot", [P, NT, 4])
        gt, io4 = sb("group_tmp", [P, NT, 4]), sb("iota_4", [P, 4])
        el, tmp, pos = sb("expert_logits", [P, NT, EXPERTS]), sb("expert_tmp", [P, NT, EXPERTS]), sb(
            "positions", [P, NT, EXPERTS])
        oh = sb("expert_hot", [P, 2, NT, EXPERTS])
        both = sb("both_hot", [P, NT, EXPERTS])
        io32, ioi = sb("iota_32", [P, EXPERTS]), sb("iota_int", [P, MAX_BLOCKS + 2], I32)
        s = sb("route_scalars", [P, 10, NT])
        m2 = sb("slots_float", [P, 2, NT])
        upper, ones = sb("strict_upper", [P, P]), sb("all_ones", [P, P])
        cnt, cnti = sb("expert_counts", [P, 6, EXPERTS]), sb("expert_counts_int", [P, EXPERTS], I32)
        cmp_ = sb("block_compare", [P, MAX_BLOCKS + 2, EXPERTS])
        iob, be = sb("iota_blocks", [P, MAX_BLOCKS + 2]), sb("block_expert_float", [P, MAX_BLOCKS + 2])
        tok = sb("token_numbers", [P, NT], I32)
        pair = sb("slot_values", [P, 2, NT, 3], I32)
        fill = sb("empty_rows", [P, MAX_BLOCKS + 2, 3], I32)
        pr = c.enter_context(nc.psum_tensor("ps_rank", [P, HALF], F32))
        pc = c.enter_context(nc.psum_tensor("ps_count", [P, HALF], F32))
        b_in, io_done, ch, ex_in, ex = sem("router_bias_in"), sem("iotas"), sem("dve_chain5"), sem("exp_args"), sem("exps")
        hots, ranks, out, filled = sem("choices_ready"), sem("ranks_ready"), sem("slots_ready"), sem("slots_cleared")
        scat = pool_dmas["slots_scattered"]
        fills = sem("fill_made")
        block = c.enter_context(nc.Block())
        W = MAX_BLOCKS + 2

        @block.sync
        def _(sp):
            sp.dma_start(bias[:, 0:4], io["b_group"].broadcast_to([P, 4])).then_inc(b_in, 16)
            sp.dma_start(bias[:, 4:LOGITS], io["b_expert"].broadcast_to([P, EXPERTS])).then_inc(b_in, 16)
            sp.wait_ge(fills, 3)
            sp.dma_start(io["slots"].rearrange("(b p) z -> p b z", p=P), fill[:]).then_inc(filled, 16)
            sp.wait_ge(filled, 16)

        @block.gpsimd
        def _(pool):
            nc.gpsimd.iota(ioi[:], pattern=[[1, W]], base=0, channel_multiplier=0).then_inc(io_done, 1)
            nc.gpsimd.iota(tok[:], pattern=[[P, NT]], base=0, channel_multiplier=1).then_inc(io_done, 1)
            nc.gpsimd.memset(upper[:], 1.0).then_inc(io_done, 1)
            nc.gpsimd.memset(ones[:], 1.0).then_inc(io_done, 1)
            pool.wait_ge(io_done, 4)
            nc.gpsimd.affine_select(out=upper[:], in_=upper[:], compare_op=ALU.is_ge, fill=0.0, base=-1,
                                    pattern=[[1, P]], channel_multiplier=-1).then_inc(io_done, 1)
            nc.gpsimd.memset(fill[:, :, 0:1], T).then_inc(fills, 1)
            nc.gpsimd.memset(fill[:, :, 1:2], 0).then_inc(fills, 1)
            nc.gpsimd.iota(fill[:, :, 2], pattern=[[P, W]], base=2 * T, channel_multiplier=1).then_inc(fills, 1)
            pool.wait_ge(filled, 16)
            pool.wait_ge(out, 1)
            for t in range(NT):
                for z in range(2):
                    nc.gpsimd.indirect_dma_start(
                        out=io["slots"], out_offset=bass.IndirectOffsetOnAxis(ap=rt["slot"][:, z, t:t + 1], axis=0),
                        in_=pair[:, z, t, :], in_offset=None).then_inc(scat, 16)
            pool.wait_ge(scat, 16 * 2 * NT)

        @block.tensor
        def _(pe):
            pe.wait_ge(io_done, 5)
            pe.wait_ge(hots, 1)
            flat = both[:].rearrange("p t e -> p (t e)")
            nc.tensor.matmul(pr[:, 0:NT * EXPERTS], upper[:], flat, start=True, stop=True)
            nc.tensor.matmul(pc[:, 0:NT * EXPERTS], ones[:], flat, start=True, stop=True).then_inc(ranks, 1)

        @block.scalar
        def _(act):
            act.wait_ge(ex_in, 1)
            nc.scalar.activation(gt[:], gt[:], ACT.Exp)
            nc.scalar.activation(s[:, 5, :], s[:, 5, :], ACT.Exp).then_inc(ex, 1)

        @block.vector
        def _(dve):
            n = [0]

            def link(ins):
                n[0] += 1
                ins.then_inc(ch, 1)
                dve.wait_ge(ch, n[0])

            V = nc.vector

            def across(vec, k):
                return vec.rearrange("p (t o) -> p t o", o=1).broadcast_to([P, NT, k])

            def over(row, k):
                return row.rearrange("p (o k) -> p o k", o=1).broadcast_to([P, NT, k])

            def first_of_max(x, hot, scratch, io_row, k, mx, idx):
                link(V.tensor_reduce(mx, x, AX.X, ALU.max))
                link(V.tensor_tensor(hot, x, across(mx, k), ALU.is_equal))
                link(V.tensor_scalar(hot, hot, -1.0, -1000.0, ALU.add, ALU.mult))
                link(V.tensor_tensor(scratch, hot, over(io_row, k), ALU.add))
                link(V.tensor_reduce(idx, scratch, AX.X, ALU.min))
                link(V.tensor_tensor(hot, over(io_row, k), across(idx, k), ALU.is_equal))

            dve.wait_ge(b_in, 32)
            dve.wait_ge(io_done, 4)
            link(V.tensor_copy(iob[:], ioi[:]))
            link(V.tensor_copy(io4[:], iob[:, 0:4]))
            link(V.tensor_copy(io32[:], iob[:, 0:EXPERTS]))
            link(V.tensor_tensor(gl[:], L[:, :, 0:4], over(bias[:, 0:4], 4), ALU.add))
            link(V.tensor_tensor(el[:], L[:, :, 4:LOGITS], over(bias[:, 4:LOGITS], EXPERTS), ALU.add))
            first_of_max(gl[:], eg[:], gt[:], io4[:], 4, s[:, 0, :], s[:, 1, :])
            link(V.tensor_tensor(gt[:], gl[:], across(s[:, 0, :], 4), ALU.subtract))
            hot8 = eg[:].rearrange("p t (g o) -> p (t g) o", o=1).broadcast_to([P, NT * 4, PER_GROUP])
            e8 = lambda a: a.rearrange("p t (g e) -> p (t g) e", g=4)
            link(V.tensor_tensor(e8(tmp[:]), e8(el[:]), hot8, ALU.mult))
            link(V.tensor_scalar(eg[:], eg[:], -1.0, -NEG, ALU.add, ALU.mult))
            link(V.tensor_tensor(e8(el[:]), e8(tmp[:]), hot8, ALU.add))
            first_of_max(el[:], oh[:, 0], tmp[:], io32[:], EXPERTS, s[:, 2, :], s[:, 3, :])
            link(V.tensor_scalar(tmp[:], oh[:, 0], 3 * NEG, None, ALU.mult))
            link(V.tensor_tensor(el[:], el[:], tmp[:], ALU.add))
            first_of_max(el[:], oh[:, 1], tmp[:], io32[:], EXPERTS, s[:, 4, :], s[:, 3, :])
            link(V.tensor_tensor(s[:, 5, :], s[:, 4, :], s[:, 2, :], ALU.subtract))
            dve.nop().then_inc(ex_in, 1)
            link(V.tensor_tensor(both[:], oh[:, 0], oh[:, 1], ALU.add))
            dve.nop().then_inc(hots, 1)
            dve.wait_ge(ex, 1)
            link(V.tensor_reduce(s[:, 6, :], gt[:], AX.X, ALU.add))
            link(V.tensor_scalar(s[:, 7, :], s[:, 5, :], 1.0, None, ALU.add))
            link(V.tensor_tensor(s[:, 6, :], s[:, 6, :], s[:, 7, :], ALU.mult))
            link(V.reciprocal(s[:, 8, :], s[:, 6, :]))
            link(V.tensor_tensor(s[:, 9, :], s[:, 8, :], s[:, 5, :], ALU.mult))
            dve.wait_ge(ranks, 1)
            link(V.tensor_copy(pos[:].rearrange("p t e -> p (t e)"), pr[:, 0:NT * EXPERTS]))
            link(V.tensor_copy(cnt[:, 0, :], pc[:, 0:EXPERTS]))
            for t in range(1, NT):
                link(V.tensor_tensor(pos[:, t, :], pos[:, t, :], cnt[:, 0, :], ALU.add))
                link(V.tensor_tensor(cnt[:, 0, :], cnt[:, 0, :], pc[:, EXPERTS * t:EXPERTS * t + EXPERTS], ALU.add))
            link(V.tensor_scalar(cnt[:, 1, :], cnt[:, 0, :], float(P - 1), None, ALU.add))
            link(V.tensor_copy(cnti[:], cnt[:, 1, :]))
            link(V.tensor_scalar(cnti[:], cnti[:], 7, None, ALU.arith_shift_right))
            link(V.tensor_copy(cnt[:, 1, :], cnti[:]))
            link(V.memset(cnt[:, 2, :], 1.0))
            link(V.tensor_tensor_scan(cnt[:, 3, :], cnt[:, 2, :], cnt[:, 1, :], 0.0, ALU.mult, ALU.add))
            link(V.tensor_tensor(cnt[:, 4, :], cnt[:, 3, :], cnt[:, 1, :], ALU.subtract))
            link(V.tensor_scalar(cnt[:, 4, :], cnt[:, 4, :], float(P), None, ALU.mult))
            link(V.tensor_tensor(pos[:], pos[:], over(cnt[:, 4, :], EXPERTS), ALU.add))
            for z in range(2):
                link(V.tensor_tensor(tmp[:], pos[:], oh[:, z], ALU.mult))
                link(V.tensor_reduce(m2[:, z, :], tmp[:], AX.X, ALU.add))
                link(V.tensor_copy(pair[:, z, :, 0], tok[:]))
                link(V.tensor_copy(pair[:, z, :, 1].bitcast(F32), s[:, 8 + z, :]))
                link(V.tensor_scalar(pair[:, z, :, 2], tok[:], 2, z, ALU.mult, ALU.add))
            link(V.tensor_copy(rt["slot"][:], m2[:]))
            dve.nop().then_inc(out, 1)
            wide = lambda a: a.rearrange("p (b o) -> p b o", o=1).broadcast_to([P, W, EXPERTS])
            link(V.tensor_tensor(cmp_[:], wide(iob[:]),
                                 cnt[:, 3, :].rearrange("p (o e) -> p o e", o=1).broadcast_to([P, W, EXPERTS]),
                                 ALU.is_ge))
            link(V.tensor_reduce(be[:], cmp_[:], AX.X, ALU.add))
            link(V.tensor_scalar(be[:], be[:], float(EXPERTS - 1), None, ALU.min))
            link(V.tensor_copy(rt["block_expert"][:], be[:]))
            link(V.tensor_scalar(cnt[:, 5, 0:1], cnt[:, 3, EXPERTS - 1:EXPERTS], 1.0, None, ALU.add))
            link(V.tensor_copy(rt["pairs"][:], cnt[:, 5, 0:1]))
            link(V.tensor_scalar(rt["pairs"][:], rt["pairs"][:], 1, None, ALU.arith_shift_right))


def experts(nc, ident, rt, pool_dmas, h2_d, y_d, io):
    with ExitStack() as c:
        def sb(name, shape, dt=F32):
            return c.enter_context(nc.sbuf_tensor(name, shape, dt))

        def sem(name):
            return c.enter_context(nc.semaphore(name))

        w1, w3, w2 = sb("w1", [P, 2, KT, FFN]), sb("w3", [P, 2, KT, FFN]), sb("w2", [P, 2, FFN // P, D])
        table = sb("slot_table", [P, MAX_BLOCKS + 2, 3], I32)
        tk, gt = sb("slots_to_gather", [P, 2, 3], I32), sb("slots_to_scatter", [P, 2, 3], I32)
        xg = sb("gathered", [P, 2, D])
        xT = sb("gathered_T", [P, 2, KT, P])
        sg, hT = sb("sigmoid", [P, 2, FFN]), sb("hidden_T", [P, 2, FFN // P, P])
        y = sb("expert_out", [P, 2, D])
        pT = c.enter_context(nc.psum_tensor("pT2", [P, 2, HALF], F32))
        pH = c.enter_context(nc.psum_tensor("pH", [P, 2, 2, HALF], F32))
        pY = c.enter_context(nc.psum_tensor("pY", [P, 2, HALF], F32))
        w13_in = [sem(f"w1_w3_in_{u}") for u in range(2)]
        w2_in = [sem(f"w2_in_{u}") for u in range(2)]
        table_in, tk_ready, gt_ready = sem("table_in"), sem("tokens_ready"), sem("gates_ready")
        xg_in = [pool_dmas[f"rows_in_{u}"] for u in range(2)]
        y_out = [pool_dmas[f"outputs_scattered_{u}"] for u in range(2)]
        turned, xT_c, h_mm, sig, hid, y_mm, y_c, ch = (sem(n) for n in (
            "rows_turned", "rows_T_copied", "hidden_product", "sigmoid_ready", "hidden_ready", "out_product",
            "out_gated", "hidden_chain"))
        gather_begun, y_free = sem("gather_begun_moe"), sem("outputs_stored")
        block = c.enter_context(nc.Block())

        def passes(eng):
            return eng.value_load(rt["pairs"][0:1, 0:1], min_val=1, max_val=(MAX_BLOCKS + 1) // 2)

        @block.sync
        def _(sp):
            sp.dma_start(table[:], io["slots"].rearrange("(b p) z -> p b z", p=P)).then_inc(table_in, 16)
            with sp.Fori(0, passes(sp)) as i:
                e = [sp.value_load(rt["block_expert"][0:1, ds(2 * i + u, 1)], min_val=0, max_val=EXPERTS - 1)
                     for u in range(2)]
                for u in range(2):
                    sp.wait_ge(h_mm, 2 * i + u + 1)
                    sp.dma_start(w1[:, u, :, :].rearrange("p k (o n) -> p o k n", o=1),
                                 io["moe_w1"][:, ds(e[u], 1), :, :]).then_inc(w13_in[u], 16)
                    sp.dma_start(w3[:, u, :, :].rearrange("p k (o n) -> p o k n", o=1),
                                 io["moe_w3"][:, ds(e[u], 1), :, :]).then_inc(w13_in[u], 16)
                for u in range(2):
                    sp.wait_ge(y_mm, 4 * i + 2 * u + 2)
                    sp.dma_start(w2[:, u, :, :].rearrange("p k (o n) -> p o k n", o=1),
                                 io["moe_w2"][:, ds(e[u], 1), :, :]).then_inc(w2_in[u], 16)

        @block.gpsimd
        def _(pool):
            def gather(i, u):
                nc.gpsimd.tensor_copy(tk[:, u, :], table[:, ds(2 * i + u, 1), :].rearrange(
                    "p o z -> p (o z)")).then_inc(tk_ready, 1)
                pool.wait_ge(tk_ready, 2 * i + u + 1)
                pool.nop().then_inc(gather_begun, 1)
                nc.gpsimd.indirect_dma_start(
                    out=xg[:, u, :], out_offset=None, in_=h2_d,
                    in_offset=bass.IndirectOffsetOnAxis(ap=tk[:, u, 0:1], axis=0)).then_inc(xg_in[u], 16)

            pool.nop().then_inc(y_free, 1)
            pool.wait_ge(table_in, 16)
            gather(0, 0)
            gather(0, 1)
            n = passes(pool)
            with pool.Fori(0, n) as i:
                for u in range(2):
                    pool.wait_ge(turned, 1 + 4 * i + 2 * u + 2)
                    pool.nop().then_inc(gather_begun, 1)
                    gather(i + 1, u)
                for u in range(2):
                    nc.gpsimd.tensor_copy(gt[:, u, :], table[:, ds(2 * i + u, 1), :].rearrange(
                        "p o z -> p (o z)")).then_inc(gt_ready, 1)
                for u in range(2):
                    pool.wait_ge(y_c, 2 + 4 * i + 2 * u + 2)
                    pool.nop().then_inc(gather_begun, 1)
                    nc.gpsimd.indirect_dma_start(
                        out=y_d, out_offset=bass.IndirectOffsetOnAxis(ap=gt[:, u, 2:3], axis=0),
                        in_=y[:, u, :], in_offset=None).then_inc(y_out[u], 16)
                for u in range(2):
                    pool.wait_ge(y_out[u], 16 * i + 16)
                    pool.nop().then_inc(y_free, 1)
            for u in range(2):
                pool.wait_ge(xg_in[u], 16 * n + 16)
                pool.nop().then_inc(gather_begun, 1)

        @block.tensor
        def _(pe):
            def turn(i, u, z):
                pe.wait_ge(xg_in[u], 16 * i + 16)
                pe.wait_ge(xT_c, 4 * i + 2 * u + z + 1)
                for k in range(4):
                    c0 = P * (4 * z + k)
                    mm = nc.tensor.transpose(pT[:, z, P * k:P * k + P], xg[:, u, c0:c0 + P], ident[:])
                mm.then_inc(turned, 1)

            def hidden(i, u):
                pe.wait_ge(xT_c, 2 + 4 * i + 2 * u + 2)
                pe.wait_ge(w13_in[u], 32 * i + 32)
                pe.wait_ge(hid, 1 + 2 * i)
                for z, w in enumerate((w1, w3)):
                    for n in range(FFN // P):
                        for k in range(KT):
                            mm = nc.tensor.matmul(pH[:, u, z, P * n:P * n + P], w[:, u, k, P * n:P * n + P],
                                                  xT[:, u, k, :], start=k == 0, stop=k == KT - 1)
                mm.then_inc(h_mm, 1)

            def output(i, u, z):
                pe.wait_ge(hid, 1 + 2 * i + u + 1)
                pe.wait_ge(w2_in[u], 16 * i + 16)
                pe.wait_ge(y_c, 4 * i + 2 * u + z + 1)
                for k in range(4):
                    mm = nc.tensor.matmul(pY[:, z, :], hT[:, u, k, :], w2[:, u, k, HALF * z:HALF * z + HALF],
                                          start=k == 0, stop=k == 3)
                mm.then_inc(y_mm, 1)

            pe.nop().then_inc(h_mm, 2)
            pe.nop().then_inc(y_mm, 4)
            pe.nop().then_inc(turned, 1)
            for u in range(2):
                for z in range(2):
                    turn(0, u, z)
            with pe.Fori(0, passes(pe)) as i:
                hidden(i, 0)
                hidden(i, 1)
                for u in range(2):
                    turn(i + 1, u, 0)
                    output(i, u, 0)
                    turn(i + 1, u, 1)
                    output(i, u, 1)

        @block.scalar
        def _(act):
            def rows(i, u, z):
                act.wait_ge(turned, 1 + 4 * i + 2 * u + z + 1)
                nc.scalar.copy(xT[:, u, 4 * z:4 * z + 4, :].rearrange("p k t -> p (k t)"),
                               pT[:, z, :]).then_inc(xT_c, 1)

            act.nop().then_inc(xT_c, 2)
            for u in range(2):
                for z in range(2):
                    rows(0, u, z)
            with act.Fori(0, passes(act)) as i:
                for u in range(2):
                    act.wait_ge(h_mm, 2 + 2 * i + u + 1)
                    nc.scalar.activation(sg[:, u, :], pH[:, u, 0, :], ACT.Sigmoid).then_inc(sig, 1)
                for u in range(2):
                    for z in range(2):
                        rows(i + 1, u, z)

        @block.vector
        def _(dve):
            dve.nop().then_inc(hid, 1)
            dve.nop().then_inc(y_c, 2)
            with dve.Fori(0, passes(dve)) as i:
                for u in range(2):
                    dve.wait_ge(sig, 2 * i + u + 1)
                    nc.vector.tensor_tensor(sg[:, u, :], sg[:, u, :], pH[:, u, 0, :], ALU.mult).then_inc(ch, 1)
                    dve.wait_ge(ch, 2 * i + u + 1)
                    nc.vector.tensor_tensor(hT[:, u].rearrange("p k t -> p (k t)"), sg[:, u, :], pH[:, u, 1, :],
                                            ALU.mult).then_inc(hid, 1)
                for u in range(2):
                    dve.wait_ge(gt_ready, 2 * i + u + 1)
                    dve.wait_ge(y_free, 1 + 2 * i)
                    for z in range(2):
                        dve.wait_ge(y_mm, 4 + 4 * i + 2 * u + z + 1)
                        nc.vector.tensor_scalar(y[:, u, HALF * z:HALF * z + HALF], pY[:, z, :],
                                                gt[:, u, 1:2].bitcast(F32), None, ALU.mult).then_inc(y_c, 1)


def combine(nc, h2_d, y_d, io):
    with ExitStack() as c:
        def sb(name, shape, dt=F32):
            return c.enter_context(nc.sbuf_tensor(name, shape, dt))

        def sem(name):
            return c.enter_context(nc.semaphore(name))

        g, b = sb("ln3_g", [P, D]), sb("ln3_b", [P, D])
        h, r = sb("h2_rows", [P, 3, D]), sb("out_rows", [P, 3, D])
        ya = sb("expert_rows", [P, 3, 2, D])
        st, bn = sb("ln3_stats", [P, 3, 16]), sb("bn_stats3", [P, 2, 6])
        cin = sem("ln3_in")
        h_in = [sem(f"h2_in_{u}") for u in range(3)]
        y_in = [sem(f"expert_rows_in_{u}") for u in range(3)]
        stored = [sem(f"y_stored_{u}") for u in range(3)]
        ch, var, root, normed, scaled, ready = (sem(n) for n in (
            "dve_chain6", "ln3_var", "ln3_sqrt", "ln3_normed", "ln3_scaled", "y_ready"))
        aggr_begun = sem("ln3_aggregation_begun")
        block = c.enter_context(nc.Block())

        @block.sync
        def _(sp):
            for u in range(3):
                sp.nop().then_inc(stored[u], 16)
            sp.dma_start(g[:], io["ln3_g"].broadcast_to([P, D])).then_inc(cin, 16)
            sp.dma_start(b[:], io["ln3_b"].broadcast_to([P, D])).then_inc(cin, 16)
            with sp.Fori(0, 3) as i:
                for u in range(3):
                    sp.wait_ge(normed, 3 * i + u + 1)
                    sp.dma_start(h[:, u, :], h2_d[ds(3 * P * i + P * u, P), :]).then_inc(h_in[u], 16)
                    sp.dma_start(ya[:, u, :, :], y_d[ds(6 * P * i + 2 * P * u, 2 * P), :].rearrange(
                        "(p z) n -> p z n", z=2)).then_inc(y_in[u], 16)
                for u in range(3):
                    sp.wait_ge(ready, 3 * i + u + 1)
                    sp.dma_start(io["out_y"][ds(3 * P * i + P * u, P), :], r[:, u, :]).then_inc(stored[u], 16)
            for u in range(3):
                sp.wait_ge(stored[u], 64)

        LINKS = 18

        @block.gpsimd
        def _(pool):
            pool.wait_ge(cin, 32)
            with pool.Fori(0, 3) as i:
                for u in range(3):
                    pool.wait_ge(normed, 3 + 3 * i + u + 1)
                    nc.gpsimd.tensor_tensor(r[:, u, :], r[:, u, :], g[:], ALU.mult).then_inc(scaled, 1)
                    pool.wait_ge(scaled, 3 * i + u + 1)
                    nc.gpsimd.tensor_tensor(r[:, u, :], r[:, u, :], b[:], ALU.add).then_inc(ready, 1)

        @block.scalar
        def _(act):
            with act.Fori(0, 3) as i:
                for u in range(3):
                    act.wait_ge(var, 3 * i + u + 1)
                    nc.scalar.activation(st[:, u, 3:4], st[:, u, 2:3], ACT.Sqrt).then_inc(root, 1)

        @block.vector
        def _(dve):
            dve.nop().then_inc(normed, 3)
            with dve.Fori(0, 3) as i:
                at = [0]

                def link(ins):
                    at[0] += 1
                    ins.then_inc(ch, 1)
                    dve.wait_ge(ch, LINKS * i + at[0])

                for u in range(3):
                    dve.wait_ge(h_in[u], 16 * i + 16)
                    dve.wait_ge(y_in[u], 16 * i + 16)
                    dve.wait_ge(stored[u], 16 * i + 16)
                    link(nc.vector.scalar_tensor_tensor(r[:, u, :], h[:, u, :], ALPHA, ya[:, u, 0, :], ALU.mult,
                                                        ALU.add))
                    link(nc.vector.tensor_tensor(r[:, u, :], r[:, u, :], ya[:, u, 1, :], ALU.add))
                    for n in range(2):
                        ins = nc.vector.bn_stats(bn[:, n, :], r[:, u, HALF * n:HALF * n + HALF])
                    link(ins)
                    dve.nop().then_inc(aggr_begun, 1)
                    link(nc.vector.bn_aggr(st[:, u, 0:2], bn[:].rearrange("p n s -> p (n s)")))
                    link(nc.vector.tensor_scalar(st[:, u, 2:3], st[:, u, 1:2], LN_EPS, None, ALU.add))
                    dve.nop().then_inc(var, 1)
                    dve.wait_ge(root, 3 * i + u + 1)
                    link(nc.vector.reciprocal(st[:, u, 4:5], st[:, u, 3:4]))
                    nc.vector.tensor_scalar(r[:, u, :], r[:, u, :], st[:, u, 0:1], st[:, u, 4:5], ALU.subtract,
                                            ALU.mult).then_inc(normed, 1)
                assert at[0] == LINKS


def setup(nc, xT, ident, io):
    with nc.semaphore("x_in") as x_in, nc.semaphore("zeroed") as zeroed, nc.semaphore("ident_made") as made:
        sems = [x_in, zeroed, made]
        with nc.Block() as block:
            @block.sync
            def _(sp):
                sp.dma_start(xT[:], io["xT"]).then_inc(x_in, 16)
                sp.wait_ge(x_in, 16)

            @block.gpsimd
            def _(pool):
                nc.gpsimd.memset(ident[:], 0.0).then_inc(zeroed, 1)
                pool.wait_ge(zeroed, 1)
                nc.gpsimd.affine_select(out=ident[:], in_=ident[:], compare_op=ALU.not_equal, fill=1.0, base=0,
                                        pattern=[[-1, P]], channel_multiplier=1).then_inc(made, 1)
                pool.wait_ge(made, 1)
    return sems


def clear(nc, sems):
    with nc.Block() as block:
        @block.gpsimd
        def _(pool):
            for s in sems:
                pool.sem_clear(s)


def program(nc, io):
    with ExitStack() as c:
        ident = c.enter_context(nc.sbuf_tensor("ident", [P, P], F32))
        L = c.enter_context(nc.sbuf_tensor("router_logits", [P, NT, LOGITS], F32))
        rt = {
            "slot": c.enter_context(nc.sbuf_tensor("choice_slots", [P, 2, NT], I32)),
            "block_expert": c.enter_context(nc.sbuf_tensor("block_expert", [P, MAX_BLOCKS + 2], I32)),
            "pairs": c.enter_context(nc.sbuf_tensor("block_pairs", [P, 1], I32)),
        }
        pool_dmas = {n: c.enter_context(nc.semaphore(n)) for n in (
            "w_even_in", "w_odd_in", "shift_loaded", "slots_scattered", "rows_in_0", "rows_in_1",
            "outputs_scattered_0", "outputs_scattered_1")}
        with ExitStack() as first_half:
            def sb(name, shape):
                return first_half.enter_context(nc.sbuf_tensor(name, shape, F32))

            mixT = sb("mixT", [P, KT, T])
            fixed = {
                "pair1": sb("pair_ones", [P, P]),
                "hone": sb("head_ones", [P, 2]),
                "i64": sb("ident_64_twice", [P, 64]),
                "cmask": [sb(f"causal_{n}", [P, 4, P]) for n in ("prompt", "sample")],
                "lmask": sb("level_masks", [P, 6, P]),
                "notfirst": [sb(f"not_first_{n}", [P, HALF]) for n in ("prompt", "sample")],
                "oneseq": sb("rows_of_sequence", [P, DB]),
                "colseq": sb("cols_of_sequence", [P, DB, P]),
            }
            with nc.sbuf_tensor("xT", [P, KT, T], F32) as xT:
                sems = setup(nc, xT, ident, io)
                sems += attention_heads(nc, xT, mixT, ident, fixed, io)
                sems += rwkv_projection(nc, xT, pool_dmas, io["pa"], io)
            sems += rwkv(nc, mixT, ident, fixed, io["pa"], io)
            clear(nc, sems)
            wq, wo = (first_half.enter_context(nc.sbuf_tensor(n, [P, KT, D], F32)) for n in ("mem_wq", "mem_wo"))
            mix_and_norm(nc, mixT, wq, wo, io["h1"], io)
            memory_and_router(nc, ident, L, wq, wo, mixT, io["h1"], io["h2"], io)
        route(nc, L, rt, pool_dmas, io)
        experts(nc, ident, rt, pool_dmas, io["h2"], io["y_rows"], io)
        combine(nc, io["h2"], io["y_rows"], io)


def kernel(**inputs):
    import numpy as np
    import concourse.bacc as bacc
    from concourse.bass_utils import run_bass_kernel_spmd

    nc = bacc.Bacc("TRN2", target_bir_lowering=False, num_devices=1)
    a = {k: np.ascontiguousarray(v) for k, v in inputs.items()}
    arrays, io = {}, {}

    def give(name, array):
        array = np.ascontiguousarray(array)
        arrays["in_" + name] = array
        io[name] = nc.dram_tensor("in_" + name, array.shape, mybir.dt.from_np(array.dtype), kind="ExternalInput").ap()
        return io[name]

    def take(name, shape):
        io[name] = nc.dram_tensor(name, shape, F32, kind="ExternalOutput").ap()

    x_all = np.concatenate([a["x_prompt"].reshape(SEQ, D), a["x_sample"].reshape(DB * DS, D)])
    io["xT"] = give("xT_", x_all.T).rearrange("(k p) t -> p k t", p=P)
    give("w_in", a["w_in"][0])
    io["w_in_diff"] = io["w_in"][:, C_RWKV:C_IN].rearrange("(k p) (s n) -> p k s n", p=P, s=3)
    give("cache_kT", a["cache_diff_k"][0].transpose(1, 0, 3, 2))
    give("cache_diff_v", a["cache_diff_v"])
    for n in ("diff_lq1", "diff_lk1", "diff_lq2", "diff_lk2"):
        give(n, a[n])
    give("subln", a["diff_subln"].reshape(P, 1))
    per_block = lambda v, n: v.reshape(n, P).T
    per_pair = lambda v: per_block(v, 4)
    io["w_in_rwkv"] = io["w_in"][:, 0:C_RWKV].rearrange("(k p) (c n) -> p k c n", p=P, n=P)
    give("shiftT", a["state_shift"].reshape(DB, NB, P).transpose(2, 1, 0))
    for n in ("w0", "a0", "k_k", "k_a", "r_k"):
        give(n, per_pair(a["rwkv_" + n]))
    give("mu", per_block(a["rwkv_mu"], NB))
    for n in ("w2", "a2", "g2"):
        give(n, a["rwkv_" + n][0])
    give("rwkv_ln_w", a["rwkv_ln_w"])
    give("rwkv_ln_b", a["rwkv_ln_b"])
    give("state", a["state_rwkv"].reshape(DB, 4, 2, 64, 64).transpose(2, 4, 1, 0, 3).reshape(P, 4, DB, 64))
    io["pa"] = nc.dram_tensor("pa_rows", (P, NB, XW), F32, kind="Internal").ap()
    give("x", x_all)
    rows = lambda w: w.rearrange("(k p) n -> p k n", p=P)
    for n in ("w_out", "mem_wq", "mem_wk", "mem_wv", "mem_wo"):
        io[n] = rows(give(n, a[n][0]))
    for n in ("ln1_g", "ln1_b", "ln2_g", "ln2_b", "ln3_g", "ln3_b"):
        give(n, a[n])
    io["memT"] = rows(give("memT", a["mem_prompt"][0].T))
    io["w_group"] = rows(give("w_group", a["moe_w_group"][0]))
    io["w_expert"] = rows(give("w_expert", a["moe_w_expert"][0]))
    give("b_group", a["moe_b_group"])
    give("b_expert", a["moe_b_expert"])
    io["cache_mem_kT"] = give("cache_mem_kT", a["cache_mem_k"][0].transpose(0, 2, 1)).rearrange(
        "b (k p) m -> b p k m", p=P)
    io["cache_mem_v"] = give("cache_mem_v", a["cache_mem_v"][0]).rearrange("b (m p) n -> b p m n", p=P)
    for n in ("w1", "w3", "w2"):
        io["moe_" + n] = give("moe_" + n, a["moe_" + n][0]).rearrange("e (k p) n -> p e k n", p=P)
    io["h1"] = nc.dram_tensor("h1_rows", (T, D), F32, kind="Internal").ap()
    io["h2"] = nc.dram_tensor("h2_rows_and_zero", (T + 1, D), F32, kind="Internal").ap()
    io["y_rows"] = nc.dram_tensor("y_rows", (2 * T + SLOTS + 2 * P, D), F32, kind="Internal").ap()
    io["slots"] = nc.dram_tensor("slots", (SLOTS + 2 * P, 3), I32, kind="Internal").ap()
    take("out_y", (T, D))
    take("out_mem_k_rows", (N_MEM, D))
    take("out_mem_v_rows", (N_MEM, D))
    for n in ("out_mem_k", "out_mem_v"):
        io[n] = io[n + "_rows"].rearrange("(m p) n -> p m n", p=P)
    take("out_shift", (P, NB, DB + 1))
    take("out_state_prompt", (P, 4, 64))
    take("out_state_sample", (P, 4, DB, 64))
    take("out_diff_k_prompt", (HEADS, SEQ, P))
    take("out_diff_v_prompt", (HEADS, SEQ, P))
    take("out_diff_k_sample", (HEADS, P, P))
    take("out_diff_v_sample", (HEADS, P, P))
    program(nc, io)
    r = run_bass_kernel_spmd(nc, [arrays], core_ids=[0]).results[0]
    sample = lambda o: o.reshape(HEADS, DB, DS, P).transpose(1, 0, 2, 3)[None]
    shift = r["out_shift"].transpose(2, 1, 0).reshape(DB + 1, C_RWKV)
    st_p = r["out_state_prompt"].reshape(2, 64, 4, 64).transpose(2, 0, 3, 1).reshape(1, 1, RH, 64, 64)
    st_s = r["out_state_sample"].reshape(2, 64, 4, DB, 64).transpose(3, 2, 0, 4, 1).reshape(1, DB, RH, 64, 64)
    return (r["out_y"][None, 0:SEQ], r["out_y"][SEQ:T].reshape(DB, DS, D),
            r["out_diff_k_prompt"][None, None], r["out_diff_v_prompt"][None, None],
            r["out_mem_k_rows"][None, None], r["out_mem_v_rows"][None, None], st_p, shift[None, None, 0:1],
            sample(r["out_diff_k_sample"]), sample(r["out_diff_v_sample"]), st_s, shift[None, 1:, None])
```
